# Optimizing a Trainium2 kernel written in Bass

```python
import math
import jax, jax.numpy as jnp
from jax import lax
import numpy as np

D_MODEL = 1024
BATCH = 1
SEQ = 256
DEPTH = 2

D_RNN = D_MODEL
RG_HEADS = 4
RG_BLOCK = D_RNN // RG_HEADS
RG_CONV_WIDTH = 4
RG_C = 8.0
D_CONV = D_MODEL
CONV_KERNEL = 31
D_FF = D_MODEL * 7 // 2
N_EXPERTS = 8
TOP_K = 2
D_FF_EXPERT = D_MODEL * 7 // 2
RMS_EPS = 1e-6
LN_EPS = 1e-5

kernel_name = "hybrid_rglru_conformer_moe_trunk"

def rms_norm(x, g):
    x32 = x.astype(jnp.float32)
    y = x32 * lax.rsqrt(jnp.mean(x32 * x32, axis=-1, keepdims=True) + RMS_EPS)
    return (y * g.astype(jnp.float32)).astype(x.dtype)

def layer_norm(x, g, b):
    x32 = x.astype(jnp.float32)
    mu = jnp.mean(x32, axis=-1, keepdims=True)
    xc = x32 - mu
    var = jnp.mean(xc * xc, axis=-1, keepdims=True)
    y = xc * lax.rsqrt(var + LN_EPS) * g.astype(jnp.float32) + b.astype(jnp.float32)
    return y.astype(x.dtype)

def causal_depthwise_conv(x, w, b):
    width, chans = w.shape
    y = lax.conv_general_dilated(
        x, w[:, None, :].astype(x.dtype), window_strides=(1,), padding=[(width - 1, 0)],
        dimension_numbers=("NWC", "WIO", "NWC"), feature_group_count=chans)
    return y + b

def rg_lru(x, gate_a_w, gate_a_b, gate_x_w, gate_x_b, lam):
    bsz, seq, ch = x.shape
    xh = x.reshape(bsz, seq, RG_HEADS, RG_BLOCK)
    r = jax.nn.sigmoid((jnp.einsum("bshi,hij->bshj", xh, gate_a_w) + gate_a_b).astype(jnp.float32))
    i = jax.nn.sigmoid((jnp.einsum("bshi,hij->bshj", xh, gate_x_w) + gate_x_b).astype(jnp.float32))
    r = r.reshape(bsz, seq, ch)
    i = i.reshape(bsz, seq, ch)
    log_a = -RG_C * r * jax.nn.softplus(-lam.astype(jnp.float32))
    a = jnp.exp(log_a)
    mult = jnp.sqrt(-jnp.expm1(2.0 * log_a))
    u = mult * (i * x.astype(jnp.float32))

    def combine(left, right):
        a1, b1 = left
        a2, b2 = right
        return a1 * a2, a2 * b1 + b2

    _, h = lax.associative_scan(combine, (a, u), axis=1)
    return h.astype(x.dtype)

def recurrent_block(h, w_in, conv_w, conv_b, ga_w, ga_b, gx_w, gx_b, lam, w_out):
    proj = jnp.einsum("bsd,dn->bsn", h, w_in)
    y_branch, x_branch = jnp.split(proj, 2, axis=-1)
    y_branch = jax.nn.gelu(y_branch, approximate=True)
    x_branch = causal_depthwise_conv(x_branch, conv_w, conv_b)
    x_branch = rg_lru(x_branch, ga_w, ga_b, gx_w, gx_b, lam)
    return jnp.einsum("bsn,nd->bsd", y_branch * x_branch, w_out)

def conformer_conv_module(h, w_pw1, b_pw1, dw_w, dw_b, ln_g, ln_b, w_pw2, b_pw2):
    u = jnp.einsum("bsd,dn->bsn", h, w_pw1) + b_pw1
    val, gate = jnp.split(u, 2, axis=-1)
    u = val * jax.nn.sigmoid(gate)
    u = causal_depthwise_conv(u, dw_w, dw_b)
    u = layer_norm(u, ln_g, ln_b)
    u = jax.nn.silu(u)
    return jnp.einsum("bsn,nd->bsd", u, w_pw2) + b_pw2

def swiglu(h, w_gate_up, w_down):
    gu = h @ w_gate_up
    g, up = jnp.split(gu, 2, axis=-1)
    return (jax.nn.silu(g) * up) @ w_down

def moe_swiglu(h, router, w_gate_up, w_down):
    bsz, seq, d = h.shape
    hf = h.reshape(bsz * seq, d)
    logits = (hf @ router).astype(jnp.float32)
    vals, idx = lax.top_k(logits, TOP_K)
    weights = jax.nn.softmax(vals, axis=-1)
    gates = jnp.sum(jax.nn.one_hot(idx, N_EXPERTS, dtype=jnp.float32) * weights[..., None], axis=1)
    gates = gates.astype(hf.dtype)
    y = jnp.zeros_like(hf)
    for e in range(N_EXPERTS):
        y = y + gates[:, e:e + 1] * swiglu(hf, w_gate_up[e], w_down[e])
    return y.reshape(bsz, seq, d)

def setup_inputs(seed: int = 0) -> dict:
    key = jax.random.key(seed)
    ks = jax.random.split(key, 32)
    f32 = jnp.float32
    n_even = (DEPTH + 1) // 2
    n_odd = DEPTH // 2

    def nrm(k, shape, fan_in):
        return jax.random.normal(k, shape, f32) * (fan_in ** -0.5)

    def small(k, shape, scale=0.02):
        return jax.random.normal(k, shape, f32) * scale

    u = jax.random.uniform(ks[11], (n_even, D_RNN), f32, minval=0.9, maxval=0.999)
    rec_lambda = jnp.log(u) - jnp.log1p(-u)

    return {
        "x": jax.random.normal(ks[0], (BATCH, SEQ, D_MODEL), f32),
        "norm_mix": 1.0 + small(ks[1], (DEPTH, D_MODEL)),
        "norm_ffn": 1.0 + small(ks[2], (DEPTH, D_MODEL)),
        "norm_out": 1.0 + small(ks[3], (D_MODEL,)),
        "rec_w_in": nrm(ks[4], (n_even, D_MODEL, 2 * D_RNN), D_MODEL),
        "rec_conv_w": nrm(ks[5], (n_even, RG_CONV_WIDTH, D_RNN), RG_CONV_WIDTH),
        "rec_conv_b": small(ks[6], (n_even, D_RNN)),
        "rec_gate_a_w": nrm(ks[7], (n_even, RG_HEADS, RG_BLOCK, RG_BLOCK), RG_BLOCK),
        "rec_gate_a_b": small(ks[8], (n_even, RG_HEADS, RG_BLOCK)),
        "rec_gate_x_w": nrm(ks[9], (n_even, RG_HEADS, RG_BLOCK, RG_BLOCK), RG_BLOCK),
        "rec_gate_x_b": small(ks[10], (n_even, RG_HEADS, RG_BLOCK)),
        "rec_lambda": rec_lambda,
        "rec_w_out": nrm(ks[12], (n_even, D_RNN, D_MODEL), D_RNN),
        "ffn_w_gate_up": nrm(ks[13], (n_even, D_MODEL, 2 * D_FF), D_MODEL),
        "ffn_w_down": nrm(ks[14], (n_even, D_FF, D_MODEL), D_FF),
        "cnv_w_pw1": nrm(ks[15], (n_odd, D_MODEL, 2 * D_CONV), D_MODEL),
        "cnv_b_pw1": small(ks[16], (n_odd, 2 * D_CONV)),
        "cnv_dw_w": nrm(ks[17], (n_odd, CONV_KERNEL, D_CONV), CONV_KERNEL),
        "cnv_dw_b": small(ks[18], (n_odd, D_CONV)),
        "cnv_ln_g": 1.0 + small(ks[19], (n_odd, D_CONV)),
        "cnv_ln_b": small(ks[20], (n_odd, D_CONV)),
        "cnv_w_pw2": nrm(ks[21], (n_odd, D_CONV, D_MODEL), D_CONV),
        "cnv_b_pw2": small(ks[22], (n_odd, D_MODEL)),
        "moe_router": nrm(ks[23], (n_odd, D_MODEL, N_EXPERTS), D_MODEL),
        "moe_w_gate_up": nrm(ks[24], (n_odd, N_EXPERTS, D_MODEL, 2 * D_FF_EXPERT), D_MODEL),
        "moe_w_down": nrm(ks[25], (n_odd, N_EXPERTS, D_FF_EXPERT, D_MODEL), D_FF_EXPERT),
    }

def reference(x, norm_mix, norm_ffn, norm_out, rec_w_in, rec_conv_w, rec_conv_b,
              rec_gate_a_w, rec_gate_a_b, rec_gate_x_w, rec_gate_x_b, rec_lambda, rec_w_out,
              ffn_w_gate_up, ffn_w_down, cnv_w_pw1, cnv_b_pw1, cnv_dw_w, cnv_dw_b,
              cnv_ln_g, cnv_ln_b, cnv_w_pw2, cnv_b_pw2, moe_router, moe_w_gate_up, moe_w_down):
    h = x
    for layer in range(DEPTH):
        j = layer // 2
        if layer % 2 == 0:
            h = h + recurrent_block(rms_norm(h, norm_mix[layer]), rec_w_in[j], rec_conv_w[j],
                                    rec_conv_b[j], rec_gate_a_w[j], rec_gate_a_b[j],
                                    rec_gate_x_w[j], rec_gate_x_b[j], rec_lambda[j], rec_w_out[j])
            h = h + swiglu(rms_norm(h, norm_ffn[layer]), ffn_w_gate_up[j], ffn_w_down[j])
        else:
            h = h + conformer_conv_module(rms_norm(h, norm_mix[layer]), cnv_w_pw1[j], cnv_b_pw1[j],
                                          cnv_dw_w[j], cnv_dw_b[j], cnv_ln_g[j], cnv_ln_b[j],
                                          cnv_w_pw2[j], cnv_b_pw2[j])
            h = h + moe_swiglu(rms_norm(h, norm_ffn[layer]), moe_router[j], moe_w_gate_up[j],
                               moe_w_down[j])
    return rms_norm(h, norm_out)


_drawn_inputs = setup_inputs


def setup_inputs(seed=0):
    import zlib

    import numpy as np

    out = dict(_drawn_inputs(seed))
    spreads = {}
    factors = {'norm_out': 27.07,
     'rec_gate_a_b': 8.0,
     'rec_gate_x_b': 8.0,
     'cnv_ln_b': 2.967,
     'cnv_b_pw1': 3.46,
     'cnv_dw_b': 2.718,
     'cnv_ln_g': 2.818}
    for name, (base, spread) in spreads.items():
        noise = np.random.default_rng([zlib.crc32(name.encode()), seed]).standard_normal(out[name].shape)
        drawn = base * np.exp(spread * noise) if base else spread * noise
        out[name] = __import__('jax').numpy.asarray(drawn.astype(out[name].dtype))
    for name, factor in factors.items():
        out[name] = (out[name] * factor).astype(out[name].dtype)
    return out
```

```python
import concourse.bass as bass
from concourse import mybir
from contextlib import ExitStack

F32 = mybir.dt.float32
F32R = mybir.dt.float32r
I32 = mybir.dt.int32
ACT = mybir.ActivationFunctionType
ALU = mybir.AluOpType
AX = mybir.AxisListType

P = 128
D = 1024
SEQ = 256
TT = SEQ // P
KT = D // P
FF = D * 7 // 2
NC = 512
NB = FF // NC
HEADS = 4
NE = 8
REC_TAPS = 4
DW_TAPS = 31
RMS_EPS = 1e-6
LN_EPS = 1e-5
RAW = 6
PARTS = 3
UNIT = 2048
BLOCK_UNITS = 6
EXPERT_UNITS = NB * BLOCK_UNITS

V_MIX, V_FFN, V_CW, V_CB, V_GA, V_GX, V_LAM = 0, 2, 4, 8, 9, 10, 11
V_PW, V_DW, V_DWB, V_LNG, V_LNB = 12, 14, 45, 46, 47
NV = 48

U_IN = 0
U_GATES = 8
U_OUT = 10
U_FFN = 14
U_PW1 = U_FFN + EXPERT_UNITS
U_PW2 = U_PW1 + 8
U_MOE = U_PW2 + 4
N_UNITS = U_MOE + NE * EXPERT_UNITS

PE_TAPS = 13


def build(nc, A, out):
    ctx = ExitStack()
    with ctx:
        def sem(name):
            return ctx.enter_context(nc.semaphore(name))

        def sb(name, shape, dt=F32, stack=ctx):
            return stack.enter_context(nc.sbuf_tensor(name, shape, dt))

        raw = sb("raw", [P, RAW, UNIT])
        w_hi = sb("w_hi", [P, PARTS, UNIT], F32R)
        w_lo = sb("w_lo", [P, PARTS, UNIT], F32R)
        res = sb("res", [P, TT, D])
        ident = sb("ident", [P, P])
        colv = sb("colv", [P, KT, NV])
        ss = sb("ss", [P, TT])
        var = sb("var", [P, TT])
        rstd = sb("rstd", [P, TT])
        mhalf = sb("mhalf", [P, SEQ])
        xt_hi = sb("xt_hi", [P, KT, SEQ], F32R)
        xt_lo = sb("xt_lo", [P, KT, SEQ], F32R)

        with ExitStack() as s:
            vec_rows = sb("vec_rows", [NV, D], F32, s)
            with ExitStack() as s2:
                normed = sb("normed_a", [P, TT, D], F32, s2)
            rtmp = sb("rtmp", [P, KT, SEQ], F32, s)
            xpad = sb("xpad", [P, KT, REC_TAPS - 1 + SEQ], F32, s)
            xc = sb("xc", [P, KT, SEQ], F32, s)
            xc_hi = sb("xc_hi", [P, KT, SEQ], F32R, s)
            xc_lo = sb("xc_lo", [P, KT, SEQ], F32R, s)
            yb = sb("yb", [P, KT, SEQ], F32, s)
            rg = sb("rg", [P, KT, SEQ], F32, s)
            ig = sb("ig", [P, KT, SEQ], F32, s)
            root = sb("root", [P, KT, SEQ], F32, s)
            sp = sb("sp", [P, 8, KT], F32, s)
        with ExitStack() as s:
            normed_f = sb("normed_f", [P, TT, D], F32, s)
            sil = sb("sil", [P, TT, NC], F32, s)
            hid = sb("hid", [P, TT, NC], F32, s)
            ht_hi = sb("ht_hi", [P, TT, 4, P], F32R, s)
            ht_lo = sb("ht_lo", [P, TT, 4, P], F32R, s)
            router = sb("router", [P, KT, NE], F32, s)
            grow = sb("grow", [P, D], F32, s)
            xs_hi = sb("xs_hi", [P, TT, D], F32R, s)
            xs_lo = sb("xs_lo", [P, TT, D], F32R, s)
            xe_hi = sb("xe_hi", [P, KT, P], F32R, s)
            xe_lo = sb("xe_lo", [P, KT, P], F32R, s)
            pick = sb("pick", [P, NE, TT, P], F32R, s)
            place = sb("place", [P, NE, TT, P], F32R, s)
            place_e = sb("place_e", [P, TT, P], F32R, s)
            with ExitStack() as s2:
                routed_t = sb("routed_t", [P, 4, NC], F32, s2)
            ye_hi = sb("ye_hi", [P, D], F32R, s)
            ye_lo = sb("ye_lo", [P, D], F32R, s)
            zeros = sb("zeros", [P, NC], F32R, s)
            iota = sb("iota", [P, 2 * P], F32, s)
            earlier = sb("earlier", [P, NE, NE], F32, s)
            upper = sb("upper", [P, P], F32, s)
            ones = sb("ones", [P, P], F32, s)
            logit = sb("logit", [P, TT, NE], F32, s)
            cmp_gt = sb("cmp_gt", [P, TT, NE, NE], F32, s)
            cmp_eq = sb("cmp_eq", [P, TT, NE, NE], F32, s)
            rank = sb("rank", [P, TT, NE], F32, s)
            chosen = sb("chosen", [P, TT, NE], F32, s)
            gate = sb("gate", [P, TT, NE], F32, s)
            slot = sb("slot", [P, TT, NE], F32, s)
            small = sb("small", [P, 8], F32, s)
            most = sb("most", [P, 1], I32, s)
        with ExitStack() as s:
            normed_c = sb("normed_c", [P, TT, D], F32, s)
            bias_row = sb("bias_row", [P, D], F32, s)
            sig = sb("sig", [P, 4, SEQ], F32, s)
            upad = sb("upad", [P, KT, DW_TAPS - 1 + SEQ], F32, s)
            dw = sb("dw", [P, KT, SEQ], F32, s)
            sq = sb("sq", [P, KT, SEQ], F32, s)
            act_c = sb("act_c", [P, KT, SEQ], F32, s)
            z_hi = sb("z_hi", [P, KT, SEQ], F32R, s)
            z_lo = sb("z_lo", [P, KT, SEQ], F32R, s)
            diag = sb("diag", [P, 4, P], F32, s)
            mean_w = sb("mean_w", [P, P], F32, s)
            ln_var = sb("ln_var", [P, SEQ], F32, s)
            ln_rstd = sb("ln_rstd", [P, SEQ], F32, s)

        ps = ctx.enter_context(nc.psum_tensor("ps", [P, 8, NC], F32))

        unit_landed = [sem(f"unit_landed{i}") for i in range(RAW)]
        hi_ready, lo_ready, units_used = sem("hi_ready"), sem("lo_ready"), sem("units_used")
        x_landed, vecs_landed, late_landed, out_landed = sem("x_landed"), sem("vecs_landed"), sem("late_landed"), sem("out_landed")
        gout_landed = sem("gout_landed")
        consts = sem("consts")
        vec_t, colv_ready = sem("vec_t"), sem("colv_ready")
        squares, var_ready, rstd_ready = sem("squares"), sem("var_ready"), sem("rstd_ready")
        normed_ready, norm_t = sem("normed_ready"), sem("norm_t")
        xt_hi_ready, xt_lo_ready = sem("xt_hi_ready"), sem("xt_lo_ready")
        dve_step = sem("dve_step")
        act_step = sem("act_step")
        pool_step = sem("pool_step")
        x_out = sem("x_out")
        conv_done, xc_hi_r, xc_lo_r = sem("conv_done"), sem("xc_hi_r"), sem("xc_lo_r")
        y_out, r_out, i_out, gated = sem("y_out"), sem("r_out"), sem("i_out"), sem("gated")
        lam_exp, lam_ready, tau_ready, root_ready = sem("lam_exp"), sem("lam_ready"), sem("tau_ready"), sem("root_ready")
        lam_neg = sem("lam_neg")
        z_ready, z_hi_r, z_lo_r = sem("z_ready"), sem("z_hi_r"), sem("z_lo_r")
        res_ready = sem("res_ready")
        f_gate, f_up, f_sil, f_hid, f_t, f_hthi, f_htlo = (sem(n) for n in (
            "f_gate", "f_up", "f_sil", "f_hid", "f_t", "f_hthi", "f_htlo"))
        c_sig, c_u = sem("c_sig"), sem("c_u")
        diag_ready, diag_used, dw_done = sem("diag_ready"), sem("diag_used"), sem("dw_done")
        mean_t, centred, sq_ready, var_t, lnv_ready, lnr_ready, ln_done, silu_c = (sem(n) for n in (
            "mean_t", "centred", "sq_ready", "var_t", "lnv_ready", "lnr_ready", "ln_done", "silu_c"))
        cz_hi, cz_lo = sem("cz_hi"), sem("cz_lo")
        xs_ready, xs_hi_r, xs_lo_r, xr_t, xr_out = sem("xs_ready"), sem("xs_hi_r"), sem("xs_lo_r"), sem("xr_t"), sem("xr_out")
        logits_t, ranked, counted, exp_l, pick_r, pick_t, place_r = (sem(n) for n in (
            "logits_t", "ranked", "counted", "exp_l", "pick_r", "pick_t", "place_r"))
        lmax_r, most_r = sem("lmax_r"), sem("most_r")
        gathered, xe_hi_r, xe_lo_r = sem("gathered"), sem("xe_hi_r"), sem("xe_lo_r")
        m_sil, m_hid, m_t, m_hthi, m_htlo = (sem(n) for n in (
            "m_sil", "m_hid", "m_t", "m_hthi", "m_htlo"))
        placee_r, ye_hi_r, ye_lo_r, scattered, added = (sem(n) for n in (
            "placee_r", "ye_hi_r", "ye_lo_r", "scattered", "added"))
        moe_over, out_ready = sem("moe_over"), sem("out_ready")

        block = ctx.enter_context(nc.Block())

        def tile4(ap):
            return ap.rearrange("(k p) n -> p k n", p=P)

        def slot4(t, s):
            return t[:, s, :].rearrange("p (k n) -> p k n", k=4)

        def half(mat, kh, col):
            return tile4(mat[kh * NC:(kh + 1) * NC, col:col + NC])

        rec_units = ([half(A["rec_w_in"][0], kh, D + g * NC) for g in range(2) for kh in range(2)]
                     + [half(A["rec_w_in"][0], kh, g * NC) for g in range(2) for kh in range(2)]
                     + [A[n][0].rearrange("h (k p) j -> p (h k) j", p=P) for n in ("rec_gate_a_w", "rec_gate_x_w")]
                     + [half(A["rec_w_out"][0], kh, g * NC) for g in range(2) for kh in range(2)])
        conv_units = ([half(A["cnv_w_pw1"][0], kh, side * D + g * NC)
                       for g in range(2) for side in range(2) for kh in range(2)]
                      + [half(A["cnv_w_pw2"][0], kh, g * NC) for g in range(2) for kh in range(2)])
        ffn_gu = A["ffn_w_gate_up"][0]
        ffn_dn = A["ffn_w_down"][0]
        moe_gu = A["moe_w_gate_up"][0]
        moe_dn = A["moe_w_down"][0].rearrange("e f n -> (e f) n")

        @block.sync
        def _(sp_):
            sp_.dma_start(res[:, 0, :], A["x"][0][0:P, :]).then_inc(x_landed, 16)
            sp_.dma_start(res[:, 1, :], A["x"][0][P:SEQ, :]).then_inc(x_landed, 16)

            def load(base, src, rounds=0):
                slot_n = base % RAW
                if base >= RAW:
                    sp_.wait_ge(lo_ready, base - (RAW - 1) + RAW * rounds)
                dst = raw[:, slot_n, :].rearrange("p (k n) -> p k n", k=src.shape[1])
                sp_.dma_start(dst, src).then_inc(unit_landed[slot_n], 16)

            for n, src in enumerate(rec_units):
                load(n, src)
            with sp_.Fori(0, NB) as j:
                for k in range(BLOCK_UNITS):
                    if k < 4:
                        col = (k // 2) * FF
                        src = tile4(ffn_gu[(k % 2) * NC:(k % 2 + 1) * NC, bass.ds(col + NC * j, NC)])
                    else:
                        src = tile4(ffn_dn[bass.ds(NC * j, NC), (k - 4) * NC:(k - 3) * NC])
                    load(U_FFN + k, src, j)
            for n, src in enumerate(conv_units):
                load(U_PW1 + n, src)

            def gate_up(e, j, k):
                col = (k // 2) * FF
                return moe_gu[bass.ds(e, 1), (k % 2) * NC:(k % 2 + 1) * NC, bass.ds(col + NC * j, NC)].rearrange(
                    "e (k p) n -> p (e k) n", p=P)

            def down(e, j, c):
                return tile4(moe_dn[bass.ds(e * FF + j * NC, NC), c * NC:(c + 1) * NC])

            def expert_weights(e, first):
                for k in range(4):
                    load(first + k, gate_up(e, 0, k), NB * e)
                with sp_.Fori(1, NB) as j:
                    for k in range(BLOCK_UNITS):
                        src = gate_up(e, j, k) if k < 4 else down(e, j - 1, k - 4)
                        load(first + 4 + k - BLOCK_UNITS, src, NB * e + j)
                for c in range(2):
                    load(first + 40 + c, down(e, NB - 1, c), NB * e)

            with sp_.Fori(0, NE) as e:
                expert_weights(e, U_MOE)
            sp_.wait_ge(most_r, 1)
            crowd = sp_.value_load(most[0:1, 0:1], min_val=0, max_val=SEQ)
            with sp_.If(crowd > P):
                with sp_.Fori(0, NE) as e:
                    expert_weights(e, N_UNITS)
            sp_.nop()
            sp_.wait_ge(out_ready, 1)
            sp_.dma_start(out[0].rearrange("(t p) d -> p t d", p=P), normed_f[:, :, :]).then_inc(out_landed, 16)
            sp_.wait_ge(out_landed, 16)

        @block.gpsimd
        def _(pool):
            nc.gpsimd.memset(ident[:], 0.0).then_inc(pool_step, 1)
            pool.wait_ge(pool_step, 1)
            nc.gpsimd.affine_select(out=ident[:], in_=ident[:], compare_op=ALU.not_equal, fill=1.0, base=0,
                                    pattern=[[-1, P]], channel_multiplier=1).then_inc(consts, 1)
            nc.gpsimd.memset(mhalf[:], -0.5).then_inc(consts, 1)
            nc.gpsimd.memset(xpad[:, :, 0:REC_TAPS - 1], 0.0).then_inc(consts, 1)

            def root_of_var(n):
                pool.wait_ge(var_ready, n + 1)
                nc.gpsimd.tensor_tensor(rstd[:], var[:], mhalf[:, 0:TT], ALU.pow).then_inc(rstd_ready, 1)

            pool.wait_ge(consts, 3)
            root_of_var(0)
            for g in range(2):
                pool.wait_ge(i_out, 4 * (g + 1))
                pool.wait_ge(xc_lo_r, g + 1)
                s = slice(4 * g, 4 * g + 4)
                nc.gpsimd.tensor_tensor(ig[:, s, :], ig[:, s, :], xc[:, s, :], ALU.mult).then_inc(gated, 1)
            root_of_var(1)
            root_of_var(2)
            nc.gpsimd.memset(upad[:, :, 0:DW_TAPS - 1], 0.0).then_inc(consts, 1)
            nc.gpsimd.memset(mean_w[:], 1.0 / D).then_inc(consts, 1)
            pool.wait_ge(lnv_ready, 1)
            nc.gpsimd.tensor_tensor(ln_rstd[:], ln_var[:], mhalf[:], ALU.pow).then_inc(lnr_ready, 1)
            root_of_var(3)
            nc.gpsimd.memset(zeros[:].bitcast(F32), 0.0).then_inc(consts, 1)
            nc.gpsimd.memset(ones[:], 1.0).then_inc(pool_step, 1)
            nc.gpsimd.memset(earlier[:], 1.0).then_inc(pool_step, 1)
            nc.gpsimd.iota(iota[:], [[1, 2 * P]], base=0, channel_multiplier=0,
                           allow_small_or_imprecise_dtypes=True).then_inc(consts, 1)
            pool.wait_ge(pool_step, 3)
            nc.gpsimd.affine_select(out=earlier[:], in_=earlier[:], compare_op=ALU.is_ge, fill=0.0, base=-1,
                                    pattern=[[1, NE], [-1, NE]], channel_multiplier=0).then_inc(consts, 1)
            nc.gpsimd.affine_select(out=upper[:], in_=ones[:], compare_op=ALU.is_ge, fill=0.0, base=-1,
                                    pattern=[[1, P]], channel_multiplier=-1).then_inc(consts, 1)
            root_of_var(4)

        @block.scalar
        def _(act):
            act.dma_start(vec_rows[V_MIX:V_MIX + 2, :], A["norm_mix"]).then_inc(vecs_landed, 16)
            act.dma_start(vec_rows[V_FFN:V_FFN + 2, :], A["norm_ffn"]).then_inc(vecs_landed, 16)
            act.dma_start(vec_rows[V_CW:V_CW + REC_TAPS, :], A["rec_conv_w"][0]).then_inc(vecs_landed, 16)
            for v, name in ((V_CB, "rec_conv_b"), (V_LAM, "rec_lambda"), (V_DWB, "cnv_dw_b"),
                            (V_LNG, "cnv_ln_g"), (V_LNB, "cnv_ln_b")):
                act.dma_start(vec_rows[v:v + 1, :], A[name]).then_inc(vecs_landed, 16)
            for v, name in ((V_GA, "rec_gate_a_b"), (V_GX, "rec_gate_x_b")):
                act.dma_start(vec_rows[v:v + 1, :], A[name].rearrange("o h j -> o (h j)")).then_inc(vecs_landed, 16)
            act.dma_start(vec_rows[V_PW:V_PW + 2, :], A["cnv_b_pw1"][0].rearrange("(s n) -> s n", s=2)).then_inc(vecs_landed, 16)
            act.dma_start(vec_rows[V_DW:V_DW + DW_TAPS, :], A["cnv_dw_w"][0]).then_inc(vecs_landed, 16)

            steps = [0]

            def link(ins):
                steps[0] += 1
                ins.then_inc(act_step, 1)
                act.wait_ge(act_step, steps[0])

            def split_hi(base, rounds=0):
                slot_n, part = base % RAW, base % PARTS
                act.wait_ge(unit_landed[slot_n], 16 * (base // RAW + 1) + 16 * rounds)
                if base >= PARTS:
                    act.wait_ge(units_used, base - (PARTS - 1) + RAW * rounds)
                nc.scalar.activation(w_hi[:, part, :], raw[:, slot_n, :], ACT.Copy).then_inc(hi_ready, 1)

            def norm_square(n, keep):
                if n:
                    act.wait_ge(res_ready, n)
                else:
                    act.wait_ge(x_landed, 32)
                for t in range(TT):
                    nc.scalar.activation(keep[:, t, :], res[:, t, :], ACT.Square,
                                         accum_out=ss[:, t:t + 1]).then_inc(squares, 1)

            def norm_hi(n, vrow):
                act.wait_ge(norm_t, n + 1)
                act.wait_ge(colv_ready, 1)
                for k in range(KT):
                    nc.scalar.activation(xt_hi[:, k, :], ps[:, k // 2, (k % 2) * SEQ:(k % 2 + 1) * SEQ], ACT.Copy,
                                         scale=colv[:, k, vrow:vrow + 1]).then_inc(xt_hi_ready, 1)

            norm_square(0, normed)
            split_hi(0), split_hi(1), split_hi(2)
            norm_hi(0, V_MIX)
            act.wait_ge(lam_neg, 1)
            nc.scalar.activation(sp[:, 1, :], sp[:, 0, :], ACT.Exp).then_inc(lam_exp, 1)
            split_hi(3)

            def x_evac(g):
                act.wait_ge(units_used, 2 * g + 2)
                b = 4 - 4 * g
                nc.scalar.activation(xpad[:, 4 * g:4 * g + 4, REC_TAPS - 1:], ps[:, b:b + 4, 0:SEQ], ACT.Copy).then_inc(x_out, 1)

            def xc_round(g):
                act.wait_ge(conv_done, g + 1)
                nc.scalar.activation(xc_hi[:, 4 * g:4 * g + 4, :], xc[:, 4 * g:4 * g + 4, :], ACT.Copy).then_inc(xc_hi_r, 1)

            def y_evac(g):
                act.wait_ge(units_used, 4 + 2 * g + 2)
                b = 4 - 4 * g
                nc.scalar.activation(yb[:, 4 * g:4 * g + 4, :], ps[:, b:b + 4, 0:SEQ], ACT.Gelu_apprx_tanh).then_inc(y_out, 1)

            x_evac(0)
            split_hi(4), split_hi(5)
            x_evac(1)
            xc_round(0)
            split_hi(6), split_hi(7)
            xc_round(1)
            y_evac(0)
            split_hi(8), split_hi(9)
            y_evac(1)
            split_hi(10)
            act.wait_ge(units_used, U_GATES + 1)
            for k in range(KT):
                nc.scalar.activation(rg[:, k, :], ps[:, 4 + k // 2, (k % 2) * SEQ:(k % 2 + 1) * SEQ], ACT.Sigmoid,
                                     bias=colv[:, k, V_GA:V_GA + 1]).then_inc(r_out, 1)
            split_hi(11)
            act.wait_ge(units_used, U_GATES + 2)
            for k in range(KT):
                nc.scalar.activation(ig[:, k, :], ps[:, k // 2, (k % 2) * SEQ:(k % 2 + 1) * SEQ], ACT.Sigmoid,
                                     bias=colv[:, k, V_GX:V_GX + 1]).then_inc(i_out, 1)
            split_hi(12)
            act.wait_ge(lam_ready, 1)
            act.wait_ge(r_out, KT)
            for k in range(KT):
                nc.scalar.activation(rg[:, k, :], rg[:, k, :], ACT.Tanh, scale=sp[:, 7, k:k + 1]).then_inc(tau_ready, 1)
            for g in range(2):
                s = slice(4 * g, 4 * g + 4)
                act.wait_ge(tau_ready, 4 * g + 4)
                nc.scalar.activation(root[:, s, :], rg[:, s, :], ACT.Sqrt).then_inc(root_ready, 1)
            for g in range(2):
                s = slice(4 * g, 4 * g + 4)
                act.wait_ge(z_ready, g + 1)
                nc.scalar.activation(xc_hi[:, s, :], yb[:, s, :], ACT.Copy).then_inc(z_hi_r, 1)
            split_hi(13), split_hi(14), split_hi(15)

            norm_square(1, normed_f)
            split_hi(16)
            norm_hi(1, V_FFN)

            def ffn_act(j, base, skip):
                for k in range(skip, 4):
                    split_hi(base + k, j)
                act.wait_ge(f_gate, j + 1)
                nc.scalar.activation(sil[:, 0, :], ps[:, 0, :], ACT.Silu).then_inc(f_sil, 1)
                act.wait_ge(units_used, base + 2 + BLOCK_UNITS * j)
                nc.scalar.activation(sil[:, 1, :], ps[:, 2, :], ACT.Silu).then_inc(f_sil, 1)
                split_hi(base + 4, j), split_hi(base + 5, j)
                for c in range(TT):
                    act.wait_ge(f_t, c + 1 + TT * j)
                    nc.scalar.activation(ht_hi[:, c, :, :], ps[:, 2 * c, :].rearrange("p (q n) -> p q n", q=4),
                                         ACT.Copy).then_inc(f_hthi, 1)

            ffn_act(0, U_FFN, 3)
            with act.Fori(1, NB) as j:
                ffn_act(j, U_FFN, 0)

            split_hi(U_PW1), split_hi(U_PW1 + 1)
            norm_square(2, normed_c)
            split_hi(U_PW1 + 2)
            act.dma_start(bias_row[:, :], A["cnv_b_pw2"][0:1, :].broadcast_to([P, D])).then_inc(late_landed, 16)
            norm_hi(2, V_MIX + 1)
            split_hi(U_PW1 + 3)
            for i in (4, 5):
                split_hi(U_PW1 + i)
            for g in range(2):
                act.wait_ge(units_used, U_PW1 + 4 * g + 4)
                for i in range(4):
                    if g:
                        act.wait_ge(c_u, i + 1)
                    nc.scalar.activation(sig[:, i, :], ps[:, i, 0:SEQ], ACT.Sigmoid,
                                         bias=colv[:, 4 * g + i, V_PW + 1:V_PW + 2]).then_inc(c_sig, 1)
                for u in ((U_PW1 + 6, U_PW1 + 7, U_PW2, U_PW2 + 1) if g == 0 else (U_PW2 + 2,)):
                    split_hi(u)
            for k in range(KT):
                for i in range(PE_TAPS):
                    n = k * PE_TAPS + i
                    if n >= 4:
                        act.wait_ge(diag_used, n - 3)
                    nc.scalar.activation(diag[:, n % 4, :], ident[:], ACT.Copy,
                                         scale=colv[:, k, V_DW + i:V_DW + i + 1]).then_inc(diag_ready, 1)
            act.wait_ge(centred, 2)
            for g in range(2):
                s = slice(4 * g, 4 * g + 4)
                nc.scalar.activation(sq[:, s, :], dw[:, s, :], ACT.Square).then_inc(sq_ready, 1)
            for k in range(KT):
                act.wait_ge(ln_done, k // 4 + 1)
                nc.scalar.activation(act_c[:, k, :], sq[:, k, :], ACT.Silu, scale=colv[:, k, V_LNG:V_LNG + 1],
                                     bias=colv[:, k, V_LNB:V_LNB + 1]).then_inc(silu_c, 1)
                if k % 4 == 3:
                    g = k // 4
                    s = slice(4 * g, 4 * g + 4)
                    act.wait_ge(silu_c, k + 1)
                    nc.scalar.activation(z_hi[:, s, :], act_c[:, s, :], ACT.Copy).then_inc(cz_hi, 1)
            split_hi(U_PW2 + 3)

            norm_square(3, normed_f)
            act.dma_start(router[:, :, :], A["moe_router"][0].rearrange("(k p) e -> p k e", p=P)).then_inc(late_landed, 16)
            act.dma_start(grow[:, :], A["norm_ffn"][1:2, :].broadcast_to([P, D])).then_inc(late_landed, 16)
            act.wait_ge(xs_ready, 1)
            nc.scalar.activation(xs_hi[:, :, :], normed_f[:, :, :], ACT.Copy).then_inc(xs_hi_r, 1)
            act.wait_ge(xr_t, 1)
            nc.scalar.activation(routed_t[:, :, :], ps[:, 0:4, :], ACT.Copy).then_inc(xr_out, 1)
            act.wait_ge(lmax_r, 1)
            nc.scalar.activation(gate[:, :, :], gate[:, :, :], ACT.Exp).then_inc(exp_l, 1)

            def place_evac(p):
                for h in range(4):
                    act.wait_ge(pick_t, 4 * p + h + 1)
                    nc.scalar.activation(place[:, 2 * h:2 * h + 2, :, :].rearrange("p e t n -> p (e t n)"), ps[:, h, :],
                                         ACT.Copy).then_inc(place_r, 1)

            def expert_act(e, n, first):
                used = EXPERT_UNITS * e

                def silu(j, gate_done):
                    act.wait_ge(units_used, gate_done)
                    if not isinstance(j, int):
                        act.wait_ge(m_hid, n * NB + j)
                    nc.scalar.activation(sil[:, 0, :], ps[:, 0, :], ACT.Silu).then_inc(m_sil, 1)

                def round_hidden(j):
                    act.wait_ge(m_t, n * NB + 1 + j)
                    nc.scalar.activation(ht_hi[:, 0, :, :].rearrange("p q n -> p (q n)"), ps[:, 2, :],
                                         ACT.Copy).then_inc(m_hthi, 1)

                split_hi(first, NB * e)
                act.wait_ge(gathered, n + 1)
                nc.scalar.activation(xe_hi[:, :, :].rearrange("p k n -> p (k n)"),
                                     ps[:, 6:8, :].rearrange("p b n -> p (b n)"), ACT.Copy).then_inc(xe_hi_r, 1)
                for v in (1, 2, 3):
                    split_hi(first + v, NB * e)
                silu(0, first + 2 + used)
                nc.scalar.activation(place_e[:, :, :], place[:, bass.ds(e, 1), :, :].rearrange("p e t n -> p (e t) n"),
                                     ACT.Copy).then_inc(placee_r, 1)
                with act.Fori(1, NB) as j:
                    for k in range(4):
                        split_hi(first + 4 + k - BLOCK_UNITS, NB * e + j)
                    silu(j, first + BLOCK_UNITS * j + used)
                    round_hidden(j - 1)
                    for k in (4, 5):
                        split_hi(first + 4 + k - BLOCK_UNITS, NB * e + j)
                split_hi(first + 40, NB * e), split_hi(first + 41, NB * e)
                round_hidden(NB - 1)
                act.wait_ge(units_used, first + 42 + used)
                nc.scalar.activation(ye_hi[:, :], ps[:, 4:6, :].rearrange("p b n -> p (b n)"), ACT.Copy).then_inc(ye_hi_r, 1)

            place_evac(0)
            with act.Fori(0, NE) as e:
                expert_act(e, e, U_MOE)
            act.wait_ge(most_r, 1)
            crowd = act.value_load(most[0:1, 0:1], min_val=0, max_val=SEQ)
            with act.If(crowd > P):
                place_evac(1)
                with act.Fori(0, NE) as e:
                    expert_act(e, e + NE, N_UNITS)

            act.wait_ge(moe_over, 1)
            act.dma_start(grow[:, :], A["norm_out"].rearrange("(o n) -> o n", o=1).broadcast_to([P, D])).then_inc(gout_landed, 16)
            for t in range(TT):
                nc.scalar.activation(normed_f[:, t, :], res[:, t, :], ACT.Square, accum_out=ss[:, t:t + 1]).then_inc(squares, 1)

        @block.vector
        def _(dve):
            steps = [0]

            def link(ins):
                steps[0] += 1
                ins.then_inc(dve_step, 1)
                dve.wait_ge(dve_step, steps[0])

            def split_lo(base, rounds=0):
                slot_n, part = base % RAW, base % PARTS
                dve.wait_ge(hi_ready, base + 1 + RAW * rounds)
                nc.vector.tensor_tensor(w_lo[:, part, :], raw[:, slot_n, :], w_hi[:, part, :].bitcast(F32),
                                        ALU.subtract).then_inc(lo_ready, 1)

            def norm_scale(n, keep):
                dve.wait_ge(squares, TT * (n + 1))
                nc.vector.tensor_scalar(var[:], ss[:], 1.0 / D, RMS_EPS, ALU.mult, ALU.add).then_inc(var_ready, 1)
                dve.wait_ge(rstd_ready, n + 1)
                for t in range(TT):
                    nc.vector.tensor_scalar(keep[:, t, :], res[:, t, :], rstd[:, t:t + 1], None,
                                            ALU.mult).then_inc(normed_ready, 1)

            def norm_lo(n, vrow):
                for k in range(KT):
                    dve.wait_ge(xt_hi_ready, KT * n + (k | 1) + 1)
                    nc.vector.scalar_tensor_tensor(
                        out=xt_lo[:, k, :], in0=ps[:, k // 2, (k % 2) * SEQ:(k % 2 + 1) * SEQ],
                        scalar=colv[:, k, vrow:vrow + 1], in1=xt_hi[:, k, :].bitcast(F32),
                        op0=ALU.mult, op1=ALU.subtract).then_inc(xt_lo_ready, 1)

            dve.wait_ge(vec_t, 1)
            nc.vector.tensor_copy(colv[:, :, :].rearrange("p k v -> p (k v)"), ps[:, 7, 0:KT * NV]).then_inc(colv_ready, 1)
            norm_scale(0, normed)
            split_lo(0), split_lo(1)
            dve.wait_ge(colv_ready, 1)
            norm_lo(0, V_MIX)
            link(nc.vector.tensor_scalar(sp[:, 0, :], colv[:, :, V_LAM], -1.0, None, ALU.mult))
            nc.vector.tensor_tensor(sp[:, 0, :], sp[:, 0, :], colv[:, :, V_LAM], ALU.min).then_inc(lam_neg, 1)
            split_lo(2), split_lo(3)

            def conv4(g):
                dve.wait_ge(x_out, g + 1)
                for i in range(REC_TAPS):
                    tap = REC_TAPS - 1 - i
                    for k in range(4 * g, 4 * g + 4):
                        src = xpad[:, k, tap:tap + SEQ]
                        w = colv[:, k, V_CW + tap:V_CW + tap + 1]
                        if i == 0:
                            ins = nc.vector.tensor_scalar(xc[:, k, :], src, w, colv[:, k, V_CB:V_CB + 1], ALU.mult, ALU.add)
                        else:
                            ins = nc.vector.scalar_tensor_tensor(out=xc[:, k, :], in0=src, scalar=w, in1=xc[:, k, :],
                                                                 op0=ALU.mult, op1=ALU.add)
                        if i == REC_TAPS - 1:
                            if k == 4 * g + 3:
                                ins.then_inc(conv_done, 1)
                        elif k == 4 * g + 3:
                            link(ins)

            def xc_rest(g):
                dve.wait_ge(xc_hi_r, g + 1)
                s = slice(4 * g, 4 * g + 4)
                nc.vector.tensor_tensor(xc_lo[:, s, :], xc[:, s, :], xc_hi[:, s, :].bitcast(F32), ALU.subtract).then_inc(xc_lo_r, 1)

            dve.wait_ge(consts, 3)
            conv4(0)
            split_lo(4)
            xc_rest(0)
            split_lo(5)
            conv4(1)
            split_lo(6), split_lo(7)
            xc_rest(1)
            dve.wait_ge(lam_exp, 1)
            ex, y, y2, acc = sp[:, 1, :], sp[:, 2, :], sp[:, 3, :], sp[:, 4, :]
            link(nc.vector.tensor_scalar(y2, ex, 2.0, None, ALU.add))
            link(nc.vector.reciprocal(acc, y2))
            link(nc.vector.tensor_tensor(y, ex, acc, ALU.mult))
            link(nc.vector.tensor_tensor(y2, y, y, ALU.mult))
            link(nc.vector.memset(acc, 1.0 / 19))
            for n in range(17, 0, -2):
                link(nc.vector.tensor_tensor(acc, acc, y2, ALU.mult))
                link(nc.vector.tensor_scalar(acc, acc, 1.0 / n, None, ALU.add))
            link(nc.vector.tensor_tensor(acc, acc, y, ALU.mult))
            link(nc.vector.tensor_scalar(sp[:, 5, :], colv[:, :, V_LAM], -1.0, 0.0, ALU.mult, ALU.max))
            link(nc.vector.scalar_tensor_tensor(out=sp[:, 6, :], in0=acc, scalar=2.0, in1=sp[:, 5, :],
                                                op0=ALU.mult, op1=ALU.add))
            nc.vector.tensor_scalar(sp[:, 7, :], sp[:, 6, :], 4.0, None, ALU.mult).then_inc(lam_ready, 1)
            for u in range(8, 13):
                split_lo(u)
            for g in range(2):
                s = slice(4 * g, 4 * g + 4)
                dve.wait_ge(tau_ready, 4 * g + 4)
                link(nc.vector.tensor_scalar(rtmp[:, s, :], rg[:, s, :], -1.0, -1.0, ALU.mult, ALU.add))
                link(nc.vector.reciprocal(rtmp[:, s, :], rtmp[:, s, :]))
                dve.wait_ge(root_ready, g + 1)
                link(nc.vector.scalar_tensor_tensor(out=rg[:, s, :], in0=rg[:, s, :], scalar=1.0, in1=rtmp[:, s, :],
                                                    op0=ALU.subtract, op1=ALU.mult))
                link(nc.vector.scalar_tensor_tensor(out=root[:, s, :], in0=root[:, s, :], scalar=-2.0, in1=rtmp[:, s, :],
                                                    op0=ALU.mult, op1=ALU.mult))
                dve.wait_ge(gated, g + 1)
                link(nc.vector.tensor_tensor(root[:, s, :], root[:, s, :], ig[:, s, :], ALU.mult))
                for k in range(4 * g, 4 * g + 4):
                    ins = nc.vector.tensor_tensor_scan(rtmp[:, k, :], rg[:, k, :], root[:, k, :], 0.0, ALU.mult, ALU.add)
                link(ins)
                dve.wait_ge(y_out, g + 1)
                nc.vector.tensor_tensor(yb[:, s, :], yb[:, s, :], rtmp[:, s, :], ALU.mult).then_inc(z_ready, 1)
            for g in range(2):
                s = slice(4 * g, 4 * g + 4)
                dve.wait_ge(z_hi_r, g + 1)
                nc.vector.tensor_tensor(xc_lo[:, s, :], yb[:, s, :], xc_hi[:, s, :].bitcast(F32), ALU.subtract).then_inc(z_lo_r, 1)
            split_lo(13), split_lo(14), split_lo(15)

            def add_residual(used):
                dve.wait_ge(units_used, used)
                for t in range(TT):
                    ins = nc.vector.tensor_tensor(res[:, t, :], res[:, t, :],
                                                  ps[:, 4 + 2 * t:6 + 2 * t, :].rearrange("p b n -> p (b n)"), ALU.add)
                ins.then_inc(res_ready, 1)

            add_residual(U_FFN)

            norm_scale(1, normed_f)
            split_lo(16)
            norm_lo(1, V_FFN)

            def ffn_dve(j, base, skip):
                for k in range(skip, BLOCK_UNITS):
                    split_lo(base + k, j)
                for c in range(TT):
                    dve.wait_ge(f_sil, c + 1 + TT * j)
                    if c == 0:
                        dve.wait_ge(f_up, j + 1)
                    else:
                        dve.wait_ge(units_used, base + 4 + BLOCK_UNITS * j)
                    nc.vector.tensor_tensor(hid[:, c, :], sil[:, c, :], ps[:, 2 * c + 1, :], ALU.mult).then_inc(f_hid, 1)
                for c in range(TT):
                    dve.wait_ge(f_hthi, c + 1 + TT * j)
                    nc.vector.tensor_tensor(ht_lo[:, c, :, :].rearrange("p q n -> p (q n)"), ps[:, 2 * c, :],
                                            ht_hi[:, c, :, :].bitcast(F32).rearrange("p q n -> p (q n)"),
                                            ALU.subtract).then_inc(f_htlo, 1)

            ffn_dve(0, U_FFN, 3)
            with dve.Fori(1, NB) as j:
                ffn_dve(j, U_FFN, 0)
            split_lo(U_PW1), split_lo(U_PW1 + 1)
            add_residual(U_PW1)

            norm_scale(2, normed_c)
            split_lo(U_PW1 + 2)
            norm_lo(2, V_MIX + 1)
            split_lo(U_PW1 + 3)
            split_lo(U_PW1 + 4), split_lo(U_PW1 + 5)
            for g in range(2):
                for i in range(4):
                    k = 4 * g + i
                    dve.wait_ge(c_sig, k + 1)
                    nc.vector.scalar_tensor_tensor(
                        out=upad[:, k, DW_TAPS - 1:], in0=ps[:, 4 + i, 0:SEQ],
                        scalar=colv[:, k, V_PW:V_PW + 1], in1=sig[:, i, :], op0=ALU.add, op1=ALU.mult).then_inc(c_u, 1)
                for u in ((U_PW1 + 6, U_PW1 + 7, U_PW2, U_PW2 + 1) if g == 0 else (U_PW2 + 2,)):
                    split_lo(u)
            dve.wait_ge(consts, 5)
            dve.wait_ge(c_u, KT)
            for pair in range(KT // 2):
                for n, tap in enumerate(range(DW_TAPS - 1, PE_TAPS - 1, -1)):
                    for k in (2 * pair, 2 * pair + 1):
                        src = upad[:, k, tap:tap + SEQ]
                        w = colv[:, k, V_DW + tap:V_DW + tap + 1]
                        if n == 0:
                            ins = nc.vector.tensor_scalar(dw[:, k, :], src, w, colv[:, k, V_DWB:V_DWB + 1], ALU.mult, ALU.add)
                        else:
                            ins = nc.vector.scalar_tensor_tensor(out=dw[:, k, :], in0=src, scalar=w, in1=dw[:, k, :],
                                                                 op0=ALU.mult, op1=ALU.add)
                    link(ins)
                for k in (2 * pair, 2 * pair + 1):
                    dve.wait_ge(diag_used, (k + 1) * PE_TAPS)
                    ins = nc.vector.tensor_tensor(dw[:, k, :], dw[:, k, :], ps[:, k % 4, 0:SEQ], ALU.add)
                    ins.then_inc(dw_done, 1)
            dve.wait_ge(mean_t, 1)
            for g in range(2):
                s = slice(4 * g, 4 * g + 4)
                nc.vector.tensor_tensor(dw[:, s, :], dw[:, s, :], ps[:, 4:5, 0:SEQ].broadcast_to([P, 4, SEQ]),
                                        ALU.subtract).then_inc(centred, 1)
            dve.wait_ge(var_t, 1)
            nc.vector.tensor_scalar(ln_var[:], ps[:, 5, 0:SEQ], LN_EPS, None, ALU.add).then_inc(lnv_ready, 1)
            dve.wait_ge(lnr_ready, 1)
            for g in range(2):
                s = slice(4 * g, 4 * g + 4)
                nc.vector.tensor_tensor(sq[:, s, :], dw[:, s, :],
                                        ln_rstd[:, :].unsqueeze(1).broadcast_to([P, 4, SEQ]), ALU.mult).then_inc(ln_done, 1)
            for g in range(2):
                s = slice(4 * g, 4 * g + 4)
                dve.wait_ge(cz_hi, g + 1)
                nc.vector.tensor_tensor(z_lo[:, s, :], act_c[:, s, :], z_hi[:, s, :].bitcast(F32), ALU.subtract).then_inc(cz_lo, 1)
            split_lo(U_PW2 + 3)
            dve.wait_ge(late_landed, 16)
            for t in range(TT):
                ins = nc.vector.tensor_tensor(res[:, t, :], res[:, t, :], bias_row[:, :], ALU.add)
            link(ins)
            add_residual(U_MOE)

            dve.wait_ge(squares, TT * 4)
            nc.vector.tensor_scalar(var[:], ss[:], 1.0 / D, RMS_EPS, ALU.mult, ALU.add).then_inc(var_ready, 1)
            dve.wait_ge(rstd_ready, 4)
            dve.wait_ge(late_landed, 48)
            for t in range(TT):
                ins = nc.vector.scalar_tensor_tensor(out=normed_f[:, t, :], in0=res[:, t, :], scalar=rstd[:, t:t + 1],
                                                     in1=grow[:, :], op0=ALU.mult, op1=ALU.mult)
            ins.then_inc(xs_ready, 1)
            dve.wait_ge(xs_hi_r, 1)
            nc.vector.tensor_tensor(xs_lo[:, :, :], normed_f[:, :, :], xs_hi[:, :, :].bitcast(F32), ALU.subtract).then_inc(xs_lo_r, 1)
            dve.wait_ge(consts, 9)
            dve.wait_ge(logits_t, 1)
            link(nc.vector.tensor_copy(logit[:, :, :], ps[:, 4:6, 0:NE]))
            for t in range(TT):
                other = logit[:, t:t + 1, :].broadcast_to([P, NE, NE])
                own = logit[:, t, :].unsqueeze(2).broadcast_to([P, NE, NE])
                nc.vector.tensor_tensor(cmp_gt[:, t, :, :], other, own, ALU.is_gt)
                ins = nc.vector.tensor_tensor(cmp_eq[:, t, :, :], other, own, ALU.is_equal)
            link(ins)
            for t in range(TT):
                ins = nc.vector.tensor_tensor(cmp_eq[:, t, :, :], cmp_eq[:, t, :, :], earlier[:, :, :], ALU.mult)
            link(ins)
            link(nc.vector.tensor_tensor(cmp_gt[:, :, :, :].rearrange("p t a b -> p (t a b)"),
                                         cmp_gt[:, :, :, :].rearrange("p t a b -> p (t a b)"),
                                         cmp_eq[:, :, :, :].rearrange("p t a b -> p (t a b)"), ALU.add))
            link(nc.vector.tensor_reduce(rank[:, :, :].rearrange("p t e -> p (t e)"),
                                         cmp_gt[:, :, :, :].rearrange("p t a b -> p (t a) b"), AX.X, ALU.add))
            nc.vector.tensor_scalar(chosen[:, :, :], rank[:, :, :], 1.5, None, ALU.is_lt).then_inc(ranked, 1)
            link(nc.vector.tensor_reduce(small[:, 0:TT], logit[:, :, :], AX.X, ALU.max))
            nc.vector.tensor_tensor(gate[:, :, :], logit[:, :, :], small[:, 0:TT].unsqueeze(2).broadcast_to([P, TT, NE]),
                                    ALU.subtract).then_inc(lmax_r, 1)
            dve.wait_ge(exp_l, 1)
            dve.wait_ge(ranked, 1)
            link(nc.vector.tensor_tensor(gate[:, :, :], gate[:, :, :], chosen[:, :, :], ALU.mult))
            link(nc.vector.tensor_reduce(small[:, 2:2 + TT], gate[:, :, :], AX.X, ALU.add))
            link(nc.vector.reciprocal(small[:, 4:4 + TT], small[:, 2:2 + TT]))
            link(nc.vector.tensor_tensor(gate[:, :, :], gate[:, :, :],
                                         small[:, 4:4 + TT].unsqueeze(2).broadcast_to([P, TT, NE]), ALU.mult))
            dve.wait_ge(counted, 1)
            link(nc.vector.tensor_scalar(slot[:, :, :], ps[:, 6, 0:TT * NE].rearrange("p (t e) -> p t e", t=TT), 1.0, None, ALU.add))
            link(nc.vector.tensor_tensor(slot[:, :, :], slot[:, :, :], chosen[:, :, :], ALU.mult))
            link(nc.vector.tensor_scalar(slot[:, :, :], slot[:, :, :], 1.0, None, ALU.subtract))
            link(nc.vector.tensor_reduce(small[:, 6:7], ps[:, 7, 0:NE], AX.X, ALU.max))
            nc.vector.tensor_copy(most[:, :], small[:, 6:7]).then_inc(most_r, 1)

            def make_picks(p):
                for e in range(NE):
                    for t in range(TT):
                        ins = nc.vector.tensor_scalar(pick[:, e, t, :], iota[:, p * P:(p + 1) * P], slot[:, t, e:e + 1],
                                                      None, ALU.is_equal)
                    ins.then_inc(pick_r, 1)

            def expert_dve(e, n, first):
                used = EXPERT_UNITS * e

                def hidden(j, up_done):
                    dve.wait_ge(m_sil, n * NB + 1 + j)
                    dve.wait_ge(units_used, up_done)
                    nc.vector.tensor_tensor(hid[:, 0, :], sil[:, 0, :], ps[:, 1, :], ALU.mult).then_inc(m_hid, 1)

                def rest_hidden(j):
                    dve.wait_ge(m_hthi, n * NB + 1 + j)
                    nc.vector.tensor_tensor(ht_lo[:, 0, :, :].rearrange("p q n -> p (q n)"), ps[:, 2, :],
                                            ht_hi[:, 0, :, :].bitcast(F32).rearrange("p q n -> p (q n)"),
                                            ALU.subtract).then_inc(m_htlo, 1)
                split_lo(first, NB * e)
                dve.wait_ge(xe_hi_r, n + 1)
                nc.vector.tensor_tensor(xe_lo[:, :, :].rearrange("p k n -> p (k n)"),
                                        ps[:, 6:8, :].rearrange("p b n -> p (b n)"),
                                        xe_hi[:, :, :].bitcast(F32).rearrange("p k n -> p (k n)"), ALU.subtract).then_inc(xe_lo_r, 1)
                for v in (1, 2, 3):
                    split_lo(first + v, NB * e)
                hidden(0, first + 4 + used)
                with dve.Fori(1, NB) as j:
                    for k in range(4):
                        split_lo(first + 4 + k - BLOCK_UNITS, NB * e + j)
                    rest_hidden(j - 1)
                    for k in (4, 5):
                        split_lo(first + 4 + k - BLOCK_UNITS, NB * e + j)
                    hidden(j, first + 2 + BLOCK_UNITS * j + used)
                split_lo(first + 40, NB * e), split_lo(first + 41, NB * e)
                rest_hidden(NB - 1)
                dve.wait_ge(ye_hi_r, n + 1)
                nc.vector.tensor_tensor(ye_lo[:, :], ps[:, 4:6, :].rearrange("p b n -> p (b n)"), ye_hi[:, :].bitcast(F32),
                                        ALU.subtract).then_inc(ye_lo_r, 1)
                for t in range(TT):
                    b = 6 if t == 0 else 2
                    dve.wait_ge(scattered, n * TT + t + 1)
                    nc.vector.scalar_tensor_tensor(
                        out=res[:, t, :], in0=ps[:, b:b + 2, :].rearrange("p b n -> p (b n)"),
                        scalar=gate[:, t, bass.ds(e, 1)], in1=res[:, t, :], op0=ALU.mult, op1=ALU.add).then_inc(added, 1)

            make_picks(0)
            with dve.Fori(0, NE) as e:
                expert_dve(e, e, U_MOE)
            dve.wait_ge(most_r, 1)
            crowd = dve.value_load(most[0:1, 0:1], min_val=0, max_val=SEQ)
            with dve.If(crowd > P):
                make_picks(1)
                with dve.Fori(0, NE) as e:
                    expert_dve(e, e + NE, N_UNITS)

            nc.vector.memset(small[:, 7:8], 0.0).then_inc(moe_over, 1)
            dve.wait_ge(squares, TT * 5)
            nc.vector.tensor_scalar(var[:], ss[:], 1.0 / D, RMS_EPS, ALU.mult, ALU.add).then_inc(var_ready, 1)
            dve.wait_ge(rstd_ready, 5)
            dve.wait_ge(gout_landed, 16)
            for t in range(TT):
                ins = nc.vector.scalar_tensor_tensor(out=normed_f[:, t, :], in0=res[:, t, :], scalar=rstd[:, t:t + 1],
                                                     in1=grow[:, :], op0=ALU.mult, op1=ALU.mult)
            ins.then_inc(out_ready, 1)

        @block.tensor
        def _(pe):
            def passes(dst, stat, mov, start, stop, loose=False):
                (sh, sl), (mh, ml) = stat, mov
                nc.tensor.matmul(dst, sh, ml, start=start, stop=False, skip_group_check=loose)
                nc.tensor.matmul(dst, sl, mh, start=False, stop=False, skip_group_check=loose)
                return nc.tensor.matmul(dst, sh, mh, start=False, stop=stop, skip_group_check=loose)

            def norm_transpose(n, src):
                pe.wait_ge(normed_ready, TT * (n + 1))
                for k in range(KT):
                    for t in range(TT):
                        c = (k % 2) * SEQ + t * P
                        ins = nc.tensor.transpose(ps[:, k // 2, c:c + P], src[:, t, k * P:(k + 1) * P], ident[:])
                ins.then_inc(norm_t, 1)

            def channel_major(u0, banks, xt):
                for kh in range(2):
                    u = u0 + kh
                    pe.wait_ge(lo_ready, u + 1)
                    q = u % PARTS
                    for nt in range(4):
                        for k in range(4):
                            c = slice(k * NC + nt * P, k * NC + nt * P + P)
                            ins = passes(ps[:, banks + nt, 0:SEQ], (w_hi[:, q, c], w_lo[:, q, c]),
                                         (xt[0][:, 4 * kh + k, :], xt[1][:, 4 * kh + k, :]),
                                         start=(kh == 0 and k == 0), stop=(kh == 1 and k == 3))
                    ins.then_inc(units_used, 1)

            def token_major(u0, zt):
                for c in range(2):
                    for kh in range(2):
                        u = u0 + 2 * c + kh
                        pe.wait_ge(lo_ready, u + 1)
                        q = u % PARTS
                        for t in range(TT):
                            for k in range(4):
                                s = slice(t * P, (t + 1) * P)
                                ins = passes(ps[:, 4 + 2 * t + c, :], (zt[0][:, 4 * kh + k, s], zt[1][:, 4 * kh + k, s]),
                                             (w_hi[:, q, k * NC:(k + 1) * NC], w_lo[:, q, k * NC:(k + 1) * NC]),
                                             start=(kh == 0 and k == 0), stop=(kh == 1 and k == 3))
                        ins.then_inc(units_used, 1)

            pe.wait_ge(consts, 1)
            pe.wait_ge(vecs_landed, 16 * 12)
            for k in range(KT):
                ins = nc.tensor.transpose(ps[:, 7, k * NV:(k + 1) * NV], vec_rows[:, k * P:(k + 1) * P], ident[0:NV, 0:NV])
            ins.then_inc(vec_t, 1)
            norm_transpose(0, normed)
            pe.wait_ge(xt_lo_ready, KT)
            xt = (xt_hi, xt_lo)
            pe.wait_ge(colv_ready, 1)
            channel_major(0, 4, xt)
            channel_major(2, 0, xt)
            pe.wait_ge(x_out, 1)
            channel_major(4, 4, xt)
            pe.wait_ge(x_out, 2)
            channel_major(6, 0, xt)
            pe.wait_ge(xc_lo_r, 2)
            for gate_n in range(2):
                u = U_GATES + gate_n
                pe.wait_ge(lo_ready, u + 1)
                pe.wait_ge(y_out, gate_n + 1)
                q = u % PARTS
                for h in range(HEADS):
                    for jt in range(2):
                        for k in range(2):
                            c = slice((2 * h + k) * 2 * P + jt * P, (2 * h + k) * 2 * P + jt * P + P)
                            ins = passes(ps[:, 4 - 4 * gate_n + h, jt * SEQ:(jt + 1) * SEQ],
                                         (w_hi[:, q, c], w_lo[:, q, c]),
                                         (xc_hi[:, 2 * h + k, :], xc_lo[:, 2 * h + k, :]), start=(k == 0), stop=(k == 1))
                ins.then_inc(units_used, 1)
            pe.wait_ge(r_out, KT)
            pe.wait_ge(z_lo_r, 2)
            token_major(U_OUT, (xc_hi, xc_lo))

            norm_transpose(1, normed_f)
            pe.wait_ge(xt_lo_ready, 2 * KT)

            def hidden_transpose(dst, src):
                for q in range(4):
                    ins = nc.tensor.transpose(dst[:, q * P:(q + 1) * P], src[:, q * P:(q + 1) * P], ident[:])
                return ins

            def project(dst, xt_k, q, k, start, stop, loose):
                return passes(dst, xt_k, (w_hi[:, q, k * NC:(k + 1) * NC], w_lo[:, q, k * NC:(k + 1) * NC]), start, stop, loose)

            def ffn_pe(j, first):
                for k6 in range(BLOCK_UNITS):
                    u = U_FFN + k6 + BLOCK_UNITS * j
                    q = (U_FFN + k6) % PARTS
                    if k6 == 4:
                        for c in range(TT):
                            pe.wait_ge(f_hid, c + 1 + TT * j)
                            hidden_transpose(ps[:, 2 * c, :], hid[:, c, :]).then_inc(f_t, 1)
                    pe.wait_ge(lo_ready, u + 1)
                    for c in range(TT):
                        if k6 == 4:
                            pe.wait_ge(f_htlo, c + 1 + TT * j)
                        for k in range(4):
                            if k6 < 4:
                                kk = 4 * (k6 % 2) + k
                                s = slice(c * P, (c + 1) * P)
                                ins = project(ps[:, 2 * c + k6 // 2, :], (xt_hi[:, kk, s], xt_lo[:, kk, s]), q, k,
                                              start=(kk == 0), stop=(kk == KT - 1), loose=False)
                            else:
                                ins = project(ps[:, 4 + 2 * c + k6 - 4, :], (ht_hi[:, c, k, :], ht_lo[:, c, k, :]), q, k,
                                              start=(first and k == 0), stop=False, loose=True)
                        if c == 0 and k6 in (1, 3):
                            ins.then_inc(f_gate if k6 == 1 else f_up, 1)
                    ins.then_inc(units_used, 1)

            pe.wait_ge(res_ready, 1)
            ffn_pe(0, True)
            with pe.Fori(1, NB) as j:
                ffn_pe(j, False)

            norm_transpose(2, normed_c)
            pe.wait_ge(xt_lo_ready, 3 * KT)
            for g in range(2):
                if g:
                    pe.wait_ge(c_u, 4)
                channel_major(U_PW1 + 4 * g, 4, xt)
                channel_major(U_PW1 + 4 * g + 2, 0, xt)
            pe.wait_ge(consts, 5)
            pe.wait_ge(c_u, KT)
            for k in range(KT):
                if k >= 4:
                    pe.wait_ge(dw_done, k - 3)
                for i in range(PE_TAPS):
                    n = k * PE_TAPS + i
                    pe.wait_ge(diag_ready, n + 1)
                    nc.tensor.matmul(ps[:, k % 4, 0:SEQ], diag[:, n % 4, :], upad[:, k, i:i + SEQ],
                                     start=(i == 0), stop=(i == PE_TAPS - 1)).then_inc(diag_used, 1)
            for k in range(KT):
                pe.wait_ge(dw_done, k + 1)
                ins = nc.tensor.matmul(ps[:, 4, 0:SEQ], mean_w[:], dw[:, k, :], start=(k == 0), stop=(k == KT - 1))
            ins.then_inc(mean_t, 1)
            for k in range(KT):
                pe.wait_ge(sq_ready, k // 4 + 1)
                ins = nc.tensor.matmul(ps[:, 5, 0:SEQ], mean_w[:], sq[:, k, :], start=(k == 0), stop=(k == KT - 1))
            ins.then_inc(var_t, 1)
            pe.wait_ge(lnv_ready, 1)
            pe.wait_ge(cz_lo, 2)
            token_major(U_PW2, (z_hi, z_lo))

            pe.wait_ge(xs_ready, 1)
            for k in range(KT):
                for t in range(TT):
                    c = (k % 2) * SEQ + t * P
                    ins = nc.tensor.transpose(ps[:, k // 2, c:c + P], normed_f[:, t, k * P:(k + 1) * P], ident[:])
            ins.then_inc(xr_t, 1)
            pe.wait_ge(xr_out, 1)
            for t in range(TT):
                for k in range(KT):
                    ins = nc.tensor.matmul(ps[:, 4 + t, 0:NE], routed_t[:, k // 2, (k % 2) * SEQ + t * P:(k % 2) * SEQ + (t + 1) * P],
                                           router[:, k, :], start=(k == 0), stop=(k == KT - 1))
            ins.then_inc(logits_t, 1)
            pe.wait_ge(ranked, 1)
            nc.tensor.matmul(ps[:, 6, 0:NE], upper[:], chosen[:, 0, :], start=True, stop=True)
            nc.tensor.matmul(ps[:, 6, NE:2 * NE], ones[:], chosen[:, 0, :], start=True, stop=False)
            nc.tensor.matmul(ps[:, 6, NE:2 * NE], upper[:], chosen[:, 1, :], start=False, stop=True)
            nc.tensor.matmul(ps[:, 7, 0:NE], ones[:], chosen[:, 0, :], start=True, stop=False)
            nc.tensor.matmul(ps[:, 7, 0:NE], ones[:], chosen[:, 1, :], start=False, stop=True).then_inc(counted, 1)

            def pick_transpose(p):
                for h in range(4):
                    for e in (2 * h, 2 * h + 1):
                        pe.wait_ge(pick_r, NE * p + e + 1)
                        for t in range(TT):
                            c = (e % 2) * TT * P + t * P
                            ins = nc.tensor.transpose(ps[:, h, c:c + P], pick[:, e, t, :].bitcast(F32), ident[:])
                    ins.then_inc(pick_t, 1)
                pe.wait_ge(place_r, 4 * (p + 1))

            def expert_pe(e, n, first):
                def weights(base, rounds):
                    pe.wait_ge(lo_ready, base + 1 + RAW * rounds)
                    return base % PARTS

                def gate_or_up(bank, base, rounds):
                    for kh in range(2):
                        q = weights(base + kh, rounds)
                        for k in range(4):
                            kk = 4 * kh + k
                            ins = project(ps[:, bank, :], (xe_hi[:, kk, :], xe_lo[:, kk, :]), q, k,
                                          start=(kk == 0), stop=(kk == KT - 1), loose=False)
                        ins.then_inc(units_used, 1)

                def turn(j):
                    pe.wait_ge(m_hid, n * NB + 1 + j)
                    hidden_transpose(ps[:, 2, :], hid[:, 0, :]).then_inc(m_t, 1)

                def down(j, base, rounds):
                    pe.wait_ge(m_htlo, n * NB + 1 + j)
                    for c in range(2):
                        q = weights(base + c, rounds)
                        for k in range(4):
                            ins = project(ps[:, 4 + c, :], (ht_hi[:, 0, k, :], ht_lo[:, 0, k, :]), q, k,
                                          start=False, stop=False, loose=True)
                        ins.then_inc(units_used, 1)

                for k in range(KT):
                    dst = ps[:, 6 + k // 4, (k % 4) * P:(k % 4 + 1) * P]
                    for t in range(TT):
                        for part, x in enumerate((xs_hi, xs_lo)):
                            ins = nc.tensor.matmul(dst, x[:, t, k * P:(k + 1) * P],
                                                   pick[:, bass.ds(e, 1), t, :].rearrange("p e n -> p (e n)"),
                                                   start=(t == 0 and part == 0), stop=(t == TT - 1 and part == 1))
                ins.then_inc(gathered, 1)
                for c in range(2):
                    nc.tensor.matmul(ps[:, 4 + c, :], zeros[:, 0:P], zeros[:, :], start=True, stop=False, skip_group_check=True)
                pe.wait_ge(xe_lo_r, n + 1)
                gate_or_up(0, first, NB * e)
                gate_or_up(1, first + 2, NB * e)
                with pe.Fori(1, NB) as j:
                    pe.wait_ge(m_sil, n * NB + j)
                    gate_or_up(0, first + 4 - BLOCK_UNITS, NB * e + j)
                    turn(j - 1)
                    gate_or_up(1, first + 6 - BLOCK_UNITS, NB * e + j)
                    down(j - 1, first + 8 - BLOCK_UNITS, NB * e + j)
                turn(NB - 1)
                down(NB - 1, first + 40, NB * e)
                pe.wait_ge(placee_r, n + 1)
                pe.wait_ge(ye_lo_r, n + 1)
                for t in range(TT):
                    b = 6 if t == 0 else 2
                    for c in range(2):
                        for part, y in enumerate((ye_hi, ye_lo)):
                            ins = nc.tensor.matmul(ps[:, b + c, :], place_e[:, t, :], y[:, c * NC:(c + 1) * NC],
                                                   start=(part == 0), stop=(part == 1))
                    ins.then_inc(scattered, 1)
                pe.wait_ge(added, n * TT + 1)

            pe.wait_ge(xs_lo_r, 1)
            pe.wait_ge(consts, 9)
            pick_transpose(0)
            with pe.Fori(0, NE) as e:
                expert_pe(e, e, U_MOE)
            pe.wait_ge(most_r, 1)
            crowd = pe.value_load(most[0:1, 0:1], min_val=0, max_val=SEQ)
            with pe.If(crowd > P):
                pick_transpose(1)
                with pe.Fori(0, NE) as e:
                    expert_pe(e, e + NE, N_UNITS)
            pe.nop()
    return nc


_INS = ["x", "norm_mix", "norm_ffn", "norm_out", "rec_w_in", "rec_conv_w", "rec_conv_b", "rec_gate_a_w", "rec_gate_a_b",
        "rec_gate_x_w", "rec_gate_x_b", "rec_lambda", "rec_w_out", "ffn_w_gate_up", "ffn_w_down", "cnv_w_pw1",
        "cnv_b_pw1", "cnv_dw_w", "cnv_dw_b", "cnv_ln_g", "cnv_ln_b", "cnv_w_pw2", "cnv_b_pw2", "moe_router",
        "moe_w_gate_up", "moe_w_down"]


def kernel(**inputs):
    import numpy as np
    import concourse.bacc as bacc
    from concourse.bass_utils import run_bass_kernel_spmd

    nc = bacc.Bacc("TRN2", target_bir_lowering=False, num_devices=1)
    arrays, aps = {}, {}
    for name in _INS:
        a = np.ascontiguousarray(inputs[name])
        arrays[f"in_{name}"] = a
        aps[name] = nc.dram_tensor(f"in_{name}", a.shape, F32, kind="ExternalInput").ap()
    out = nc.dram_tensor("out", (1, SEQ, D), F32, kind="ExternalOutput").ap()
    build(nc, aps, out)
    r = run_bass_kernel_spmd(nc, [arrays], core_ids=[0])
    return r.results[0]["out"]
```

```python
import concourse.bass as bass
from concourse import mybir
from contextlib import ExitStack

F32 = mybir.dt.float32
F32R = mybir.dt.float32r
I32 = mybir.dt.int32
ACT = mybir.ActivationFunctionType
ALU = mybir.AluOpType
AX = mybir.AxisListType

P = 128
D = 1024
SEQ = 256
TT = SEQ // P
KT = D // P
FF = D * 7 // 2
NC = 512
NB = FF // NC
HEADS = 4
NE = 8
REC_TAPS = 4
DW_TAPS = 31
RMS_EPS = 1e-6
LN_EPS = 1e-5
RAW = 6
PARTS = 3
UNIT = 2048
BLOCK_UNITS = 6
EXPERT_UNITS = NB * BLOCK_UNITS

V_MIX, V_FFN, V_CW, V_CB, V_GA, V_GX, V_LAM = 0, 2, 4, 8, 9, 10, 11
V_PW, V_DW, V_DWB, V_LNG, V_LNB = 12, 14, 45, 46, 47
NV = 48

U_IN = 0
U_GATES = 6
U_Y1 = 8
U_OUT = 10
U_FFN = 14
U_PW1 = U_FFN + EXPERT_UNITS
U_PW2 = U_PW1 + 8
U_MOE = U_PW2 + 4
N_UNITS = U_MOE + NE * EXPERT_UNITS

PE_TAPS = 13


def build(nc, A, out):
    ctx = ExitStack()
    with ctx:
        def sem(name):
            return ctx.enter_context(nc.semaphore(name))

        def sb(name, shape, dt=F32, stack=ctx):
            return stack.enter_context(nc.sbuf_tensor(name, shape, dt))

        raw = sb("raw", [P, RAW, UNIT])
        w_hi = sb("w_hi", [P, PARTS, UNIT], F32R)
        w_lo = sb("w_lo", [P, PARTS, UNIT], F32R)
        res = sb("res", [P, TT, D])
        ident = sb("ident", [P, P])
        colv = sb("colv", [P, KT, NV])
        ss = sb("ss", [P, TT])
        var = sb("var", [P, TT])
        rstd = sb("rstd", [P, TT])
        mhalf = sb("mhalf", [P, TT])
        xt_hi = sb("xt_hi", [P, KT, SEQ], F32R)
        xt_lo = sb("xt_lo", [P, KT, SEQ], F32R)

        with ExitStack() as s:
            vec_rows = sb("vec_rows", [NV, D], F32, s)
            with ExitStack() as s2:
                normed = sb("normed_a", [P, TT, D], F32, s2)
            rtmp = sb("rtmp", [P, KT, SEQ], F32, s)
            xpad = sb("xpad", [P, KT, REC_TAPS - 1 + SEQ], F32, s)
            xc = sb("xc", [P, KT, SEQ], F32, s)
            xc_hi = sb("xc_hi", [P, KT, SEQ], F32R, s)
            xc_lo = sb("xc_lo", [P, KT, SEQ], F32R, s)
            yb = sb("yb", [P, KT, SEQ], F32, s)
            rg = sb("rg", [P, KT, SEQ], F32, s)
            ig = sb("ig", [P, KT, SEQ], F32, s)
            root = sb("root", [P, KT, SEQ], F32, s)
            sp = sb("sp", [P, 8, KT], F32, s)
        with ExitStack() as s:
            normed_f = sb("normed_f", [P, TT, D], F32, s)
            sil = sb("sil", [P, TT, NC], F32, s)
            hid = sb("hid", [P, TT, NC], F32, s)
            ht_hi = sb("ht_hi", [P, TT, 4, P], F32R, s)
            ht_lo = sb("ht_lo", [P, TT, 4, P], F32R, s)
            router = sb("router", [P, KT, NE], F32, s)
            grow = sb("grow", [P, D], F32, s)
            xs_hi = sb("xs_hi", [P, TT, D], F32R, s)
            xs_lo = sb("xs_lo", [P, TT, D], F32R, s)
            xe_hi = sb("xe_hi", [P, KT, P], F32R, s)
            xe_lo = sb("xe_lo", [P, KT, P], F32R, s)
            pick = sb("pick", [P, TT, P], F32R, s)
            place_e = sb("place_e", [P, TT, P], F32R, s)
            with ExitStack() as s2:
                routed_t = sb("routed_t", [P, 4, NC], F32, s2)
            ye_hi = sb("ye_hi", [P, D], F32R, s)
            ye_lo = sb("ye_lo", [P, D], F32R, s)
            zeros = sb("zeros", [P, NC], F32R, s)
            iota = sb("iota", [P, 2 * P], F32, s)
            earlier = sb("earlier", [P, NE, NE], F32, s)
            upper = sb("upper", [P, P], F32, s)
            ones = sb("ones", [P, P], F32, s)
            logit = sb("logit", [P, TT, NE], F32, s)
            cmp_gt = sb("cmp_gt", [P, TT, NE, NE], F32, s)
            cmp_eq = sb("cmp_eq", [P, TT, NE, NE], F32, s)
            rank = sb("rank", [P, TT, NE], F32, s)
            chosen = sb("chosen", [P, TT, NE], F32, s)
            gate = sb("gate", [P, TT, NE], F32, s)
            slot = sb("slot", [P, TT, NE + 1], F32, s)
            small = sb("small", [P, 8], F32, s)
            most = sb("most", [P, 1], I32, s)
        with ExitStack() as s:
            normed_c = sb("normed_c", [P, TT, D], F32, s)
            bias_row = sb("bias_row", [P, D], F32, s)
            sig = sb("sig", [P, 4, SEQ], F32, s)
            upad = sb("upad", [P, KT, DW_TAPS - 1 + SEQ], F32, s)
            dw = sb("dw", [P, KT, SEQ], F32, s)
            sq = sb("sq", [P, KT, SEQ], F32, s)
            act_c = sb("act_c", [P, KT, SEQ], F32, s)
            z_hi = sb("z_hi", [P, KT, SEQ], F32R, s)
            z_lo = sb("z_lo", [P, KT, SEQ], F32R, s)
            diag = sb("diag", [P, 4, P], F32, s)
            mean_w = sb("mean_w", [P, P], F32, s)
            ln_var = sb("ln_var", [P, TT], F32, s)
            ln_rstd = sb("ln_rstd", [P, TT], F32, s)
            spread = sb("spread", [P, TT, P], F32, s)

        ps = ctx.enter_context(nc.psum_tensor("ps", [P, 8, NC], F32))

        unit_landed = [sem(f"unit_landed{i}") for i in range(RAW)]
        hi_ready, lo_ready, units_used = sem("hi_ready"), sem("lo_ready"), sem("units_used")
        x_landed, vecs_landed, late_landed, out_landed = sem("x_landed"), sem("vecs_landed"), sem("late_landed"), sem("out_landed")
        gout_landed = sem("gout_landed")
        consts = sem("consts")
        vec_t, colv_ready = sem("vec_t"), sem("colv_ready")
        squares, var_ready, rstd_ready = sem("squares"), sem("var_ready"), sem("rstd_ready")
        normed_ready, norm_t = sem("normed_ready"), sem("norm_t")
        xt_hi_ready, xt_lo_ready = sem("xt_hi_ready"), sem("xt_lo_ready")
        dve_step = sem("dve_step")
        act_step = sem("act_step")
        pool_step = sem("pool_step")
        x_out = sem("x_out")
        conv_done, xc_hi_r, xc_lo_r = sem("conv_done"), sem("xc_hi_r"), sem("xc_lo_r")
        y_out, r_out, i_out, gated = sem("y_out"), sem("r_out"), sem("i_out"), sem("gated")
        lam_exp, lam_ready, tau_ready, root_ready = sem("lam_exp"), sem("lam_ready"), sem("tau_ready"), sem("root_ready")
        lam_neg = sem("lam_neg")
        z_ready, z_hi_r, z_lo_r = sem("z_ready"), sem("z_hi_r"), sem("z_lo_r")
        res_ready = sem("res_ready")
        f_gate, f_up, f_sil, f_hid, f_t, f_hthi, f_htlo = (sem(n) for n in (
            "f_gate", "f_up", "f_sil", "f_hid", "f_t", "f_hthi", "f_htlo"))
        c_sig, c_u = sem("c_sig"), sem("c_u")
        diag_ready, diag_used, dw_done = sem("diag_ready"), sem("diag_used"), sem("dw_done")
        mean_t, centred, sq_ready, var_t, lnv_ready, lnr_ready, ln_done, silu_c = (sem(n) for n in (
            "mean_t", "centred", "sq_ready", "var_t", "lnv_ready", "lnr_ready", "ln_done", "silu_c"))
        spread_r, lnb_t = sem("spread_r"), sem("lnb_t")
        cz_hi, cz_lo = sem("cz_hi"), sem("cz_lo")
        xs_ready, xs_hi_r, xs_lo_r, xr_t, xr_out = sem("xs_ready"), sem("xs_hi_r"), sem("xs_lo_r"), sem("xr_t"), sem("xr_out")
        logits_t, ranked, counted, exp_l, pick_r, pick_t, place_r = (sem(n) for n in (
            "logits_t", "ranked", "counted", "exp_l", "pick_r", "pick_t", "place_r"))
        lmax_r, most_r = sem("lmax_r"), sem("most_r")
        gathered, xe_hi_r, xe_lo_r = sem("gathered"), sem("xe_hi_r"), sem("xe_lo_r")
        m_sil, m_hid, m_t, m_hthi, m_htlo = (sem(n) for n in (
            "m_sil", "m_hid", "m_t", "m_hthi", "m_htlo"))
        ye_hi_r, ye_lo_r, scattered, added = (sem(n) for n in (
            "ye_hi_r", "ye_lo_r", "scattered", "added"))
        moe_over, out_ready = sem("moe_over"), sem("out_ready")

        block = ctx.enter_context(nc.Block())

        def tile4(ap):
            return ap.rearrange("(k p) n -> p k n", p=P)

        def slot4(t, s):
            return t[:, s, :].rearrange("p (k n) -> p k n", k=4)

        def half(mat, kh, col):
            return tile4(mat[kh * NC:(kh + 1) * NC, col:col + NC])

        rec_units = ([half(A["rec_w_in"][0], kh, D + g * NC) for g in range(2) for kh in range(2)]
                     + [half(A["rec_w_in"][0], kh, 0) for kh in range(2)]
                     + [A[n][0].rearrange("h (k p) j -> p (h k) j", p=P) for n in ("rec_gate_a_w", "rec_gate_x_w")]
                     + [half(A["rec_w_in"][0], kh, NC) for kh in range(2)]
                     + [half(A["rec_w_out"][0], kh, g * NC) for kh in range(2) for g in range(2)])
        conv_units = ([half(A["cnv_w_pw1"][0], kh, side * D + g * NC)
                       for g in range(2) for side in range(2) for kh in range(2)]
                      + [half(A["cnv_w_pw2"][0], kh, g * NC) for kh in range(2) for g in range(2)])
        ffn_gu = A["ffn_w_gate_up"][0]
        ffn_dn = A["ffn_w_down"][0]
        moe_gu = A["moe_w_gate_up"][0]
        moe_dn = A["moe_w_down"][0].rearrange("e f n -> (e f) n")

        @block.sync
        def _(sp_):
            sp_.dma_start(res[:, 0, :], A["x"][0][0:P, :]).then_inc(x_landed, 16)
            sp_.dma_start(res[:, 1, :], A["x"][0][P:SEQ, :]).then_inc(x_landed, 16)

            def load(base, src, rounds=0):
                slot_n = base % RAW
                if base >= RAW:
                    sp_.wait_ge(lo_ready, base - (RAW - 1) + RAW * rounds)
                dst = raw[:, slot_n, :].rearrange("p (k n) -> p k n", k=src.shape[1])
                sp_.dma_start(dst, src).then_inc(unit_landed[slot_n], 16)

            for n, src in enumerate(rec_units):
                load(n, src)
            with sp_.Fori(0, NB) as j:
                for k in range(BLOCK_UNITS):
                    if k < 4:
                        col = (k // 2) * FF
                        src = tile4(ffn_gu[(k % 2) * NC:(k % 2 + 1) * NC, bass.ds(col + NC * j, NC)])
                    else:
                        src = tile4(ffn_dn[bass.ds(NC * j, NC), (k - 4) * NC:(k - 3) * NC])
                    load(U_FFN + k, src, j)
            for n, src in enumerate(conv_units):
                load(U_PW1 + n, src)

            def gate_up(e, j, k):
                col = (k // 2) * FF
                return moe_gu[bass.ds(e, 1), (k % 2) * NC:(k % 2 + 1) * NC, bass.ds(col + NC * j, NC)].rearrange(
                    "e (k p) n -> p (e k) n", p=P)

            def down(s, c):
                return tile4(moe_dn[bass.ds(s * NC, NC), c * NC:(c + 1) * NC])

            def expert_step(e, j, first):
                s = NB * e + j
                for k in range(BLOCK_UNITS):
                    load(first - 2 + k, gate_up(e, j, k) if k < 4 else down(s - 1, k - 4), s)

            def expert_weights(first):
                for k in range(4):
                    load(first + k, gate_up(0, 0, k))
                with sp_.Fori(1, NB) as j:
                    expert_step(0, j, first)
                with sp_.Fori(1, NE) as e:
                    with sp_.Fori(0, NB) as j:
                        expert_step(e, j, first)
                for c in range(2):
                    load(first + NE * EXPERT_UNITS - 2 + c, down(NE * NB - 1, c))

            expert_weights(U_MOE)
            sp_.wait_ge(most_r, 1)
            crowd = sp_.value_load(most[0:1, 0:1], min_val=0, max_val=SEQ)
            with sp_.If(crowd > P):
                expert_weights(N_UNITS)
            sp_.nop()
            sp_.wait_ge(out_ready, 1)
            sp_.dma_start(out[0].rearrange("(t p) d -> p t d", p=P), normed_f[:, :, :]).then_inc(out_landed, 16)
            sp_.wait_ge(out_landed, 16)

        @block.gpsimd
        def _(pool):
            nc.gpsimd.memset(ident[:], 0.0).then_inc(pool_step, 1)
            pool.wait_ge(pool_step, 1)
            nc.gpsimd.affine_select(out=ident[:], in_=ident[:], compare_op=ALU.not_equal, fill=1.0, base=0,
                                    pattern=[[-1, P]], channel_multiplier=1).then_inc(consts, 1)
            nc.gpsimd.memset(mhalf[:], -0.5).then_inc(consts, 1)
            nc.gpsimd.memset(xpad[:, :, 0:REC_TAPS - 1], 0.0).then_inc(consts, 1)

            def root_of_var(n):
                pool.wait_ge(var_ready, n + 1)
                nc.gpsimd.tensor_tensor(rstd[:], var[:], mhalf[:], ALU.pow).then_inc(rstd_ready, 1)

            pool.wait_ge(consts, 3)
            root_of_var(0)
            for g in range(2):
                pool.wait_ge(i_out, 4 * (g + 1))
                pool.wait_ge(xc_lo_r, g + 1)
                s = slice(4 * g, 4 * g + 4)
                nc.gpsimd.tensor_tensor(ig[:, s, :], ig[:, s, :], xc[:, s, :], ALU.mult).then_inc(gated, 1)
            root_of_var(1)
            root_of_var(2)
            nc.gpsimd.memset(upad[:, :, 0:DW_TAPS - 1], 0.0).then_inc(consts, 1)
            nc.gpsimd.memset(mean_w[:], 1.0 / D).then_inc(consts, 1)
            pool.wait_ge(lnv_ready, 1)
            nc.gpsimd.tensor_tensor(ln_rstd[:], ln_var[:], mhalf[:], ALU.pow).then_inc(lnr_ready, 1)
            root_of_var(3)
            nc.gpsimd.memset(zeros[:].bitcast(F32), 0.0).then_inc(consts, 1)
            nc.gpsimd.memset(ones[:], 1.0).then_inc(pool_step, 1)
            nc.gpsimd.memset(earlier[:], 1.0).then_inc(pool_step, 1)
            nc.gpsimd.iota(iota[:], [[1, 2 * P]], base=0, channel_multiplier=0,
                           allow_small_or_imprecise_dtypes=True).then_inc(consts, 1)
            pool.wait_ge(pool_step, 3)
            nc.gpsimd.affine_select(out=earlier[:], in_=earlier[:], compare_op=ALU.is_ge, fill=0.0, base=-1,
                                    pattern=[[1, NE], [-1, NE]], channel_multiplier=0).then_inc(consts, 1)
            nc.gpsimd.affine_select(out=upper[:], in_=ones[:], compare_op=ALU.is_ge, fill=0.0, base=-1,
                                    pattern=[[1, P]], channel_multiplier=-1).then_inc(consts, 1)
            root_of_var(4)

        @block.scalar
        def _(act):
            act.dma_start(vec_rows[:, :], A["vectors"]).then_inc(vecs_landed, 16)

            steps = [0]

            def link(ins):
                steps[0] += 1
                ins.then_inc(act_step, 1)
                act.wait_ge(act_step, steps[0])

            def split_hi(base, rounds=0):
                slot_n, part = base % RAW, base % PARTS
                act.wait_ge(unit_landed[slot_n], 16 * (base // RAW + 1) + 16 * rounds)
                if base >= PARTS:
                    act.wait_ge(units_used, base - (PARTS - 1) + RAW * rounds)
                nc.scalar.activation(w_hi[:, part, :], raw[:, slot_n, :], ACT.Copy).then_inc(hi_ready, 1)

            def norm_square(n, keep):
                if n:
                    act.wait_ge(res_ready, n)
                else:
                    act.wait_ge(x_landed, 32)
                for t in range(TT):
                    nc.scalar.activation(keep[:, t, :], res[:, t, :], ACT.Square,
                                         accum_out=ss[:, t:t + 1]).then_inc(squares, 1)

            def norm_hi(n, vrow):
                act.wait_ge(norm_t, n + 1)
                act.wait_ge(colv_ready, 1)
                for k in range(KT):
                    nc.scalar.activation(xt_hi[:, k, :], ps[:, k // 2, (k % 2) * SEQ:(k % 2 + 1) * SEQ], ACT.Copy,
                                         scale=colv[:, k, vrow:vrow + 1]).then_inc(xt_hi_ready, 1)

            norm_square(0, normed)
            split_hi(0), split_hi(1), split_hi(2)
            norm_hi(0, V_MIX)
            act.wait_ge(lam_neg, 1)
            nc.scalar.activation(sp[:, 1, :], sp[:, 0, :], ACT.Exp).then_inc(lam_exp, 1)
            split_hi(3)

            def x_evac(g):
                act.wait_ge(units_used, 2 * g + 2)
                b = 4 - 4 * g
                nc.scalar.activation(xpad[:, 4 * g:4 * g + 4, REC_TAPS - 1:], ps[:, b:b + 4, 0:SEQ], ACT.Copy).then_inc(x_out, 1)

            def xc_round(g):
                act.wait_ge(conv_done, g + 1)
                nc.scalar.activation(xc_hi[:, 4 * g:4 * g + 4, :], xc[:, 4 * g:4 * g + 4, :], ACT.Copy).then_inc(xc_hi_r, 1)

            def y_evac(g, used):
                act.wait_ge(units_used, used)
                nc.scalar.activation(yb[:, 4 * g:4 * g + 4, :], ps[:, 4:8, 0:SEQ], ACT.Gelu_apprx_tanh).then_inc(y_out, 1)

            def gate_evac(g, dst, bank, vrow, ready):
                for k in range(4 * g, 4 * g + 4):
                    nc.scalar.activation(dst[:, k, :], ps[:, bank + k // 2, (k % 2) * SEQ:(k % 2 + 1) * SEQ], ACT.Sigmoid,
                                         bias=colv[:, k, vrow:vrow + 1]).then_inc(ready, 1)

            x_evac(0)
            split_hi(4), split_hi(5)
            x_evac(1)
            xc_round(0)
            split_hi(6)
            xc_round(1)
            split_hi(7)
            y_evac(0, 6)
            split_hi(8)
            act.wait_ge(units_used, U_GATES + 1)
            gate_evac(0, rg, 0, V_GA, r_out)
            gate_evac(1, rg, 0, V_GA, r_out)
            split_hi(9)
            act.wait_ge(units_used, U_GATES + 2)
            gate_evac(0, ig, 4, V_GX, i_out)
            gate_evac(1, ig, 4, V_GX, i_out)
            act.wait_ge(lam_ready, 1)
            act.wait_ge(r_out, KT)
            for k in range(KT):
                nc.scalar.activation(rg[:, k, :], rg[:, k, :], ACT.Tanh, scale=sp[:, 7, k:k + 1]).then_inc(tau_ready, 1)
            for g in range(2):
                s = slice(4 * g, 4 * g + 4)
                act.wait_ge(tau_ready, 4 * g + 4)
                nc.scalar.activation(root[:, s, :], rg[:, s, :], ACT.Sqrt).then_inc(root_ready, 1)
            split_hi(10)
            y_evac(1, U_Y1 + 2)
            split_hi(11), split_hi(12)
            for g in range(2):
                s = slice(4 * g, 4 * g + 4)
                act.wait_ge(z_ready, g + 1)
                nc.scalar.activation(xc_hi[:, s, :], yb[:, s, :], ACT.Copy).then_inc(z_hi_r, 1)
                if g == 0:
                    split_hi(13)
            split_hi(14), split_hi(15)

            norm_square(1, normed_f)
            split_hi(16)
            norm_hi(1, V_FFN)

            def ffn_act(j, base, skip):
                for k in range(skip, 4):
                    split_hi(base + k, j)
                act.wait_ge(f_gate, j + 1)
                nc.scalar.activation(sil[:, 0, :], ps[:, 0, :], ACT.Silu).then_inc(f_sil, 1)
                act.wait_ge(units_used, base + 2 + BLOCK_UNITS * j)
                nc.scalar.activation(sil[:, 1, :], ps[:, 2, :], ACT.Silu).then_inc(f_sil, 1)
                split_hi(base + 4, j), split_hi(base + 5, j)
                for c in range(TT):
                    act.wait_ge(f_t, c + 1 + TT * j)
                    nc.scalar.activation(ht_hi[:, c, :, :], ps[:, 2 * c, :].rearrange("p (q n) -> p q n", q=4),
                                         ACT.Copy).then_inc(f_hthi, 1)

            ffn_act(0, U_FFN, 3)
            with act.Fori(1, NB) as j:
                ffn_act(j, U_FFN, 0)

            split_hi(U_PW1), split_hi(U_PW1 + 1)
            norm_square(2, normed_c)
            split_hi(U_PW1 + 2)
            act.dma_start(bias_row[:, :], A["cnv_b_pw2"][0:1, :].broadcast_to([P, D])).then_inc(late_landed, 16)
            norm_hi(2, V_MIX + 1)
            split_hi(U_PW1 + 3)
            for i in (4, 5):
                split_hi(U_PW1 + i)
            for g in range(2):
                act.wait_ge(units_used, U_PW1 + 4 * g + 4)
                for i in range(4):
                    if g:
                        act.wait_ge(c_u, i + 1)
                    nc.scalar.activation(sig[:, i, :], ps[:, i, 0:SEQ], ACT.Sigmoid,
                                         bias=colv[:, 4 * g + i, V_PW + 1:V_PW + 2]).then_inc(c_sig, 1)
                for u in ((U_PW1 + 6, U_PW1 + 7, U_PW2, U_PW2 + 1) if g == 0 else (U_PW2 + 2,)):
                    split_hi(u)
            for k in range(KT):
                for i in range(PE_TAPS):
                    n = k * PE_TAPS + i
                    if n >= 4:
                        act.wait_ge(diag_used, n - 3)
                    nc.scalar.activation(diag[:, n % 4, :], ident[:], ACT.Copy,
                                         scale=colv[:, k, V_DW + i:V_DW + i + 1]).then_inc(diag_ready, 1)
            act.wait_ge(centred, 2)
            for g in range(2):
                s = slice(4 * g, 4 * g + 4)
                nc.scalar.activation(sq[:, s, :], dw[:, s, :], ACT.Square).then_inc(sq_ready, 1)
            for k in range(KT):
                act.wait_ge(ln_done, k // 4 + 1)
                nc.scalar.activation(act_c[:, k, :], sq[:, k, :], ACT.Silu, scale=colv[:, k, V_LNG:V_LNG + 1],
                                     bias=colv[:, k, V_LNB:V_LNB + 1]).then_inc(silu_c, 1)
                if k % 4 == 3:
                    g = k // 4
                    s = slice(4 * g, 4 * g + 4)
                    act.wait_ge(silu_c, k + 1)
                    nc.scalar.activation(z_hi[:, s, :], act_c[:, s, :], ACT.Copy).then_inc(cz_hi, 1)
            split_hi(U_PW2 + 3)

            norm_square(3, normed_f)
            act.dma_start(router[:, :, :], A["moe_router"][0].rearrange("(k p) e -> p k e", p=P)).then_inc(late_landed, 16)
            act.dma_start(grow[:, :], A["norm_ffn"][1:2, :].broadcast_to([P, D])).then_inc(late_landed, 16)
            act.wait_ge(xs_ready, 1)
            nc.scalar.activation(xs_hi[:, :, :], normed_f[:, :, :], ACT.Copy).then_inc(xs_hi_r, 1)
            act.wait_ge(xr_t, 1)
            nc.scalar.activation(routed_t[:, :, :], ps[:, 0:4, :], ACT.Copy).then_inc(xr_out, 1)
            act.wait_ge(lmax_r, 1)
            nc.scalar.activation(gate[:, :, :], gate[:, :, :], ACT.Exp).then_inc(exp_l, 1)

            def expert_pass(p, first):
                n0, s0 = p * NE, p * NE * NB

                def tokens_in(n):
                    act.wait_ge(gathered, n + 1 + p * (NE + 1))
                    if not isinstance(n, int) or n > 0:
                        act.wait_ge(units_used, RAW * (NB * n - 1) + first + 2)
                    nc.scalar.activation(xe_hi[:, :, :].rearrange("p k n -> p (k n)"),
                                         ps[:, 6:8, :].rearrange("p b n -> p (b n)"), ACT.Copy).then_inc(xe_hi_r, 1)

                def silu(s, gate_done):
                    act.wait_ge(units_used, gate_done)
                    if not isinstance(s, int):
                        act.wait_ge(m_hid, s0 + s)
                    nc.scalar.activation(sil[:, 0, :], ps[:, 0, :], ACT.Silu).then_inc(m_sil, 1)

                def round_hidden(s):
                    act.wait_ge(m_t, s0 + 1 + s)
                    nc.scalar.activation(ht_hi[:, 0, :, :].rearrange("p q n -> p (q n)"), ps[:, 2, :],
                                         ACT.Copy).then_inc(m_hthi, 1)

                def round_output(e, used):
                    act.wait_ge(units_used, used)
                    nc.scalar.activation(ye_hi[:, :], ps[:, 4:6, :].rearrange("p b n -> p (b n)"), ACT.Copy).then_inc(ye_hi_r, 1)

                def keep_place(e, scattered_before):
                    if scattered_before is not None:
                        act.wait_ge(scattered, scattered_before)
                    act.wait_ge(pick_t, e + 1 + p * (NE + 1))
                    nc.scalar.activation(place_e[:, :, :].rearrange("p t n -> p (t n)"), ps[:, 3, 0:TT * P],
                                         ACT.Copy).then_inc(place_r, 1)

                def step(e, j, output_of_last=False):
                    s = NB * e + j
                    for k in (0, 1):
                        split_hi(first - 2 + k, s)
                    if output_of_last:
                        round_output(e - 1, first - 2 + RAW * s)
                    for k in (2, 3):
                        split_hi(first - 2 + k, s)
                    silu(s, first + RAW * s)
                    round_hidden(s - 1)
                    for k in (4, 5):
                        split_hi(first - 2 + k, s)

                split_hi(first)
                tokens_in(0)
                for k in (1, 2, 3):
                    split_hi(first + k)
                silu(0, first + 2)
                with act.Fori(1, 2) as j:
                    step(0, j)
                keep_place(0, None)
                with act.Fori(2, NB) as j:
                    step(0, j)
                tokens_in(1)
                with act.Fori(1, NE) as e:
                    step(e, 0)
                    step(e, 1, output_of_last=True)
                    keep_place(e, TT * (n0 + e))
                    with act.Fori(2, NB) as j:
                        step(e, j)
                    tokens_in(e + 1)
                last = first + NE * EXPERT_UNITS - 2
                split_hi(last), split_hi(last + 1)
                round_hidden(NE * NB - 1)
                round_output(NE - 1, last + 2)

            expert_pass(0, U_MOE)
            act.wait_ge(most_r, 1)
            crowd = act.value_load(most[0:1, 0:1], min_val=0, max_val=SEQ)
            with act.If(crowd > P):
                expert_pass(1, N_UNITS)

            act.wait_ge(moe_over, 1)
            act.dma_start(grow[:, :], A["norm_out"].rearrange("(o n) -> o n", o=1).broadcast_to([P, D])).then_inc(gout_landed, 16)
            for t in range(TT):
                nc.scalar.activation(normed_f[:, t, :], res[:, t, :], ACT.Square, accum_out=ss[:, t:t + 1]).then_inc(squares, 1)

        @block.vector
        def _(dve):
            steps = [0]

            def link(ins):
                steps[0] += 1
                ins.then_inc(dve_step, 1)
                dve.wait_ge(dve_step, steps[0])

            def split_lo(base, rounds=0):
                slot_n, part = base % RAW, base % PARTS
                dve.wait_ge(hi_ready, base + 1 + RAW * rounds)
                nc.vector.tensor_tensor(w_lo[:, part, :], raw[:, slot_n, :], w_hi[:, part, :].bitcast(F32),
                                        ALU.subtract).then_inc(lo_ready, 1)

            def norm_scale(n, keep):
                dve.wait_ge(squares, TT * (n + 1))
                nc.vector.tensor_scalar(var[:], ss[:], 1.0 / D, RMS_EPS, ALU.mult, ALU.add).then_inc(var_ready, 1)
                dve.wait_ge(rstd_ready, n + 1)
                for t in range(TT):
                    nc.vector.tensor_scalar(keep[:, t, :], res[:, t, :], rstd[:, t:t + 1], None,
                                            ALU.mult).then_inc(normed_ready, 1)

            def norm_lo(n, vrow):
                for k in range(KT):
                    dve.wait_ge(xt_hi_ready, KT * n + (k | 1) + 1)
                    nc.vector.scalar_tensor_tensor(
                        out=xt_lo[:, k, :], in0=ps[:, k // 2, (k % 2) * SEQ:(k % 2 + 1) * SEQ],
                        scalar=colv[:, k, vrow:vrow + 1], in1=xt_hi[:, k, :].bitcast(F32),
                        op0=ALU.mult, op1=ALU.subtract).then_inc(xt_lo_ready, 1)

            norm_scale(0, normed)
            dve.wait_ge(vec_t, 1)
            nc.vector.tensor_copy(colv[:, :, :].rearrange("p k v -> p (k v)"), ps[:, 7, 0:KT * NV]).then_inc(colv_ready, 1)
            split_lo(0), split_lo(1)
            dve.wait_ge(colv_ready, 1)
            norm_lo(0, V_MIX)
            link(nc.vector.tensor_scalar(sp[:, 0, :], colv[:, :, V_LAM], -1.0, None, ALU.mult))
            nc.vector.tensor_tensor(sp[:, 0, :], sp[:, 0, :], colv[:, :, V_LAM], ALU.min).then_inc(lam_neg, 1)
            split_lo(2), split_lo(3)

            def conv4(g):
                dve.wait_ge(x_out, g + 1)
                for i in range(REC_TAPS):
                    tap = REC_TAPS - 1 - i
                    for k in range(4 * g, 4 * g + 4):
                        src = xpad[:, k, tap:tap + SEQ]
                        w = colv[:, k, V_CW + tap:V_CW + tap + 1]
                        if i == 0:
                            ins = nc.vector.tensor_scalar(xc[:, k, :], src, w, colv[:, k, V_CB:V_CB + 1], ALU.mult, ALU.add)
                        else:
                            ins = nc.vector.scalar_tensor_tensor(out=xc[:, k, :], in0=src, scalar=w, in1=xc[:, k, :],
                                                                 op0=ALU.mult, op1=ALU.add)
                        if i == REC_TAPS - 1:
                            if k == 4 * g + 3:
                                ins.then_inc(conv_done, 1)
                        elif k == 4 * g + 3:
                            link(ins)

            def xc_rest(g):
                dve.wait_ge(xc_hi_r, g + 1)
                s = slice(4 * g, 4 * g + 4)
                nc.vector.tensor_tensor(xc_lo[:, s, :], xc[:, s, :], xc_hi[:, s, :].bitcast(F32), ALU.subtract).then_inc(xc_lo_r, 1)

            dve.wait_ge(consts, 3)
            conv4(0)
            split_lo(4)
            xc_rest(0)
            split_lo(5)
            conv4(1)
            split_lo(6)
            xc_rest(1)
            split_lo(7), split_lo(8)
            dve.wait_ge(lam_exp, 1)
            ex, y, y2, acc = sp[:, 1, :], sp[:, 2, :], sp[:, 3, :], sp[:, 4, :]
            link(nc.vector.tensor_scalar(y2, ex, 2.0, None, ALU.add))
            link(nc.vector.reciprocal(acc, y2))
            link(nc.vector.tensor_tensor(y, ex, acc, ALU.mult))
            link(nc.vector.tensor_tensor(y2, y, y, ALU.mult))
            link(nc.vector.memset(acc, 1.0 / 19))
            for n in range(17, 0, -2):
                link(nc.vector.tensor_tensor(acc, acc, y2, ALU.mult))
                link(nc.vector.tensor_scalar(acc, acc, 1.0 / n, None, ALU.add))
            link(nc.vector.tensor_tensor(acc, acc, y, ALU.mult))
            link(nc.vector.tensor_scalar(sp[:, 5, :], colv[:, :, V_LAM], -1.0, 0.0, ALU.mult, ALU.max))
            link(nc.vector.scalar_tensor_tensor(out=sp[:, 6, :], in0=acc, scalar=2.0, in1=sp[:, 5, :],
                                                op0=ALU.mult, op1=ALU.add))
            nc.vector.tensor_scalar(sp[:, 7, :], sp[:, 6, :], 4.0, None, ALU.mult).then_inc(lam_ready, 1)
            split_lo(9), split_lo(10)
            for g in range(2):
                s = slice(4 * g, 4 * g + 4)
                dve.wait_ge(tau_ready, 4 * g + 4)
                link(nc.vector.tensor_scalar(rtmp[:, s, :], rg[:, s, :], -1.0, -1.0, ALU.mult, ALU.add))
                link(nc.vector.reciprocal(rtmp[:, s, :], rtmp[:, s, :]))
                dve.wait_ge(root_ready, g + 1)
                link(nc.vector.scalar_tensor_tensor(out=rg[:, s, :], in0=rg[:, s, :], scalar=1.0, in1=rtmp[:, s, :],
                                                    op0=ALU.subtract, op1=ALU.mult))
                link(nc.vector.scalar_tensor_tensor(out=root[:, s, :], in0=root[:, s, :], scalar=-2.0, in1=rtmp[:, s, :],
                                                    op0=ALU.mult, op1=ALU.mult))
                dve.wait_ge(gated, g + 1)
                link(nc.vector.tensor_tensor(root[:, s, :], root[:, s, :], ig[:, s, :], ALU.mult))
                for k in range(4 * g, 4 * g + 4):
                    ins = nc.vector.tensor_tensor_scan(rtmp[:, k, :], rg[:, k, :], root[:, k, :], 0.0, ALU.mult, ALU.add)
                link(ins)
                dve.wait_ge(y_out, g + 1)
                nc.vector.tensor_tensor(yb[:, s, :], yb[:, s, :], rtmp[:, s, :], ALU.mult).then_inc(z_ready, 1)
                if g == 0:
                    split_lo(11)
                dve.wait_ge(z_hi_r, g + 1)
                nc.vector.tensor_tensor(xc_lo[:, s, :], yb[:, s, :], xc_hi[:, s, :].bitcast(F32), ALU.subtract).then_inc(z_lo_r, 1)
                if g == 0:
                    split_lo(12)
            split_lo(13), split_lo(14), split_lo(15)

            def add_residual(used, bank):
                dve.wait_ge(units_used, used)
                for t in range(TT):
                    ins = nc.vector.tensor_tensor(res[:, t, :], res[:, t, :],
                                                  ps[:, bank + 2 * t:bank + 2 * t + 2, :].rearrange("p b n -> p (b n)"), ALU.add)
                ins.then_inc(res_ready, 1)

            add_residual(U_FFN, 0)

            norm_scale(1, normed_f)
            split_lo(16)
            norm_lo(1, V_FFN)

            def ffn_dve(j, base, skip):
                for k in range(skip, BLOCK_UNITS):
                    split_lo(base + k, j)
                for c in range(TT):
                    dve.wait_ge(f_sil, c + 1 + TT * j)
                    if c == 0:
                        dve.wait_ge(f_up, j + 1)
                    else:
                        dve.wait_ge(units_used, base + 4 + BLOCK_UNITS * j)
                    nc.vector.tensor_tensor(hid[:, c, :], sil[:, c, :], ps[:, 2 * c + 1, :], ALU.mult).then_inc(f_hid, 1)
                for c in range(TT):
                    dve.wait_ge(f_hthi, c + 1 + TT * j)
                    nc.vector.tensor_tensor(ht_lo[:, c, :, :].rearrange("p q n -> p (q n)"), ps[:, 2 * c, :],
                                            ht_hi[:, c, :, :].bitcast(F32).rearrange("p q n -> p (q n)"),
                                            ALU.subtract).then_inc(f_htlo, 1)

            ffn_dve(0, U_FFN, 3)
            with dve.Fori(1, NB) as j:
                ffn_dve(j, U_FFN, 0)
            split_lo(U_PW1), split_lo(U_PW1 + 1)
            add_residual(U_PW1, 4)

            norm_scale(2, normed_c)
            split_lo(U_PW1 + 2)
            norm_lo(2, V_MIX + 1)
            split_lo(U_PW1 + 3)
            split_lo(U_PW1 + 4), split_lo(U_PW1 + 5)

            def glu(g):
                for i in range(4):
                    k = 4 * g + i
                    dve.wait_ge(c_sig, k + 1)
                    nc.vector.scalar_tensor_tensor(
                        out=upad[:, k, DW_TAPS - 1:], in0=ps[:, 4 + i, 0:SEQ],
                        scalar=colv[:, k, V_PW:V_PW + 1], in1=sig[:, i, :], op0=ALU.add, op1=ALU.mult).then_inc(c_u, 1)

            def taps(g, count):
                for tap in count:
                    for k in range(4 * g, 4 * g + 4):
                        src = upad[:, k, tap:tap + SEQ]
                        w = colv[:, k, V_DW + tap:V_DW + tap + 1]
                        if tap == DW_TAPS - 1:
                            ins = nc.vector.tensor_scalar(dw[:, k, :], src, w, colv[:, k, V_DWB:V_DWB + 1], ALU.mult, ALU.add)
                        else:
                            ins = nc.vector.scalar_tensor_tensor(out=dw[:, k, :], in0=src, scalar=w, in1=dw[:, k, :],
                                                                 op0=ALU.mult, op1=ALU.add)
                    link(ins)

            def join_taps(g):
                for k in range(4 * g, 4 * g + 4):
                    dve.wait_ge(diag_used, (k + 1) * PE_TAPS)
                    nc.vector.tensor_tensor(dw[:, k, :], dw[:, k, :], ps[:, k % 4, 0:SEQ], ALU.add).then_inc(dw_done, 1)

            mine = list(range(DW_TAPS - 1, PE_TAPS - 1, -1))
            glu(0)
            dve.wait_ge(consts, 5)
            dve.wait_ge(c_u, 4)
            taps(0, mine[:1])
            split_lo(U_PW1 + 6)
            taps(0, mine[1:4])
            split_lo(U_PW1 + 7)
            taps(0, mine[4:8])
            glu(1)
            dve.wait_ge(c_u, KT)
            for u in range(U_PW2, U_PW2 + 3):
                split_lo(u)
            taps(0, mine[8:])
            join_taps(0)
            taps(1, mine)
            join_taps(1)
            dve.wait_ge(mean_t, 1)
            for g in range(2):
                s = slice(4 * g, 4 * g + 4)
                nc.vector.tensor_tensor(dw[:, s, :], dw[:, s, :], ps[:, 4:5, 0:SEQ].broadcast_to([P, 4, SEQ]),
                                        ALU.subtract).then_inc(centred, 1)
            dve.wait_ge(var_t, 1)
            nc.vector.tensor_scalar(ln_var[:], ps[:, 5, 0:TT], LN_EPS, None, ALU.add).then_inc(lnv_ready, 1)
            dve.wait_ge(lnr_ready, 1)
            for t in range(TT):
                ins = nc.vector.tensor_scalar(spread[:, t, :], ident[:], ln_rstd[:, t:t + 1], float(D), ALU.mult, ALU.mult)
            ins.then_inc(spread_r, 1)
            dve.wait_ge(lnb_t, 1)
            for g in range(2):
                s = slice(4 * g, 4 * g + 4)
                nc.vector.tensor_tensor(sq[:, s, :], dw[:, s, :], ps[:, 6:7, 0:SEQ].broadcast_to([P, 4, SEQ]),
                                        ALU.mult).then_inc(ln_done, 1)
            for g in range(2):
                s = slice(4 * g, 4 * g + 4)
                dve.wait_ge(cz_hi, g + 1)
                nc.vector.tensor_tensor(z_lo[:, s, :], act_c[:, s, :], z_hi[:, s, :].bitcast(F32), ALU.subtract).then_inc(cz_lo, 1)
            split_lo(U_PW2 + 3)
            dve.wait_ge(late_landed, 16)
            for t in range(TT):
                ins = nc.vector.tensor_tensor(res[:, t, :], res[:, t, :], bias_row[:, :], ALU.add)
            link(ins)
            add_residual(U_MOE, 0)

            dve.wait_ge(squares, TT * 4)
            nc.vector.tensor_scalar(var[:], ss[:], 1.0 / D, RMS_EPS, ALU.mult, ALU.add).then_inc(var_ready, 1)
            dve.wait_ge(rstd_ready, 4)
            dve.wait_ge(late_landed, 48)
            for t in range(TT):
                ins = nc.vector.scalar_tensor_tensor(out=normed_f[:, t, :], in0=res[:, t, :], scalar=rstd[:, t:t + 1],
                                                     in1=grow[:, :], op0=ALU.mult, op1=ALU.mult)
            ins.then_inc(xs_ready, 1)
            dve.wait_ge(xs_hi_r, 1)
            nc.vector.tensor_tensor(xs_lo[:, :, :], normed_f[:, :, :], xs_hi[:, :, :].bitcast(F32), ALU.subtract).then_inc(xs_lo_r, 1)
            dve.wait_ge(consts, 9)
            dve.wait_ge(logits_t, 1)
            link(nc.vector.tensor_copy(logit[:, :, :], ps[:, 4:6, 0:NE]))
            for t in range(TT):
                other = logit[:, t:t + 1, :].broadcast_to([P, NE, NE])
                own = logit[:, t, :].unsqueeze(2).broadcast_to([P, NE, NE])
                nc.vector.tensor_tensor(cmp_gt[:, t, :, :], other, own, ALU.is_gt)
                ins = nc.vector.tensor_tensor(cmp_eq[:, t, :, :], other, own, ALU.is_equal)
            link(ins)
            for t in range(TT):
                ins = nc.vector.tensor_tensor(cmp_eq[:, t, :, :], cmp_eq[:, t, :, :], earlier[:, :, :], ALU.mult)
            link(ins)
            link(nc.vector.tensor_tensor(cmp_gt[:, :, :, :].rearrange("p t a b -> p (t a b)"),
                                         cmp_gt[:, :, :, :].rearrange("p t a b -> p (t a b)"),
                                         cmp_eq[:, :, :, :].rearrange("p t a b -> p (t a b)"), ALU.add))
            link(nc.vector.tensor_reduce(rank[:, :, :].rearrange("p t e -> p (t e)"),
                                         cmp_gt[:, :, :, :].rearrange("p t a b -> p (t a) b"), AX.X, ALU.add))
            nc.vector.tensor_scalar(chosen[:, :, :], rank[:, :, :], 1.5, None, ALU.is_lt).then_inc(ranked, 1)
            link(nc.vector.tensor_reduce(small[:, 0:TT], logit[:, :, :], AX.X, ALU.max))
            nc.vector.tensor_tensor(gate[:, :, :], logit[:, :, :], small[:, 0:TT].unsqueeze(2).broadcast_to([P, TT, NE]),
                                    ALU.subtract).then_inc(lmax_r, 1)
            link(nc.vector.memset(slot[:, :, NE:NE + 1], -1.0))
            dve.wait_ge(counted, 1)
            link(nc.vector.tensor_scalar(slot[:, :, 0:NE], ps[:, 6, 0:TT * NE].rearrange("p (t e) -> p t e", t=TT), 1.0, None, ALU.add))
            link(nc.vector.tensor_tensor(slot[:, :, 0:NE], slot[:, :, 0:NE], chosen[:, :, :], ALU.mult))
            link(nc.vector.tensor_scalar(slot[:, :, 0:NE], slot[:, :, 0:NE], 1.0, None, ALU.subtract))
            dve.wait_ge(exp_l, 1)
            dve.wait_ge(ranked, 1)
            link(nc.vector.tensor_tensor(gate[:, :, :], gate[:, :, :], chosen[:, :, :], ALU.mult))
            link(nc.vector.tensor_reduce(small[:, 2:2 + TT], gate[:, :, :], AX.X, ALU.add))
            link(nc.vector.reciprocal(small[:, 4:4 + TT], small[:, 2:2 + TT]))
            link(nc.vector.tensor_tensor(gate[:, :, :], gate[:, :, :],
                                         small[:, 4:4 + TT].unsqueeze(2).broadcast_to([P, TT, NE]), ALU.mult))
            link(nc.vector.tensor_reduce(small[:, 6:7], ps[:, 7, 0:NE], AX.X, ALU.max))
            nc.vector.tensor_copy(most[:, :], small[:, 6:7]).then_inc(most_r, 1)

            def expert_pass(p, first):
                n0, s0 = p * NE, p * NE * NB

                def make_pick(n):
                    if not isinstance(n, int):
                        dve.wait_ge(pick_t, n + p * (NE + 1))
                    for t in range(TT):
                        ins = nc.vector.tensor_scalar(pick[:, t, :], iota[:, p * P:(p + 1) * P],
                                                      slot[:, t, bass.ds(n, 1)], None, ALU.is_equal)
                    ins.then_inc(pick_r, 1)

                def tokens_in(n):
                    dve.wait_ge(xe_hi_r, n + 1 + p * (NE + 1))
                    nc.vector.tensor_tensor(xe_lo[:, :, :].rearrange("p k n -> p (k n)"),
                                            ps[:, 6:8, :].rearrange("p b n -> p (b n)"),
                                            xe_hi[:, :, :].bitcast(F32).rearrange("p k n -> p (k n)"),
                                            ALU.subtract).then_inc(xe_lo_r, 1)

                def hidden(s, up_done):
                    dve.wait_ge(m_sil, s0 + 1 + s)
                    dve.wait_ge(units_used, up_done)
                    nc.vector.tensor_tensor(hid[:, 0, :], sil[:, 0, :], ps[:, 1, :], ALU.mult).then_inc(m_hid, 1)

                def rest_hidden(s):
                    dve.wait_ge(m_hthi, s0 + 1 + s)
                    nc.vector.tensor_tensor(ht_lo[:, 0, :, :].rearrange("p q n -> p (q n)"), ps[:, 2, :],
                                            ht_hi[:, 0, :, :].bitcast(F32).rearrange("p q n -> p (q n)"),
                                            ALU.subtract).then_inc(m_htlo, 1)

                def rest_output(e):
                    dve.wait_ge(ye_hi_r, n0 + 1 + e)
                    nc.vector.tensor_tensor(ye_lo[:, :], ps[:, 4:6, :].rearrange("p b n -> p (b n)"), ye_hi[:, :].bitcast(F32),
                                            ALU.subtract).then_inc(ye_lo_r, 1)

                def add_output(e, t, bank=6):
                    dve.wait_ge(scattered, TT * (n0 + e) + t + 1)
                    nc.vector.scalar_tensor_tensor(
                        out=res[:, t, :], in0=ps[:, bank:bank + 2, :].rearrange("p b n -> p (b n)"),
                        scalar=gate[:, t, bass.ds(e, 1)], in1=res[:, t, :], op0=ALU.mult, op1=ALU.add).then_inc(added, 1)

                def step(e, j, output_of_last=False):
                    s = NB * e + j
                    for k in (0, 1):
                        split_lo(first - 2 + k, s)
                    if output_of_last:
                        rest_output(e - 1)
                    split_lo(first, s)
                    if output_of_last:
                        add_output(e - 1, 0)
                    split_lo(first + 1, s)
                    rest_hidden(s - 1)
                    for k in (4, 5):
                        split_lo(first - 2 + k, s)
                    hidden(s, first + 2 + RAW * s)
                    if output_of_last:
                        add_output(e - 1, 1)

                make_pick(0)
                split_lo(first)
                tokens_in(0)
                for k in (1, 2, 3):
                    split_lo(first + k)
                hidden(0, first + 4)
                with dve.Fori(1, 2) as j:
                    step(0, j)
                with dve.Fori(1, 2) as n:
                    make_pick(n)
                with dve.Fori(2, NB) as j:
                    step(0, j)
                tokens_in(1)
                with dve.Fori(1, NE) as e:
                    step(e, 0)
                    step(e, 1, output_of_last=True)
                    make_pick(e + 1)
                    with dve.Fori(2, NB) as j:
                        step(e, j)
                    tokens_in(e + 1)
                last = first + NE * EXPERT_UNITS - 2
                split_lo(last), split_lo(last + 1)
                rest_hidden(NE * NB - 1)
                rest_output(NE - 1)
                add_output(NE - 1, 0)
                add_output(NE - 1, 1, bank=0)

            expert_pass(0, U_MOE)
            dve.wait_ge(most_r, 1)
            crowd = dve.value_load(most[0:1, 0:1], min_val=0, max_val=SEQ)
            with dve.If(crowd > P):
                expert_pass(1, N_UNITS)

            nc.vector.memset(small[:, 7:8], 0.0).then_inc(moe_over, 1)
            dve.wait_ge(squares, TT * 5)
            nc.vector.tensor_scalar(var[:], ss[:], 1.0 / D, RMS_EPS, ALU.mult, ALU.add).then_inc(var_ready, 1)
            dve.wait_ge(rstd_ready, 5)
            dve.wait_ge(gout_landed, 16)
            for t in range(TT):
                ins = nc.vector.scalar_tensor_tensor(out=normed_f[:, t, :], in0=res[:, t, :], scalar=rstd[:, t:t + 1],
                                                     in1=grow[:, :], op0=ALU.mult, op1=ALU.mult)
            ins.then_inc(out_ready, 1)

        @block.tensor
        def _(pe):
            def passes(dst, stat, mov, start, stop, loose=False):
                (sh, sl), (mh, ml) = stat, mov
                nc.tensor.matmul(dst, sh, ml, start=start, stop=False, skip_group_check=loose)
                nc.tensor.matmul(dst, sl, mh, start=False, stop=False, skip_group_check=loose)
                return nc.tensor.matmul(dst, sh, mh, start=False, stop=stop, skip_group_check=loose)

            def norm_transpose(n, src):
                pe.wait_ge(normed_ready, TT * (n + 1))
                for k in range(KT):
                    for t in range(TT):
                        c = (k % 2) * SEQ + t * P
                        ins = nc.tensor.transpose(ps[:, k // 2, c:c + P], src[:, t, k * P:(k + 1) * P], ident[:])
                ins.then_inc(norm_t, 1)

            def channel_major(u0, banks, xt):
                for kh in range(2):
                    u = u0 + kh
                    pe.wait_ge(lo_ready, u + 1)
                    q = u % PARTS
                    for nt in range(4):
                        for k in range(4):
                            c = slice(k * NC + nt * P, k * NC + nt * P + P)
                            ins = passes(ps[:, banks + nt, 0:SEQ], (w_hi[:, q, c], w_lo[:, q, c]),
                                         (xt[0][:, 4 * kh + k, :], xt[1][:, 4 * kh + k, :]),
                                         start=(kh == 0 and k == 0), stop=(kh == 1 and k == 3))
                    ins.then_inc(units_used, 1)

            def token_major(u0, zt, bank, ready):
                for kh in range(2):
                    pe.wait_ge(ready, kh + 1)
                    for c in range(2):
                        u = u0 + 2 * kh + c
                        pe.wait_ge(lo_ready, u + 1)
                        q = u % PARTS
                        for t in range(TT):
                            for k in range(4):
                                s = slice(t * P, (t + 1) * P)
                                ins = passes(ps[:, bank + 2 * t + c, :], (zt[0][:, 4 * kh + k, s], zt[1][:, 4 * kh + k, s]),
                                             (w_hi[:, q, k * NC:(k + 1) * NC], w_lo[:, q, k * NC:(k + 1) * NC]),
                                             start=(kh == 0 and k == 0), stop=(kh == 1 and k == 3))
                        ins.then_inc(units_used, 1)

            pe.wait_ge(consts, 1)
            norm_transpose(0, normed)
            pe.wait_ge(vecs_landed, 16)
            for k in range(KT):
                ins = nc.tensor.transpose(ps[:, 7, k * NV:(k + 1) * NV], vec_rows[:, k * P:(k + 1) * P], ident[0:NV, 0:NV])
            ins.then_inc(vec_t, 1)
            pe.wait_ge(xt_lo_ready, KT)
            xt = (xt_hi, xt_lo)
            pe.wait_ge(colv_ready, 1)
            channel_major(0, 4, xt)
            channel_major(2, 0, xt)
            pe.wait_ge(x_out, 1)
            channel_major(4, 4, xt)
            pe.wait_ge(x_out, 2)
            pe.wait_ge(xc_lo_r, 2)
            for gate_n in range(2):
                u = U_GATES + gate_n
                pe.wait_ge(lo_ready, u + 1)
                if gate_n:
                    pe.wait_ge(y_out, 1)
                q = u % PARTS
                for h in range(HEADS):
                    for jt in range(2):
                        for k in range(2):
                            c = slice((2 * h + k) * 2 * P + jt * P, (2 * h + k) * 2 * P + jt * P + P)
                            ins = passes(ps[:, 4 * gate_n + h, jt * SEQ:(jt + 1) * SEQ],
                                         (w_hi[:, q, c], w_lo[:, q, c]),
                                         (xc_hi[:, 2 * h + k, :], xc_lo[:, 2 * h + k, :]), start=(k == 0), stop=(k == 1))
                ins.then_inc(units_used, 1)
            pe.wait_ge(i_out, KT)
            channel_major(U_Y1, 4, xt)
            token_major(U_OUT, (xc_hi, xc_lo), 0, z_lo_r)

            norm_transpose(1, normed_f)
            pe.wait_ge(xt_lo_ready, 2 * KT)

            def hidden_transpose(dst, src):
                for q in range(4):
                    ins = nc.tensor.transpose(dst[:, q * P:(q + 1) * P], src[:, q * P:(q + 1) * P], ident[:])
                return ins

            def project(dst, xt_k, q, k, start, stop, loose):
                return passes(dst, xt_k, (w_hi[:, q, k * NC:(k + 1) * NC], w_lo[:, q, k * NC:(k + 1) * NC]), start, stop, loose)

            def ffn_pe(j, first):
                for k6 in range(BLOCK_UNITS):
                    u = U_FFN + k6 + BLOCK_UNITS * j
                    q = (U_FFN + k6) % PARTS
                    if k6 == 4:
                        for c in range(TT):
                            pe.wait_ge(f_hid, c + 1 + TT * j)
                            hidden_transpose(ps[:, 2 * c, :], hid[:, c, :]).then_inc(f_t, 1)
                    pe.wait_ge(lo_ready, u + 1)
                    for c in range(TT):
                        if k6 == 4:
                            pe.wait_ge(f_htlo, c + 1 + TT * j)
                        for k in range(4):
                            if k6 < 4:
                                kk = 4 * (k6 % 2) + k
                                s = slice(c * P, (c + 1) * P)
                                ins = project(ps[:, 2 * c + k6 // 2, :], (xt_hi[:, kk, s], xt_lo[:, kk, s]), q, k,
                                              start=(kk == 0), stop=(kk == KT - 1), loose=False)
                            else:
                                ins = project(ps[:, 4 + 2 * c + k6 - 4, :], (ht_hi[:, c, k, :], ht_lo[:, c, k, :]), q, k,
                                              start=(first and k == 0), stop=False, loose=True)
                        if c == 0 and k6 in (1, 3):
                            ins.then_inc(f_gate if k6 == 1 else f_up, 1)
                    ins.then_inc(units_used, 1)

            pe.wait_ge(res_ready, 1)
            ffn_pe(0, True)
            with pe.Fori(1, NB) as j:
                ffn_pe(j, False)

            norm_transpose(2, normed_c)
            pe.wait_ge(xt_lo_ready, 3 * KT)
            for g in range(2):
                if g:
                    pe.wait_ge(c_u, 4)
                channel_major(U_PW1 + 4 * g, 4, xt)
                channel_major(U_PW1 + 4 * g + 2, 0, xt)
            pe.wait_ge(consts, 5)
            pe.wait_ge(c_sig, KT)
            for k in range(KT):
                pe.wait_ge(c_u, k + 1)
                if k >= 4:
                    pe.wait_ge(dw_done, k - 3)
                for i in range(PE_TAPS):
                    n = k * PE_TAPS + i
                    pe.wait_ge(diag_ready, n + 1)
                    nc.tensor.matmul(ps[:, k % 4, 0:SEQ], diag[:, n % 4, :], upad[:, k, i:i + SEQ],
                                     start=(i == 0), stop=(i == PE_TAPS - 1)).then_inc(diag_used, 1)
            for k in range(KT):
                pe.wait_ge(dw_done, k + 1)
                ins = nc.tensor.matmul(ps[:, 4, 0:SEQ], mean_w[:], dw[:, k, :], start=(k == 0), stop=(k == KT - 1))
            ins.then_inc(mean_t, 1)
            pe.wait_ge(sq_ready, 2)
            for t in range(TT):
                for k in range(KT):
                    ins = nc.tensor.matmul(ps[:, 5, t:t + 1], sq[:, k, t * P:(t + 1) * P], mean_w[:, 0:1],
                                           start=(k == 0), stop=(k == KT - 1))
            ins.then_inc(var_t, 1)
            pe.wait_ge(spread_r, 1)
            for t in range(TT):
                ins = nc.tensor.matmul(ps[:, 6, t * P:(t + 1) * P], mean_w[:], spread[:, t, :], start=True, stop=True)
            ins.then_inc(lnb_t, 1)
            token_major(U_PW2, (z_hi, z_lo), 0, cz_lo)

            pe.wait_ge(xs_ready, 1)
            for k in range(KT):
                for t in range(TT):
                    c = (k % 2) * SEQ + t * P
                    ins = nc.tensor.transpose(ps[:, k // 2, c:c + P], normed_f[:, t, k * P:(k + 1) * P], ident[:])
            ins.then_inc(xr_t, 1)
            pe.wait_ge(xr_out, 1)
            for t in range(TT):
                for k in range(KT):
                    ins = nc.tensor.matmul(ps[:, 4 + t, 0:NE], routed_t[:, k // 2, (k % 2) * SEQ + t * P:(k % 2) * SEQ + (t + 1) * P],
                                           router[:, k, :], start=(k == 0), stop=(k == KT - 1))
            ins.then_inc(logits_t, 1)
            pe.wait_ge(ranked, 1)
            nc.tensor.matmul(ps[:, 6, 0:NE], upper[:], chosen[:, 0, :], start=True, stop=True)
            nc.tensor.matmul(ps[:, 6, NE:2 * NE], ones[:], chosen[:, 0, :], start=True, stop=False)
            nc.tensor.matmul(ps[:, 6, NE:2 * NE], upper[:], chosen[:, 1, :], start=False, stop=True)
            nc.tensor.matmul(ps[:, 7, 0:NE], ones[:], chosen[:, 0, :], start=True, stop=False)
            nc.tensor.matmul(ps[:, 7, 0:NE], ones[:], chosen[:, 1, :], start=False, stop=True).then_inc(counted, 1)

            def expert_pass(p, first):
                n0, s0 = p * NE, p * NE * NB

                def weights(base, rounds=0):
                    pe.wait_ge(lo_ready, base + 1 + RAW * rounds)
                    return base % PARTS

                def gate_or_up(bank, base, rounds=0):
                    for kh in range(2):
                        q = weights(base + kh, rounds)
                        for k in range(4):
                            kk = 4 * kh + k
                            ins = project(ps[:, bank, :], (xe_hi[:, kk, :], xe_lo[:, kk, :]), q, k,
                                          start=(kk == 0), stop=(kk == KT - 1), loose=False)
                        ins.then_inc(units_used, 1)

                def turn(s):
                    pe.wait_ge(m_hid, s0 + 1 + s)
                    hidden_transpose(ps[:, 2, :], hid[:, 0, :]).then_inc(m_t, 1)

                def down(s, base, rounds=0):
                    pe.wait_ge(m_htlo, s0 + 1 + s)
                    for c in range(2):
                        q = weights(base + c, rounds)
                        for k in range(4):
                            ins = project(ps[:, 4 + c, :], (ht_hi[:, 0, k, :], ht_lo[:, 0, k, :]), q, k,
                                          start=False, stop=False, loose=True)
                        ins.then_inc(units_used, 1)

                def gather(n):
                    pe.wait_ge(pick_r, n + 1 + p * (NE + 1))
                    for k in range(KT):
                        dst = ps[:, 6 + k // 4, (k % 4) * P:(k % 4 + 1) * P]
                        for t in range(TT):
                            for part, x in enumerate((xs_hi, xs_lo)):
                                ins = nc.tensor.matmul(dst, x[:, t, k * P:(k + 1) * P], pick[:, t, :],
                                                       start=(t == 0 and part == 0), stop=(t == TT - 1 and part == 1))
                    ins.then_inc(gathered, 1)
                    for t in range(TT):
                        ins = nc.tensor.transpose(ps[:, 3, t * P:(t + 1) * P], pick[:, t, :].bitcast(F32), ident[:])
                    ins.then_inc(pick_t, 1)

                def scatter(t, bank=6):
                    for c in range(2):
                        for part, y in enumerate((ye_hi, ye_lo)):
                            ins = nc.tensor.matmul(ps[:, bank + c, :], place_e[:, t, :], y[:, c * NC:(c + 1) * NC],
                                                   start=(part == 0), stop=(part == 1))
                    ins.then_inc(scattered, 1)

                def open_output():
                    for c in range(2):
                        nc.tensor.matmul(ps[:, 4 + c, :], zeros[:, 0:P], zeros[:, :], start=True, stop=False,
                                         skip_group_check=True)

                def step(e, j, scatter_last=False):
                    s = NB * e + j
                    pe.wait_ge(m_sil, s0 + s)
                    gate_or_up(0, first - 2, s)
                    if scatter_last:
                        pe.wait_ge(place_r, n0 + e)
                        pe.wait_ge(ye_lo_r, n0 + e)
                        scatter(0)
                    turn(s - 1)
                    gate_or_up(1, first, s)
                    if scatter_last:
                        pe.wait_ge(added, TT * (n0 + e) - 1)
                        scatter(1)
                        open_output()
                    down(s - 1, first + 2, s)

                gather(0)
                pe.wait_ge(xe_lo_r, 1 + p * (NE + 1))
                open_output()
                gate_or_up(0, first)
                gate_or_up(1, first + 2)
                with pe.Fori(1, 2) as j:
                    step(0, j)
                pe.wait_ge(place_r, n0 + 1)
                gather(1)
                with pe.Fori(2, NB) as j:
                    step(0, j)
                with pe.Fori(1, NE) as e:
                    pe.wait_ge(xe_lo_r, e + 1 + p * (NE + 1))
                    step(e, 0)
                    step(e, 1, scatter_last=True)
                    pe.wait_ge(place_r, n0 + e + 1)
                    pe.wait_ge(added, TT * (n0 + e))
                    gather(e + 1)
                    with pe.Fori(2, NB) as j:
                        step(e, j)
                last = first + NE * EXPERT_UNITS - 2
                turn(NE * NB - 1)
                down(NE * NB - 1, last)
                pe.wait_ge(xe_lo_r, (p + 1) * (NE + 1))
                pe.wait_ge(ye_lo_r, n0 + NE)
                scatter(0)
                scatter(1, bank=0)
                pe.wait_ge(added, TT * (n0 + NE))

            pe.wait_ge(xs_lo_r, 1)
            pe.wait_ge(consts, 9)
            expert_pass(0, U_MOE)
            pe.wait_ge(most_r, 1)
            crowd = pe.value_load(most[0:1, 0:1], min_val=0, max_val=SEQ)
            with pe.If(crowd > P):
                expert_pass(1, N_UNITS)
            pe.nop()
    return nc


_VECTORS = ["norm_mix", "norm_ffn", "rec_conv_w", "rec_conv_b", "rec_gate_a_b", "rec_gate_x_b", "rec_lambda",
            "cnv_b_pw1", "cnv_dw_w", "cnv_dw_b", "cnv_ln_g", "cnv_ln_b"]
_INS = ["x", "norm_ffn", "norm_out", "rec_w_in", "rec_gate_a_w", "rec_gate_x_w", "rec_w_out", "ffn_w_gate_up",
        "ffn_w_down", "cnv_w_pw1", "cnv_w_pw2", "cnv_b_pw2", "moe_router", "moe_w_gate_up", "moe_w_down"]


def kernel(**inputs):
    import numpy as np
    import concourse.bacc as bacc
    from concourse.bass_utils import run_bass_kernel_spmd

    nc = bacc.Bacc("TRN2", target_bir_lowering=False, num_devices=1)
    arrays, aps = {}, {}
    laid = {name: inputs[name] for name in _INS}
    laid["vectors"] = np.concatenate([np.asarray(inputs[name]).reshape(-1, D) for name in _VECTORS])
    for name, a in laid.items():
        a = np.ascontiguousarray(a)
        arrays[f"in_{name}"] = a
        aps[name] = nc.dram_tensor(f"in_{name}", a.shape, F32, kind="ExternalInput").ap()
    out = nc.dram_tensor("out", (1, SEQ, D), F32, kind="ExternalOutput").ap()
    build(nc, aps, out)
    r = run_bass_kernel_spmd(nc, [arrays], core_ids=[0])
    return r.results[0]["out"]
```

```python
import concourse.bass as bass
from concourse import mybir
from contextlib import ExitStack

F32 = mybir.dt.float32
F32R = mybir.dt.float32r
I32 = mybir.dt.int32
ACT = mybir.ActivationFunctionType
ALU = mybir.AluOpType
AX = mybir.AxisListType

P = 128
D = 1024
SEQ = 256
TT = SEQ // P
KT = D // P
FF = D * 7 // 2
NC = 512
NB = FF // NC
HEADS = 4
NE = 8
REC_TAPS = 4
DW_TAPS = 31
RMS_EPS = 1e-6
LN_EPS = 1e-5
RAW = 6
PARTS = 3
UNIT = 2048
BLOCK_UNITS = 6
EXPERT_UNITS = NB * BLOCK_UNITS

V_MIX, V_FFN, V_CW, V_CB, V_GA, V_GX, V_LAM = 0, 2, 4, 8, 9, 10, 11
V_PW, V_DW, V_DWB, V_LNG, V_LNB = 12, 14, 45, 46, 47
NV = 48

U_IN = 0
U_GATES = 6
U_Y1 = 8
U_OUT = 10
U_FFN = 14
U_PW1 = U_FFN + EXPERT_UNITS
U_PW2 = U_PW1 + 8
U_MOE = U_PW2 + 4
N_UNITS = U_MOE + NE * EXPERT_UNITS

TURN_BANKS = ((0, 1, 2, 3), (0, 2, 1, 3), (4, 6, 5, 7))

LAST_BANKS = (6, 0)

PE_TAPS = (14, 15)
PE_TAP_LIST = [(k, i) for k in range(KT) for i in range(PE_TAPS[k // 4])]


def build(nc, A, out):
    ctx = ExitStack()
    with ctx:
        def sem(name):
            return ctx.enter_context(nc.semaphore(name))

        def sb(name, shape, dt=F32, stack=ctx):
            return stack.enter_context(nc.sbuf_tensor(name, shape, dt))

        raw = sb("raw", [P, RAW, UNIT])
        w_hi = sb("w_hi", [P, PARTS, UNIT], F32R)
        w_lo = sb("w_lo", [P, PARTS, UNIT], F32R)
        res = sb("res", [P, TT, D])
        ident = sb("ident", [P, P])
        colv = sb("colv", [P, KT, NV])
        ss = sb("ss", [P, 2, TT])
        router = sb("router", [P, KT, NE])
        var = sb("var", [P, TT])
        rstd = sb("rstd", [P, TT])
        mhalf = sb("mhalf", [P, TT])
        xt_hi = sb("xt_hi", [P, KT, SEQ], F32R)
        xt_lo = sb("xt_lo", [P, KT, SEQ], F32R)

        with ExitStack() as s:
            vec_rows = sb("vec_rows", [NV, D], F32, s)
            with ExitStack() as s2:
                normed = sb("normed_a", [P, TT, D], F32, s2)
            rtmp = sb("rtmp", [P, KT, SEQ], F32, s)
            xpad = sb("xpad", [P, KT, REC_TAPS - 1 + SEQ], F32, s)
            xc = sb("xc", [P, KT, SEQ], F32, s)
            xc_hi = sb("xc_hi", [P, KT, SEQ], F32R, s)
            xc_lo = sb("xc_lo", [P, KT, SEQ], F32R, s)
            yb = sb("yb", [P, KT, SEQ], F32, s)
            rg = sb("rg", [P, KT, SEQ], F32, s)
            ig = sb("ig", [P, KT, SEQ], F32, s)
            root = sb("root", [P, KT, SEQ], F32, s)
            sp = sb("sp", [P, 8, KT], F32, s)
        with ExitStack() as s:
            normed_f = sb("normed_f", [P, TT, D], F32, s)
            sil = sb("sil", [P, TT, NC], F32, s)
            grow = sb("grow", [P, D], F32, s)
            hid = sb("hid", [P, TT, NC], F32, s)
            ht_hi = sb("ht_hi", [P, TT, 4, P], F32R, s)
            ht_lo = sb("ht_lo", [P, TT, 4, P], F32R, s)
            logit_rows = sb("logit_rows", [NE, SEQ], F32, s)
            xs_hi = sb("xs_hi", [P, TT, D], F32R, s)
            xs_lo = sb("xs_lo", [P, TT, D], F32R, s)
            xe_hi = sb("xe_hi", [P, KT, P], F32R, s)
            xe_lo = sb("xe_lo", [P, KT, P], F32R, s)
            pick = sb("pick", [P, TT, P], F32R, s)
            place_e = sb("place_e", [P, TT, P], F32R, s)
            with ExitStack() as s2:
                routed_t = sb("routed_t", [P, 4, NC], F32, s2)
            ye_hi = sb("ye_hi", [P, D], F32R, s)
            ye_lo = sb("ye_lo", [P, D], F32R, s)
            zeros = sb("zeros", [P, NC], F32R, s)
            iota = sb("iota", [P, 2 * P], F32, s)
            earlier = sb("earlier", [P, NE, NE], F32, s)
            upper = sb("upper", [P, P], F32, s)
            ones = sb("ones", [P, P], F32, s)
            logit = sb("logit", [P, TT, NE], F32, s)
            cmp_gt = sb("cmp_gt", [P, TT, NE, NE], F32, s)
            cmp_eq = sb("cmp_eq", [P, TT, NE, NE], F32, s)
            rank = sb("rank", [P, TT, NE], F32, s)
            chosen = sb("chosen", [P, TT, NE], F32, s)
            gate = sb("gate", [P, TT, NE], F32, s)
            slot = sb("slot", [P, TT, NE + 1], F32, s)
            small = sb("small", [P, 8], F32, s)
            most = sb("most", [P, 1], I32, s)
        with ExitStack() as s:
            normed_c = sb("normed_c", [P, TT, D], F32, s)
            bias_row = sb("bias_row", [P, D], F32, s)
            sig = sb("sig", [P, 4, SEQ], F32, s)
            upad = sb("upad", [P, KT, DW_TAPS - 1 + SEQ], F32, s)
            dw = sb("dw", [P, KT, SEQ], F32, s)
            sq = sb("sq", [P, KT, SEQ], F32, s)
            act_c = sb("act_c", [P, KT, SEQ], F32, s)
            z_hi = sb("z_hi", [P, KT, SEQ], F32R, s)
            z_lo = sb("z_lo", [P, KT, SEQ], F32R, s)
            diag = sb("diag", [P, 4, P], F32, s)
            mean_w = sb("mean_w", [P, P], F32, s)
            ln_var = sb("ln_var", [P, TT], F32, s)
            ln_rstd = sb("ln_rstd", [P, TT], F32, s)
            spread = sb("spread", [P, TT, P], F32, s)
            sq_sum = sb("sq_sum", [P, 2, SEQ], F32, s)

        ps = ctx.enter_context(nc.psum_tensor("ps", [P, 8, NC], F32))

        unit_landed = [sem(f"unit_landed{i}") for i in range(RAW)]
        hi_ready, lo_ready, units_used = sem("hi_ready"), sem("lo_ready"), sem("units_used")
        x_landed, vecs_landed, bias_landed, out_landed = sem("x_landed"), sem("vecs_landed"), sem("bias_landed"), sem("out_landed")
        grow_landed, gout_landed = sem("grow_landed"), sem("gout_landed")
        consts = sem("consts")
        vec_t, colv_ready = sem("vec_t"), sem("colv_ready")
        squares, var_ready, rstd_ready = sem("squares"), sem("var_ready"), sem("rstd_ready")
        normed_ready, norm_t = sem("normed_ready"), sem("norm_t")
        xt_hi_ready, xt_lo_ready = sem("xt_hi_ready"), sem("xt_lo_ready")
        dve_step = sem("dve_step")
        act_step = sem("act_step")
        pool_step = sem("pool_step")
        x_out = sem("x_out")
        conv_done, xc_hi_r, xc_lo_r = sem("conv_done"), sem("xc_hi_r"), sem("xc_lo_r")
        y_out, r_out, i_out, gated = sem("y_out"), sem("r_out"), sem("i_out"), sem("gated")
        lam_exp, lam_ready, tau_ready, root_ready = sem("lam_exp"), sem("lam_ready"), sem("tau_ready"), sem("root_ready")
        decay_ready = sem("decay_ready")
        lam_neg = sem("lam_neg")
        z_ready, z_hi_r, z_lo_r = sem("z_ready"), sem("z_hi_r"), sem("z_lo_r")
        res_ready = sem("res_ready")
        f_sil, f_hid, f_t, f_hthi, f_htlo = (sem(n) for n in ("f_sil", "f_hid", "f_t", "f_hthi", "f_htlo"))
        c_sig, c_u = sem("c_sig"), sem("c_u")
        diag_ready, diag_used, dw_done = sem("diag_ready"), sem("diag_used"), sem("dw_done")
        mean_t, centred, sq_ready, var_t, lnv_ready, lnr_ready, ln_done, silu_c = (sem(n) for n in (
            "mean_t", "centred", "sq_ready", "var_t", "lnv_ready", "lnr_ready", "ln_done", "silu_c"))
        spread_r, lnb_t, sq_sum_ready = sem("spread_r"), sem("lnb_t"), sem("sq_sum_ready")
        cz_hi, cz_lo = sem("cz_hi"), sem("cz_lo")
        xs_ready, xs_hi_r, xs_lo_r, xr_t, xr_out = sem("xs_ready"), sem("xs_hi_r"), sem("xs_lo_r"), sem("xr_t"), sem("xr_out")
        router_landed, router_ready, logit_rows_r = sem("router_landed"), sem("router_ready"), sem("logit_rows_r")
        logits_t, ranked, counted, exp_l, pick_r, pick_t, place_r = (sem(n) for n in (
            "logits_t", "ranked", "counted", "exp_l", "pick_r", "pick_t", "place_r"))
        lmax_r, most_r = sem("lmax_r"), sem("most_r")
        gathered, xe_hi_r, xe_lo_r = sem("gathered"), sem("xe_hi_r"), sem("xe_lo_r")
        m_sil, m_hid, m_t, m_hthi, m_htlo = (sem(n) for n in (
            "m_sil", "m_hid", "m_t", "m_hthi", "m_htlo"))
        ye_hi_r, ye_lo_r, scattered, added = (sem(n) for n in (
            "ye_hi_r", "ye_lo_r", "scattered", "added"))
        moe_over, out_ready = sem("moe_over"), sem("out_ready")

        block = ctx.enter_context(nc.Block())

        def tile4(ap):
            return ap.rearrange("(k p) n -> p k n", p=P)

        def slot4(t, s):
            return t[:, s, :].rearrange("p (k n) -> p k n", k=4)

        def half(mat, kh, col):
            return tile4(mat[kh * NC:(kh + 1) * NC, col:col + NC])

        rec_units = ([half(A["rec_w_in"][0], kh, D + g * NC) for g in range(2) for kh in range(2)]
                     + [half(A["rec_w_in"][0], kh, 0) for kh in range(2)]
                     + [A[n][0].rearrange("h (k p) j -> p (h k) j", p=P) for n in ("rec_gate_a_w", "rec_gate_x_w")]
                     + [half(A["rec_w_in"][0], kh, NC) for kh in range(2)]
                     + [half(A["rec_w_out"][0], kh, g * NC) for kh in range(2) for g in range(2)])
        conv_units = ([half(A["cnv_w_pw1"][0], kh, side * D + g * NC)
                       for g in range(2) for side in (1, 0) for kh in range(2)]
                      + [half(A["cnv_w_pw2"][0], kh, g * NC) for kh in range(2) for g in range(2)])
        ffn_gu = A["ffn_w_gate_up"][0]
        ffn_dn = A["ffn_w_down"][0]
        moe_gu = A["moe_w_gate_up"][0]
        moe_dn = A["moe_w_down"][0].rearrange("e f n -> (e f) n")

        @block.sync
        def _(sp_):
            sp_.dma_start(res[:, 0, :], A["x"][0][0:P, :]).then_inc(x_landed, 16)
            sp_.dma_start(res[:, 1, :], A["x"][0][P:SEQ, :]).then_inc(x_landed, 16)

            def load(base, src, rounds=0):
                slot_n = base % RAW
                if base >= RAW:
                    sp_.wait_ge(lo_ready, base - (RAW - 1) + RAW * rounds)
                dst = raw[:, slot_n, :].rearrange("p (k n) -> p k n", k=src.shape[1])
                sp_.dma_start(dst, src).then_inc(unit_landed[slot_n], 16)

            for n, src in enumerate(rec_units):
                load(n, src)

            def ffn_gate_up(side, kh, j):
                return tile4(ffn_gu[kh * NC:(kh + 1) * NC, bass.ds(side * FF + NC * j, NC)])

            def ffn_down(j, c):
                return tile4(ffn_dn[bass.ds(NC * j, NC), c * NC:(c + 1) * NC])

            for k in range(4):
                load(U_FFN + k, ffn_gate_up(k // 2, k % 2, 0))
            with sp_.Fori(1, NB) as j:
                for k in range(BLOCK_UNITS):
                    load(U_FFN - 2 + k, ffn_down(j - 1, k - 2) if k in (2, 3) else ffn_gate_up(k // 4, k % 2, j), j)
            for c in range(2):
                load(U_PW1 - 2 + c, ffn_down(NB - 1, c))
            for n, src in enumerate(conv_units):
                load(U_PW1 + n, src)

            def gate_up(e, j, k):
                col = (k // 2) * FF
                return moe_gu[bass.ds(e, 1), (k % 2) * NC:(k % 2 + 1) * NC, bass.ds(col + NC * j, NC)].rearrange(
                    "e (k p) n -> p (e k) n", p=P)

            def down(s, c):
                return tile4(moe_dn[bass.ds(s * NC, NC), c * NC:(c + 1) * NC])

            def expert_step(e, j, first):
                s = NB * e + j
                for k in range(BLOCK_UNITS):
                    load(first - 2 + k, gate_up(e, j, k) if k < 4 else down(s - 1, k - 4), s)

            def expert_weights(first):
                for k in range(4):
                    load(first + k, gate_up(0, 0, k))
                with sp_.Fori(1, NB) as j:
                    expert_step(0, j, first)
                with sp_.Fori(1, NE) as e:
                    with sp_.Fori(0, NB) as j:
                        expert_step(e, j, first)
                for c in range(2):
                    load(first + NE * EXPERT_UNITS - 2 + c, down(NE * NB - 1, c))

            expert_weights(U_MOE)
            sp_.wait_ge(most_r, 1)
            crowd = sp_.value_load(most[0:1, 0:1], min_val=0, max_val=SEQ)
            with sp_.If(crowd > P):
                expert_weights(N_UNITS)
            sp_.nop()
            for t in range(TT):
                sp_.wait_ge(out_ready, t + 1)
                sp_.dma_start(out[0, t * P:(t + 1) * P, :], normed_f[:, t, :]).then_inc(out_landed, 16)
            sp_.wait_ge(out_landed, 16 * TT)

        @block.gpsimd
        def _(pool):
            nc.gpsimd.memset(ident[:], 0.0).then_inc(pool_step, 1)
            pool.wait_ge(pool_step, 1)
            nc.gpsimd.affine_select(out=ident[:], in_=ident[:], compare_op=ALU.not_equal, fill=1.0, base=0,
                                    pattern=[[-1, P]], channel_multiplier=1).then_inc(consts, 1)
            nc.gpsimd.memset(mhalf[:], -0.5).then_inc(consts, 1)
            nc.gpsimd.memset(xpad[:, :, 0:REC_TAPS - 1], 0.0).then_inc(consts, 1)

            def root_of_var(n):
                pool.wait_ge(var_ready, n + 1)
                nc.gpsimd.tensor_tensor(rstd[:], var[:], mhalf[:], ALU.pow).then_inc(rstd_ready, 1)

            pool.wait_ge(consts, 3)
            root_of_var(0)
            for g in range(2):
                pool.wait_ge(i_out, 4 * (g + 1))
                pool.wait_ge(xc_lo_r, g + 1)
                s = slice(4 * g, 4 * g + 4)
                nc.gpsimd.tensor_tensor(ig[:, s, :], ig[:, s, :], xc[:, s, :], ALU.mult).then_inc(gated, 1)
            root_of_var(1)
            root_of_var(2)
            nc.gpsimd.memset(upad[:, :, 0:DW_TAPS - 1], 0.0).then_inc(consts, 1)
            nc.gpsimd.memset(mean_w[:], 1.0 / D).then_inc(consts, 1)
            pool.wait_ge(lnv_ready, 1)
            nc.gpsimd.tensor_tensor(ln_rstd[:], ln_var[:], mhalf[:], ALU.pow).then_inc(lnr_ready, 1)
            root_of_var(3)
            nc.gpsimd.memset(zeros[:].bitcast(F32), 0.0).then_inc(consts, 1)
            nc.gpsimd.memset(ones[:], 1.0).then_inc(pool_step, 1)
            nc.gpsimd.memset(earlier[:], 1.0).then_inc(pool_step, 1)
            nc.gpsimd.iota(iota[:], [[1, 2 * P]], base=0, channel_multiplier=0,
                           allow_small_or_imprecise_dtypes=True).then_inc(consts, 1)
            pool.wait_ge(pool_step, 3)
            nc.gpsimd.affine_select(out=earlier[:], in_=earlier[:], compare_op=ALU.is_ge, fill=0.0, base=-1,
                                    pattern=[[1, NE], [-1, NE]], channel_multiplier=0).then_inc(consts, 1)
            nc.gpsimd.affine_select(out=upper[:], in_=ones[:], compare_op=ALU.is_ge, fill=0.0, base=-1,
                                    pattern=[[1, P]], channel_multiplier=-1).then_inc(consts, 1)
            root_of_var(4)

        @block.scalar
        def _(act):
            act.dma_start(vec_rows[:, :], A["vectors"]).then_inc(vecs_landed, 16)
            act.dma_start(router[:, :, :], A["moe_router"][0].rearrange("(k p) e -> p k e", p=P)).then_inc(router_landed, 16)

            steps = [0]

            def link(ins):
                steps[0] += 1
                ins.then_inc(act_step, 1)
                act.wait_ge(act_step, steps[0])

            def split_hi(base, rounds=0):
                slot_n, part = base % RAW, base % PARTS
                act.wait_ge(unit_landed[slot_n], 16 * (base // RAW + 1) + 16 * rounds)
                if base >= PARTS:
                    act.wait_ge(units_used, base - (PARTS - 1) + RAW * rounds)
                nc.scalar.activation(w_hi[:, part, :], raw[:, slot_n, :], ACT.Copy).then_inc(hi_ready, 1)

            def half_squares(c, keep):
                for t in range(TT):
                    s = slice(c * NC, (c + 1) * NC)
                    nc.scalar.activation(keep[:, t, s], res[:, t, s], ACT.Square, scale=D ** -0.5,
                                         accum_out=ss[:, c, t:t + 1]).then_inc(squares, 1)

            def norm_square(n, keep):
                for c in range(2):
                    if n:
                        act.wait_ge(res_ready, 2 * (n - 1) + c + 1)
                    elif c == 0:
                        act.wait_ge(x_landed, 32)
                    half_squares(c, keep)

            def norm_hi(n, vrow):
                act.wait_ge(colv_ready, 1)
                for k in range(KT):
                    act.wait_ge(norm_t, 4 * n + k // 2 + 1)
                    nc.scalar.activation(xt_hi[:, k, :], ps[:, TURN_BANKS[n][k // 2], (k % 2) * SEQ:(k % 2 + 1) * SEQ], ACT.Copy,
                                         scale=colv[:, k, vrow:vrow + 1]).then_inc(xt_hi_ready, 1)

            norm_square(0, normed)
            split_hi(0)
            norm_hi(0, V_MIX)
            split_hi(1), split_hi(2)
            act.wait_ge(lam_neg, 1)
            nc.scalar.activation(sp[:, 1, :], sp[:, 0, :], ACT.Exp).then_inc(lam_exp, 1)
            split_hi(3)

            def x_evac(g):
                act.wait_ge(units_used, 2 * g + 2)
                b = 4 - 4 * g
                nc.scalar.activation(xpad[:, 4 * g:4 * g + 4, REC_TAPS - 1:], ps[:, b:b + 4, 0:SEQ], ACT.Copy).then_inc(x_out, 1)

            def xc_round(g):
                act.wait_ge(conv_done, g + 1)
                nc.scalar.activation(xc_hi[:, 4 * g:4 * g + 4, :], xc[:, 4 * g:4 * g + 4, :], ACT.Copy).then_inc(xc_hi_r, 1)

            def y_evac(g, used):
                act.wait_ge(units_used, used)
                b = 4 - 4 * g
                nc.scalar.activation(yb[:, 4 * g:4 * g + 4, :], ps[:, b:b + 4, 0:SEQ], ACT.Gelu_apprx_tanh).then_inc(y_out, 1)

            def gate_evac(g, dst, bank, vrow, ready):
                for k in range(4 * g, 4 * g + 4):
                    nc.scalar.activation(dst[:, k, :], ps[:, bank + k // 2, (k % 2) * SEQ:(k % 2 + 1) * SEQ], ACT.Sigmoid,
                                         bias=colv[:, k, vrow:vrow + 1]).then_inc(ready, 1)

            x_evac(0)
            split_hi(4), split_hi(5)
            x_evac(1)
            xc_round(0)
            split_hi(6)
            xc_round(1)
            split_hi(7)
            y_evac(0, 6)
            split_hi(8)
            act.wait_ge(units_used, U_GATES + 1)
            gate_evac(0, rg, 0, V_GA, r_out)
            gate_evac(1, rg, 0, V_GA, r_out)
            split_hi(9)
            act.wait_ge(units_used, U_GATES + 2)
            gate_evac(0, ig, 4, V_GX, i_out)
            gate_evac(1, ig, 4, V_GX, i_out)
            split_hi(10)
            act.wait_ge(lam_ready, 1)
            act.wait_ge(r_out, KT)
            for g in range(2):
                s = slice(4 * g, 4 * g + 4)
                for k in range(4 * g, 4 * g + 4):
                    nc.scalar.activation(rtmp[:, k, :], rg[:, k, :], ACT.Exp, scale=sp[:, 0, k:k + 1]).then_inc(decay_ready, 1)
                if g == 1:
                    split_hi(11)
                    act.wait_ge(z_ready, 1)
                    nc.scalar.activation(xc_hi[:, 0:4, :], yb[:, 0:4, :], ACT.Copy).then_inc(z_hi_r, 1)
                    split_hi(12)
                for k in range(4 * g, 4 * g + 4):
                    nc.scalar.activation(rg[:, k, :], rg[:, k, :], ACT.Tanh, scale=sp[:, 7, k:k + 1]).then_inc(tau_ready, 1)
                act.wait_ge(tau_ready, 4 * g + 4)
                nc.scalar.activation(root[:, s, :], rg[:, s, :], ACT.Sqrt).then_inc(root_ready, 1)
            y_evac(1, U_Y1 + 2)
            act.wait_ge(z_ready, 2)
            nc.scalar.activation(xc_hi[:, 4:8, :], yb[:, 4:8, :], ACT.Copy).then_inc(z_hi_r, 1)
            split_hi(13)
            split_hi(14), split_hi(15)

            norm_hi(1, V_FFN)
            norm_square(1, normed_f)
            split_hi(16)

            def silu_gates(j, gate_done):
                act.wait_ge(units_used, gate_done)
                for t in range(TT):
                    nc.scalar.activation(sil[:, t, :], ps[:, 2 * t, :], ACT.Silu, scale=rstd[:, t:t + 1]).then_inc(f_sil, 1)

            def round_hidden(j):
                for t in range(TT):
                    act.wait_ge(f_t, TT * j + t + 1)
                    nc.scalar.activation(ht_hi[:, t, :, :], ps[:, 2 * t + 1, :].rearrange("p (q n) -> p q n", q=4),
                                         ACT.Copy).then_inc(f_hthi, 1)

            split_hi(U_FFN + 3)
            act.wait_ge(rstd_ready, 2)
            silu_gates(0, U_FFN + 2)
            with act.Fori(1, NB) as j:
                first = U_FFN - 2
                for k in range(3):
                    split_hi(first + k, j)
                round_hidden(j - 1)
                split_hi(first + 3, j), split_hi(first + 4, j)
                silu_gates(j, first + 2 + RAW * j)
                split_hi(first + 5, j)
            split_hi(U_PW1 - 2), split_hi(U_PW1 - 1)
            round_hidden(NB - 1)

            split_hi(U_PW1), split_hi(U_PW1 + 1)
            norm_square(2, normed_c)
            act.dma_start(bias_row[:, :], A["cnv_b_pw2"][0:1, :].broadcast_to([P, D])).then_inc(bias_landed, 16)
            norm_hi(2, V_MIX + 1)
            split_hi(U_PW1 + 2), split_hi(U_PW1 + 3)
            for g in range(2):
                act.wait_ge(units_used, U_PW1 + 4 * g + 2)
                for i in range(4):
                    if g:
                        act.wait_ge(c_u, i + 1)
                    nc.scalar.activation(sig[:, i, :], ps[:, i, 0:SEQ], ACT.Sigmoid,
                                         bias=colv[:, 4 * g + i, V_PW + 1:V_PW + 2]).then_inc(c_sig, 1)
                for u in range(U_PW1 + 4 + 4 * g, U_PW1 + 8 + 2 * g):
                    split_hi(u)
            for n, (k, i) in enumerate(PE_TAP_LIST):
                if n == 4:
                    split_hi(U_PW2 + 2)
                if n >= 4:
                    act.wait_ge(diag_used, n - 3)
                nc.scalar.activation(diag[:, n % 4, :], ident[:], ACT.Copy,
                                     scale=colv[:, k, V_DW + i:V_DW + i + 1]).then_inc(diag_ready, 1)
            act.wait_ge(c_u, KT)
            act.dma_start(grow[:, :], A["norm_ffn"][1:2, :].broadcast_to([P, D])).then_inc(grow_landed, 16)
            for g in range(2):
                s = slice(4 * g, 4 * g + 4)
                act.wait_ge(centred, g + 1)
                nc.scalar.activation(sq[:, s, :], dw[:, s, :], ACT.Square).then_inc(sq_ready, 1)
            for k in range(KT):
                act.wait_ge(ln_done, k // 2 + 1)
                nc.scalar.activation(act_c[:, k, :], sq[:, k, :], ACT.Silu, scale=colv[:, k, V_LNG:V_LNG + 1],
                                     bias=colv[:, k, V_LNB:V_LNB + 1]).then_inc(silu_c, 1)
                if k % 4 == 3:
                    g = k // 4
                    s = slice(4 * g, 4 * g + 4)
                    act.wait_ge(silu_c, k + 1)
                    nc.scalar.activation(z_hi[:, s, :], act_c[:, s, :], ACT.Copy).then_inc(cz_hi, 1)
            split_hi(U_PW2 + 3)

            split_hi(U_MOE), split_hi(U_MOE + 1)
            act.wait_ge(res_ready, 5)
            half_squares(0, normed_f)
            for b in range(4):
                if b == 2:
                    act.wait_ge(res_ready, 6)
                    half_squares(1, normed_f)
                act.wait_ge(xr_t, b + 1)
                nc.scalar.activation(routed_t[:, b, :], ps[:, 4 + b, :], ACT.Copy).then_inc(xr_out, 1)
            act.wait_ge(xs_ready, 1)
            nc.scalar.activation(xs_hi[:, 0, :], normed_f[:, 0, :], ACT.Copy).then_inc(xs_hi_r, 1)
            act.wait_ge(logits_t, 1)
            nc.scalar.activation(logit_rows[:, :], ps[0:NE, 0, 0:SEQ], ACT.Copy).then_inc(logit_rows_r, 1)
            act.wait_ge(xs_ready, 2)
            nc.scalar.activation(xs_hi[:, 1, :], normed_f[:, 1, :], ACT.Copy).then_inc(xs_hi_r, 1)
            act.wait_ge(lmax_r, 1)
            nc.scalar.activation(gate[:, :, :], gate[:, :, :], ACT.Exp).then_inc(exp_l, 1)

            def expert_pass(p, first):
                n0, s0 = p * NE, p * NE * NB
                y0, a0 = p * (NE + 1), p * TT * (NE + 1)

                def tokens_in(n):
                    if not isinstance(n, int) or n > 0:
                        act.wait_ge(units_used, RAW * (NB * n - 1) + first + 2)
                    for h in range(2):
                        act.wait_ge(gathered, 2 * n + h + 1 + 2 * p * (NE + 1))
                        nc.scalar.activation(xe_hi[:, 4 * h:4 * h + 4, :].rearrange("p k n -> p (k n)"),
                                             ps[:, 6 + h, :], ACT.Copy).then_inc(xe_hi_r, 1)

                def silu(s, gate_done):
                    act.wait_ge(units_used, gate_done)
                    if not isinstance(s, int) or s > 0:
                        act.wait_ge(m_hid, s0 + s)
                    nc.scalar.activation(sil[:, 0, :], ps[:, 0, :], ACT.Silu).then_inc(m_sil, 1)

                def round_hidden(s):
                    act.wait_ge(m_t, s0 + 1 + s)
                    nc.scalar.activation(ht_hi[:, 0, :, :].rearrange("p q n -> p (q n)"), ps[:, 2, :],
                                         ACT.Copy).then_inc(m_hthi, 1)

                def round_output(e, used):
                    act.wait_ge(units_used, used)
                    nc.scalar.activation(ye_hi[:, :], ps[:, 4:6, :].rearrange("p b n -> p (b n)"), ACT.Copy).then_inc(ye_hi_r, 1)

                def keep_place(e, scattered_before):
                    if scattered_before is not None:
                        act.wait_ge(scattered, scattered_before)
                    act.wait_ge(pick_t, e + 1 + p * (NE + 1))
                    nc.scalar.activation(place_e[:, :, :].rearrange("p t n -> p (t n)"), ps[:, 3, 0:TT * P],
                                         ACT.Copy).then_inc(place_r, 1)

                def step(e, j, output_of_last=False, skip=0):
                    s = NB * e + j
                    for k in range(skip, 2):
                        split_hi(first - 2 + k, s)
                    if output_of_last:
                        round_output(e - 1, first - 2 + RAW * s)
                    for k in (2, 3):
                        split_hi(first - 2 + k, s)
                    silu(s, first + RAW * s)
                    round_hidden(s - 1)
                    for k in (4, 5):
                        split_hi(first - 2 + k, s)

                for k in range(0 if p else 2, PARTS):
                    split_hi(first + k)
                tokens_in(0)
                split_hi(first + 3), split_hi(first + 4)
                silu(0, first + 2)
                split_hi(first + 5)
                step(0, 1, skip=2)
                keep_place(0, None)
                with act.Fori(2, NB) as j:
                    step(0, j)
                tokens_in(1)
                with act.Fori(1, NE) as e:
                    step(e, 0)
                    step(e, 1, output_of_last=True)
                    keep_place(e, a0 + TT * e)
                    with act.Fori(2, NB) as j:
                        step(e, j)
                    tokens_in(e + 1)
                last = first + NE * EXPERT_UNITS - 2
                split_hi(last)
                round_hidden(NE * NB - 1)
                split_hi(last + 1)
                for c in range(2):
                    act.wait_ge(units_used, last + 1 + c)
                    nc.scalar.activation(ye_hi[:, c * NC:(c + 1) * NC], ps[:, 4 + c, :], ACT.Copy).then_inc(ye_hi_r, 1)

            expert_pass(0, U_MOE)
            act.wait_ge(most_r, 1)
            crowd = act.value_load(most[0:1, 0:1], min_val=0, max_val=SEQ)
            with act.If(crowd > P):
                expert_pass(1, N_UNITS)

            act.wait_ge(moe_over, 1)
            act.dma_start(grow[:, :], A["norm_out"].rearrange("(o n) -> o n", o=1).broadcast_to([P, D])).then_inc(gout_landed, 16)
            half_squares(0, normed_f)
            half_squares(1, normed_f)

        @block.vector
        def _(dve):
            steps = [0]

            def link(ins):
                steps[0] += 1
                ins.then_inc(dve_step, 1)
                dve.wait_ge(dve_step, steps[0])

            def split_lo(base, rounds=0):
                slot_n, part = base % RAW, base % PARTS
                dve.wait_ge(hi_ready, base + 1 + RAW * rounds)
                nc.vector.tensor_tensor(w_lo[:, part, :], raw[:, slot_n, :], w_hi[:, part, :].bitcast(F32),
                                        ALU.subtract).then_inc(lo_ready, 1)

            def mean_square(n):
                dve.wait_ge(squares, 2 * TT * (n + 1))
                nc.vector.scalar_tensor_tensor(out=var[:], in0=ss[:, 0, :], scalar=RMS_EPS, in1=ss[:, 1, :],
                                               op0=ALU.add, op1=ALU.add).then_inc(var_ready, 1)

            def norm_scale(n, keep):
                mean_square(n)
                dve.wait_ge(rstd_ready, n + 1)
                for c in range(2):
                    s = slice(c * NC, (c + 1) * NC)
                    for t in range(TT):
                        ins = nc.vector.tensor_scalar(keep[:, t, s], res[:, t, s], rstd[:, t:t + 1], None, ALU.mult)
                    ins.then_inc(normed_ready, 1)

            def norm_lo(n, vrow):
                for k in range(KT):
                    dve.wait_ge(xt_hi_ready, KT * n + (k | 1) + 1)
                    nc.vector.scalar_tensor_tensor(
                        out=xt_lo[:, k, :], in0=ps[:, TURN_BANKS[n][k // 2], (k % 2) * SEQ:(k % 2 + 1) * SEQ],
                        scalar=colv[:, k, vrow:vrow + 1], in1=xt_hi[:, k, :].bitcast(F32),
                        op0=ALU.mult, op1=ALU.subtract).then_inc(xt_lo_ready, 1)

            dve.wait_ge(vec_t, 1)
            nc.vector.tensor_copy(colv[:, :, :].rearrange("p k v -> p (k v)"), ps[:, 7, 0:KT * NV]).then_inc(colv_ready, 1)
            norm_scale(0, normed)
            split_lo(0)
            dve.wait_ge(colv_ready, 1)
            norm_lo(0, V_MIX)
            split_lo(1)
            link(nc.vector.tensor_scalar(sp[:, 0, :], colv[:, :, V_LAM], -1.0, None, ALU.mult))
            nc.vector.tensor_tensor(sp[:, 0, :], sp[:, 0, :], colv[:, :, V_LAM], ALU.min).then_inc(lam_neg, 1)
            split_lo(2), split_lo(3)

            def conv4(g):
                dve.wait_ge(x_out, g + 1)
                for i in range(REC_TAPS):
                    tap = REC_TAPS - 1 - i
                    for k in range(4 * g, 4 * g + 4):
                        src = xpad[:, k, tap:tap + SEQ]
                        w = colv[:, k, V_CW + tap:V_CW + tap + 1]
                        if i == 0:
                            ins = nc.vector.tensor_scalar(xc[:, k, :], src, w, colv[:, k, V_CB:V_CB + 1], ALU.mult, ALU.add)
                        else:
                            ins = nc.vector.scalar_tensor_tensor(out=xc[:, k, :], in0=src, scalar=w, in1=xc[:, k, :],
                                                                 op0=ALU.mult, op1=ALU.add)
                        if i == REC_TAPS - 1:
                            if k == 4 * g + 3:
                                ins.then_inc(conv_done, 1)
                        elif k == 4 * g + 3:
                            link(ins)

            def xc_rest(g):
                dve.wait_ge(xc_hi_r, g + 1)
                s = slice(4 * g, 4 * g + 4)
                nc.vector.tensor_tensor(xc_lo[:, s, :], xc[:, s, :], xc_hi[:, s, :].bitcast(F32), ALU.subtract).then_inc(xc_lo_r, 1)

            dve.wait_ge(consts, 3)
            conv4(0)
            split_lo(4), split_lo(5)
            conv4(1)
            xc_rest(0)
            split_lo(6)
            xc_rest(1)
            split_lo(7), split_lo(8)
            dve.wait_ge(lam_exp, 1)
            ex, y, y2, acc = sp[:, 1, :], sp[:, 2, :], sp[:, 3, :], sp[:, 4, :]
            link(nc.vector.tensor_scalar(y2, ex, 2.0, None, ALU.add))
            link(nc.vector.reciprocal(acc, y2))
            link(nc.vector.tensor_tensor(y, ex, acc, ALU.mult))
            link(nc.vector.tensor_tensor(y2, y, y, ALU.mult))
            link(nc.vector.memset(acc, 1.0 / 19))
            for n in range(17, 0, -2):
                link(nc.vector.tensor_tensor(acc, acc, y2, ALU.mult))
                link(nc.vector.tensor_scalar(acc, acc, 1.0 / n, None, ALU.add))
            link(nc.vector.tensor_tensor(acc, acc, y, ALU.mult))
            link(nc.vector.tensor_scalar(sp[:, 5, :], colv[:, :, V_LAM], -1.0, 0.0, ALU.mult, ALU.max))
            link(nc.vector.scalar_tensor_tensor(out=sp[:, 6, :], in0=acc, scalar=2.0, in1=sp[:, 5, :],
                                                op0=ALU.mult, op1=ALU.add))
            nc.vector.tensor_scalar(sp[:, 7, :], sp[:, 6, :], 4.0, None, ALU.mult)
            nc.vector.tensor_scalar(sp[:, 0, :], sp[:, 6, :], -8.0, None, ALU.mult).then_inc(lam_ready, 1)
            split_lo(9), split_lo(10)
            for g in range(2):
                s = slice(4 * g, 4 * g + 4)
                dve.wait_ge(decay_ready, 4 * g + 4)
                dve.wait_ge(gated, g + 1)
                link(nc.vector.scalar_tensor_tensor(out=ig[:, s, :], in0=rtmp[:, s, :], scalar=1.0, in1=ig[:, s, :],
                                                    op0=ALU.add, op1=ALU.mult))
                dve.wait_ge(root_ready, g + 1)
                link(nc.vector.tensor_tensor(root[:, s, :], root[:, s, :], ig[:, s, :], ALU.mult))
                for k in range(4 * g, 4 * g + 4):
                    ins = nc.vector.tensor_tensor_scan(rg[:, k, :], rtmp[:, k, :], root[:, k, :], 0.0, ALU.mult, ALU.add)
                link(ins)
                dve.wait_ge(y_out, g + 1)
                nc.vector.tensor_tensor(yb[:, s, :], yb[:, s, :], rg[:, s, :], ALU.mult).then_inc(z_ready, 1)
                dve.wait_ge(z_hi_r, g + 1)
                nc.vector.tensor_tensor(xc_lo[:, s, :], yb[:, s, :], xc_hi[:, s, :].bitcast(F32), ALU.subtract).then_inc(z_lo_r, 1)
                if g == 0:
                    split_lo(11), split_lo(12)
            split_lo(13), split_lo(14), split_lo(15)

            def add_residual(used, bank, between=None):
                for c in range(2):
                    if c and between is not None:
                        split_lo(between)
                    dve.wait_ge(units_used, used - 1 + c)
                    for t in range(TT):
                        s = slice(c * NC, (c + 1) * NC)
                        ins = nc.vector.tensor_tensor(res[:, t, s], res[:, t, s], ps[:, bank + 2 * t + c, :], ALU.add)
                    ins.then_inc(res_ready, 1)

            add_residual(U_FFN, 4)

            norm_lo(1, V_FFN)
            mean_square(1)
            split_lo(16)
            dve.wait_ge(router_landed, 16)
            for e in range(NE):
                ins = nc.vector.tensor_tensor(router[:, :, e], router[:, :, e], colv[:, :, V_FFN + 1], ALU.mult)
            ins.then_inc(router_ready, 1)

            def hidden_block(j, up_done):
                dve.wait_ge(units_used, up_done)
                for t in range(TT):
                    dve.wait_ge(f_sil, TT * j + t + 1)
                    nc.vector.scalar_tensor_tensor(out=hid[:, t, :], in0=ps[:, 2 * t + 1, :], scalar=rstd[:, t:t + 1],
                                                   in1=sil[:, t, :], op0=ALU.mult, op1=ALU.mult).then_inc(f_hid, 1)

            def rest_hidden(j):
                for t in range(TT):
                    dve.wait_ge(f_hthi, TT * j + t + 1)
                    nc.vector.tensor_tensor(ht_lo[:, t, :, :].rearrange("p q n -> p (q n)"), ps[:, 2 * t + 1, :],
                                            ht_hi[:, t, :, :].bitcast(F32).rearrange("p q n -> p (q n)"),
                                            ALU.subtract).then_inc(f_htlo, 1)

            split_lo(U_FFN + 3)
            dve.wait_ge(rstd_ready, 2)
            with dve.Fori(1, NB) as j:
                first = U_FFN - 2
                split_lo(first, j), split_lo(first + 1, j)
                hidden_block(j - 1, first + RAW * j)
                split_lo(first + 2, j)
                rest_hidden(j - 1)
                for k in range(3, 6):
                    split_lo(first + k, j)
            split_lo(U_PW1 - 2), split_lo(U_PW1 - 1)
            hidden_block(NB - 1, U_PW1 - 2)
            rest_hidden(NB - 1)
            split_lo(U_PW1)
            add_residual(U_PW1, 4)

            norm_scale(2, normed_c)
            norm_lo(2, V_MIX + 1)
            for i in range(1, 6):
                split_lo(U_PW1 + i)

            def glu(g):
                dve.wait_ge(units_used, U_PW1 + 4 * g + 4)
                for i in range(4):
                    k = 4 * g + i
                    dve.wait_ge(c_sig, k + 1)
                    nc.vector.scalar_tensor_tensor(
                        out=upad[:, k, DW_TAPS - 1:], in0=ps[:, 4 + i, 0:SEQ],
                        scalar=colv[:, k, V_PW:V_PW + 1], in1=sig[:, i, :], op0=ALU.add, op1=ALU.mult).then_inc(c_u, 1)

            def taps(g, count):
                for tap in count:
                    for k in range(4 * g, 4 * g + 4):
                        src = upad[:, k, tap:tap + SEQ]
                        w = colv[:, k, V_DW + tap:V_DW + tap + 1]
                        if tap == DW_TAPS - 1:
                            ins = nc.vector.tensor_scalar(dw[:, k, :], src, w, colv[:, k, V_DWB:V_DWB + 1], ALU.mult, ALU.add)
                        else:
                            ins = nc.vector.scalar_tensor_tensor(out=dw[:, k, :], in0=src, scalar=w, in1=dw[:, k, :],
                                                                 op0=ALU.mult, op1=ALU.add)
                    link(ins)

            def join_taps(g):
                for k in range(4 * g, 4 * g + 4):
                    dve.wait_ge(diag_used, sum(PE_TAPS[n // 4] for n in range(k + 1)))
                    nc.vector.tensor_tensor(dw[:, k, :], dw[:, k, :], ps[:, k % 4, 0:SEQ], ALU.add).then_inc(dw_done, 1)

            mine, mine_1 = ([*range(DW_TAPS - 1, PE_TAPS[g] - 1, -1)] for g in range(2))
            glu(0)
            dve.wait_ge(consts, 5)
            dve.wait_ge(c_u, 4)
            taps(0, mine[:1])
            split_lo(U_PW1 + 6)
            taps(0, mine[1:4])
            split_lo(U_PW1 + 7)
            taps(0, mine[4:8])
            glu(1)
            dve.wait_ge(c_u, KT)
            for u in range(U_PW2, U_PW2 + 3):
                split_lo(u)
            taps(0, mine[8:])
            join_taps(0)
            taps(1, mine_1)
            join_taps(1)
            dve.wait_ge(mean_t, 1)
            for g in range(2):
                s = slice(4 * g, 4 * g + 4)
                nc.vector.tensor_tensor(dw[:, s, :], dw[:, s, :], ps[:, 4:5, 0:SEQ].broadcast_to([P, 4, SEQ]),
                                        ALU.subtract).then_inc(centred, 1)
            for g in range(2):
                dve.wait_ge(sq_ready, g + 1)
                nc.vector.tensor_reduce(sq_sum[:, g, :], sq[:, 4 * g:4 * g + 4, :].rearrange("p k n -> p n k"),
                                        AX.X, ALU.add).then_inc(sq_sum_ready, 1)
            dve.wait_ge(var_t, 1)
            nc.vector.tensor_scalar(ln_var[:], ps[:, 5, 0:TT], LN_EPS, None, ALU.add).then_inc(lnv_ready, 1)
            dve.wait_ge(lnr_ready, 1)
            for t in range(TT):
                ins = nc.vector.tensor_scalar(spread[:, t, :], ident[:], ln_rstd[:, t:t + 1], float(D), ALU.mult, ALU.mult)
            ins.then_inc(spread_r, 1)
            dve.wait_ge(lnb_t, 1)
            for k in range(0, KT, 2):
                s = slice(k, k + 2)
                nc.vector.tensor_tensor(sq[:, s, :], dw[:, s, :], ps[:, 6:7, 0:SEQ].broadcast_to([P, 2, SEQ]),
                                        ALU.mult).then_inc(ln_done, 1)
            for g in range(2):
                s = slice(4 * g, 4 * g + 4)
                dve.wait_ge(cz_hi, g + 1)
                nc.vector.tensor_tensor(z_lo[:, s, :], act_c[:, s, :], z_hi[:, s, :].bitcast(F32), ALU.subtract).then_inc(cz_lo, 1)
            split_lo(U_PW2 + 3)
            dve.wait_ge(bias_landed, 16)
            for t in range(TT):
                ins = nc.vector.tensor_tensor(res[:, t, :], res[:, t, :], bias_row[:, :], ALU.add)
            link(ins)
            split_lo(U_MOE)
            add_residual(U_MOE, 0, between=U_MOE + 1)

            mean_square(3)
            dve.wait_ge(rstd_ready, 4)
            dve.wait_ge(grow_landed, 16)
            for t in range(TT):
                nc.vector.scalar_tensor_tensor(out=normed_f[:, t, :], in0=res[:, t, :], scalar=rstd[:, t:t + 1],
                                               in1=grow[:, :], op0=ALU.mult, op1=ALU.mult).then_inc(xs_ready, 1)
            def rest_tokens(t):
                dve.wait_ge(xs_hi_r, t + 1)
                nc.vector.tensor_tensor(xs_lo[:, t, :], normed_f[:, t, :], xs_hi[:, t, :].bitcast(F32), ALU.subtract).then_inc(xs_lo_r, 1)

            rest_tokens(0)
            dve.wait_ge(consts, 9)
            dve.wait_ge(logits_t, 2)
            for t in range(TT):
                ins = nc.vector.tensor_scalar(logit[:, t, :], ps[:, 1, t * NE:(t + 1) * NE], rstd[:, t:t + 1], None, ALU.mult)
            link(ins)
            for t in range(TT):
                other = logit[:, t:t + 1, :].broadcast_to([P, NE, NE])
                own = logit[:, t, :].unsqueeze(2).broadcast_to([P, NE, NE])
                nc.vector.tensor_tensor(cmp_gt[:, t, :, :], other, own, ALU.is_gt)
                ins = nc.vector.tensor_tensor(cmp_eq[:, t, :, :], other, own, ALU.is_equal)
            link(ins)
            for t in range(TT):
                ins = nc.vector.tensor_tensor(cmp_eq[:, t, :, :], cmp_eq[:, t, :, :], earlier[:, :, :], ALU.mult)
            link(ins)
            link(nc.vector.tensor_tensor(cmp_gt[:, :, :, :].rearrange("p t a b -> p (t a b)"),
                                         cmp_gt[:, :, :, :].rearrange("p t a b -> p (t a b)"),
                                         cmp_eq[:, :, :, :].rearrange("p t a b -> p (t a b)"), ALU.add))
            link(nc.vector.tensor_reduce(rank[:, :, :].rearrange("p t e -> p (t e)"),
                                         cmp_gt[:, :, :, :].rearrange("p t a b -> p (t a) b"), AX.X, ALU.add))
            nc.vector.tensor_scalar(chosen[:, :, :], rank[:, :, :], 1.5, None, ALU.is_lt).then_inc(ranked, 1)
            link(nc.vector.tensor_reduce(small[:, 0:TT], logit[:, :, :], AX.X, ALU.max))
            nc.vector.tensor_tensor(gate[:, :, :], logit[:, :, :], small[:, 0:TT].unsqueeze(2).broadcast_to([P, TT, NE]),
                                    ALU.subtract).then_inc(lmax_r, 1)
            rest_tokens(1)
            link(nc.vector.memset(slot[:, :, NE:NE + 1], -1.0))
            dve.wait_ge(counted, 1)
            link(nc.vector.tensor_scalar(slot[:, :, 0:NE], ps[:, 6, 0:TT * NE].rearrange("p (t e) -> p t e", t=TT), 1.0, None, ALU.add))
            link(nc.vector.tensor_tensor(slot[:, :, 0:NE], slot[:, :, 0:NE], chosen[:, :, :], ALU.mult))
            link(nc.vector.tensor_scalar(slot[:, :, 0:NE], slot[:, :, 0:NE], 1.0, None, ALU.subtract))

            def softmax():
                dve.wait_ge(exp_l, 1)
                dve.wait_ge(ranked, 1)
                link(nc.vector.tensor_tensor(gate[:, :, :], gate[:, :, :], chosen[:, :, :], ALU.mult))
                link(nc.vector.tensor_reduce(small[:, 2:2 + TT], gate[:, :, :], AX.X, ALU.add))
                link(nc.vector.reciprocal(small[:, 4:4 + TT], small[:, 2:2 + TT]))
                link(nc.vector.tensor_tensor(gate[:, :, :], gate[:, :, :],
                                             small[:, 4:4 + TT].unsqueeze(2).broadcast_to([P, TT, NE]), ALU.mult))
                link(nc.vector.tensor_reduce(small[:, 6:7], ps[:, 2, 0:NE], AX.X, ALU.max))
                nc.vector.tensor_copy(most[:, :], small[:, 6:7]).then_inc(most_r, 1)

            def expert_pass(p, first):
                n0, s0 = p * NE, p * NE * NB
                y0, a0 = p * (NE + 1), p * TT * (NE + 1)

                def make_pick(n):
                    if not isinstance(n, int) or n > 0:
                        dve.wait_ge(pick_t, n + p * (NE + 1))
                    for t in range(TT):
                        ins = nc.vector.tensor_scalar(pick[:, t, :], iota[:, p * P:(p + 1) * P],
                                                      slot[:, t, bass.ds(n, 1)], None, ALU.is_equal)
                    ins.then_inc(pick_r, 1)

                def tokens_in(n):
                    for h in range(2):
                        dve.wait_ge(xe_hi_r, 2 * n + h + 1 + 2 * p * (NE + 1))
                        nc.vector.tensor_tensor(xe_lo[:, 4 * h:4 * h + 4, :].rearrange("p k n -> p (k n)"), ps[:, 6 + h, :],
                                                xe_hi[:, 4 * h:4 * h + 4, :].bitcast(F32).rearrange("p k n -> p (k n)"),
                                                ALU.subtract).then_inc(xe_lo_r, 1)

                def hidden(s, up_done):
                    dve.wait_ge(m_sil, s0 + 1 + s)
                    dve.wait_ge(units_used, up_done)
                    nc.vector.tensor_tensor(hid[:, 0, :], sil[:, 0, :], ps[:, 1, :], ALU.mult).then_inc(m_hid, 1)

                def rest_hidden(s):
                    dve.wait_ge(m_hthi, s0 + 1 + s)
                    nc.vector.tensor_tensor(ht_lo[:, 0, :, :].rearrange("p q n -> p (q n)"), ps[:, 2, :],
                                            ht_hi[:, 0, :, :].bitcast(F32).rearrange("p q n -> p (q n)"),
                                            ALU.subtract).then_inc(m_htlo, 1)

                def rest_output(e):
                    dve.wait_ge(ye_hi_r, y0 + 1 + e)
                    nc.vector.tensor_tensor(ye_lo[:, :], ps[:, 4:6, :].rearrange("p b n -> p (b n)"), ye_hi[:, :].bitcast(F32),
                                            ALU.subtract).then_inc(ye_lo_r, 1)

                def add_output(e, t):
                    dve.wait_ge(scattered, a0 + TT * e + t + 1)
                    nc.vector.scalar_tensor_tensor(
                        out=res[:, t, :], in0=ps[:, 6:8, :].rearrange("p b n -> p (b n)"),
                        scalar=gate[:, t, bass.ds(e, 1)], in1=res[:, t, :], op0=ALU.mult, op1=ALU.add).then_inc(added, 1)

                def step(e, j, output_of_last=False, skip=0):
                    s = NB * e + j
                    for k in range(skip, 2):
                        split_lo(first - 2 + k, s)
                    if output_of_last:
                        rest_output(e - 1)
                    split_lo(first, s)
                    if output_of_last:
                        add_output(e - 1, 0)
                    split_lo(first + 1, s)
                    rest_hidden(s - 1)
                    for k in (4, 5):
                        split_lo(first - 2 + k, s)
                    hidden(s, first + 2 + RAW * s)
                    if output_of_last:
                        add_output(e - 1, 1)

                make_pick(0)
                if p == 0:
                    softmax()
                for k in range(0 if p else 2, PARTS):
                    split_lo(first + k)
                tokens_in(0)
                for k in range(3, 6):
                    split_lo(first + k)
                hidden(0, first + 4)
                step(0, 1, skip=2)
                make_pick(1)
                with dve.Fori(2, NB) as j:
                    step(0, j)
                tokens_in(1)
                with dve.Fori(1, NE) as e:
                    step(e, 0)
                    step(e, 1, output_of_last=True)
                    make_pick(e + 1)
                    with dve.Fori(2, NB) as j:
                        step(e, j)
                    tokens_in(e + 1)
                last = first + NE * EXPERT_UNITS - 2
                split_lo(last)
                rest_hidden(NE * NB - 1)
                split_lo(last + 1)
                for c in range(2):
                    s = slice(c * NC, (c + 1) * NC)
                    dve.wait_ge(ye_hi_r, y0 + NE + c)
                    nc.vector.tensor_tensor(ye_lo[:, s], ps[:, 4 + c, :], ye_hi[:, s].bitcast(F32), ALU.subtract).then_inc(ye_lo_r, 1)
                for c in range(2):
                    s = slice(c * NC, (c + 1) * NC)
                    for t in range(TT):
                        dve.wait_ge(scattered, a0 + TT * (NE - 1 + c) + t + 1)
                        nc.vector.scalar_tensor_tensor(
                            out=res[:, t, s], in0=ps[:, LAST_BANKS[t] + c, :], scalar=gate[:, t, NE - 1:NE],
                            in1=res[:, t, s], op0=ALU.mult, op1=ALU.add).then_inc(added, 1)

            expert_pass(0, U_MOE)
            dve.wait_ge(most_r, 1)
            crowd = dve.value_load(most[0:1, 0:1], min_val=0, max_val=SEQ)
            with dve.If(crowd > P):
                expert_pass(1, N_UNITS)

            nc.vector.memset(small[:, 7:8], 0.0).then_inc(moe_over, 1)
            mean_square(4)
            dve.wait_ge(rstd_ready, 5)
            dve.wait_ge(gout_landed, 16)
            for t in range(TT):
                nc.vector.scalar_tensor_tensor(out=normed_f[:, t, :], in0=res[:, t, :], scalar=rstd[:, t:t + 1],
                                               in1=grow[:, :], op0=ALU.mult, op1=ALU.mult).then_inc(out_ready, 1)

        @block.tensor
        def _(pe):
            def passes(dst, stat, mov, start, stop, loose=False):
                (sh, sl), (mh, ml) = stat, mov
                nc.tensor.matmul(dst, sh, ml, start=start, stop=False, skip_group_check=loose)
                nc.tensor.matmul(dst, sl, mh, start=False, stop=False, skip_group_check=loose)
                return nc.tensor.matmul(dst, sh, mh, start=False, stop=stop, skip_group_check=loose)

            def turn_tokens(src, ready, count, banks, done):
                for k in range(KT):
                    if k % 4 == 0:
                        pe.wait_ge(ready, count + k // 4 + 1)
                    for t in range(TT):
                        c = (k % 2) * SEQ + t * P
                        ins = nc.tensor.transpose(ps[:, banks[k // 2], c:c + P], src[:, t, k * P:(k + 1) * P], ident[:])
                    if k % 2:
                        ins.then_inc(done, 1)

            def channel_major(u0, banks, xt, fresh=None):
                for kh in range(2):
                    if fresh is not None:
                        pe.wait_ge(xt_lo_ready, fresh + 4 * (kh + 1))
                    u = u0 + kh
                    pe.wait_ge(lo_ready, u + 1)
                    q = u % PARTS
                    for nt in range(4):
                        for k in range(4):
                            c = slice(k * NC + nt * P, k * NC + nt * P + P)
                            ins = passes(ps[:, banks + nt, 0:SEQ], (w_hi[:, q, c], w_lo[:, q, c]),
                                         (xt[0][:, 4 * kh + k, :], xt[1][:, 4 * kh + k, :]),
                                         start=(kh == 0 and k == 0), stop=(kh == 1 and k == 3))
                    ins.then_inc(units_used, 1)

            def token_major(u0, zt, bank, ready):
                for kh in range(2):
                    pe.wait_ge(ready, kh + 1)
                    for c in range(2):
                        u = u0 + 2 * kh + c
                        pe.wait_ge(lo_ready, u + 1)
                        q = u % PARTS
                        for t in range(TT):
                            for k in range(4):
                                s = slice(t * P, (t + 1) * P)
                                ins = passes(ps[:, bank + 2 * t + c, :], (zt[0][:, 4 * kh + k, s], zt[1][:, 4 * kh + k, s]),
                                             (w_hi[:, q, k * NC:(k + 1) * NC], w_lo[:, q, k * NC:(k + 1) * NC]),
                                             start=(kh == 0 and k == 0), stop=(kh == 1 and k == 3))
                        ins.then_inc(units_used, 1)

            def keep_clock(count, bank):
                for _ in range(count):
                    nc.tensor.matmul(ps[:, bank, :], xt_hi[:, 0, 0:P], xt_hi[:, 0:2, :].rearrange("p k n -> p (k n)"),
                                     start=True, stop=True)

            pe.wait_ge(consts, 1)
            pe.wait_ge(vecs_landed, 16)
            for k in range(KT):
                ins = nc.tensor.transpose(ps[:, 7, k * NV:(k + 1) * NV], vec_rows[:, k * P:(k + 1) * P], ident[0:NV, 0:NV])
            ins.then_inc(vec_t, 1)
            for _ in range(10):
                nc.tensor.matmul(ps[:, 6, 0:P], ident[:], ident[:], start=True, stop=True)
            turn_tokens(normed, normed_ready, 0, TURN_BANKS[0], norm_t)
            xt = (xt_hi, xt_lo)
            pe.wait_ge(colv_ready, 1)
            channel_major(0, 4, xt, fresh=0)
            channel_major(2, 0, xt)
            pe.wait_ge(x_out, 1)
            channel_major(4, 4, xt)
            pe.wait_ge(x_out, 2)
            pe.wait_ge(xc_lo_r, 2)
            for gate_n in range(2):
                u = U_GATES + gate_n
                pe.wait_ge(lo_ready, u + 1)
                if gate_n:
                    pe.wait_ge(y_out, 1)
                q = u % PARTS
                for h in range(HEADS):
                    for jt in range(2):
                        for k in range(2):
                            c = slice((2 * h + k) * 2 * P + jt * P, (2 * h + k) * 2 * P + jt * P + P)
                            ins = passes(ps[:, 4 * gate_n + h, jt * SEQ:(jt + 1) * SEQ],
                                         (w_hi[:, q, c], w_lo[:, q, c]),
                                         (xc_hi[:, 2 * h + k, :], xc_lo[:, 2 * h + k, :]), start=(k == 0), stop=(k == 1))
                ins.then_inc(units_used, 1)
            pe.wait_ge(r_out, KT)
            channel_major(U_Y1, 0, xt)
            pe.wait_ge(i_out, KT)
            keep_clock(28, 7)
            token_major(U_OUT, (xc_hi, xc_lo), 4, z_lo_r)

            pe.wait_ge(y_out, 2)
            turn_tokens(res, res_ready, 0, TURN_BANKS[1], norm_t)

            def hidden_transpose(dst, src):
                for q in range(4):
                    ins = nc.tensor.transpose(dst[:, q * P:(q + 1) * P], src[:, q * P:(q + 1) * P], ident[:])
                return ins

            def project(dst, xt_k, q, k, start, stop, loose):
                return passes(dst, xt_k, (w_hi[:, q, k * NC:(k + 1) * NC], w_lo[:, q, k * NC:(k + 1) * NC]), start, stop, loose)

            def ffn_project(side, base, rounds=0, fresh=False):
                for kh in range(2):
                    if fresh:
                        pe.wait_ge(xt_lo_ready, KT + 4 * (kh + 1))
                    pe.wait_ge(lo_ready, base + kh + 1 + RAW * rounds)
                    for t in range(TT):
                        s = slice(t * P, (t + 1) * P)
                        for k in range(4):
                            kk = 4 * kh + k
                            ins = project(ps[:, 2 * t + side, :], (xt_hi[:, kk, s], xt_lo[:, kk, s]), (base + kh) % PARTS, k,
                                          start=(kk == 0), stop=(kk == KT - 1), loose=False)
                    ins.then_inc(units_used, 1)
                    if side == 0 and kh == 0 and not fresh:
                        ffn_turn(rounds - 1)

            def ffn_turn(j):
                for t in range(TT):
                    pe.wait_ge(f_hid, TT * j + t + 1)
                    hidden_transpose(ps[:, 2 * t + 1, :], hid[:, t, :]).then_inc(f_t, 1)

            def ffn_down(j, base, rounds=0, first=False):
                for c in range(2):
                    pe.wait_ge(lo_ready, base + c + 1 + RAW * rounds)
                    for t in range(TT):
                        if c == 0:
                            pe.wait_ge(f_htlo, TT * j + t + 1)
                        for k in range(4):
                            ins = project(ps[:, 4 + 2 * t + c, :], (ht_hi[:, t, k, :], ht_lo[:, t, k, :]), (base + c) % PARTS, k,
                                          start=(first and k == 0), stop=False, loose=True)
                    ins.then_inc(units_used, 1)

            def ffn_step(j, first=False):
                pe.wait_ge(f_sil, TT * j)
                ffn_project(0, U_FFN - 2, j)
                ffn_down(j - 1, U_FFN, j, first)
                ffn_project(1, U_FFN + 2, j)

            ffn_project(0, U_FFN, fresh=True)
            ffn_project(1, U_FFN + 2)
            ffn_step(1, first=True)
            with pe.Fori(2, NB) as j:
                ffn_step(j)
            ffn_turn(NB - 1)
            ffn_down(NB - 1, U_PW1 - 2)

            keep_clock(16, 0)
            turn_tokens(normed_c, normed_ready, 2, TURN_BANKS[2], norm_t)
            for g in range(2):
                if g:
                    pe.wait_ge(c_sig, 4)
                channel_major(U_PW1 + 4 * g, 0, xt, fresh=None if g else 2 * KT)
                if g:
                    pe.wait_ge(c_u, 4)
                channel_major(U_PW1 + 4 * g + 2, 4, xt)
            pe.wait_ge(consts, 5)
            pe.wait_ge(c_sig, KT)
            for k in range(KT):
                pe.wait_ge(c_u, k + 1)
                if k >= 4:
                    pe.wait_ge(dw_done, k - 3)
                for i in range(PE_TAPS[k // 4]):
                    n = PE_TAP_LIST.index((k, i))
                    pe.wait_ge(diag_ready, n + 1)
                    nc.tensor.matmul(ps[:, k % 4, 0:SEQ], diag[:, n % 4, :], upad[:, k, i:i + SEQ],
                                     start=(i == 0), stop=(i == PE_TAPS[k // 4] - 1)).then_inc(diag_used, 1)
            for k in range(KT):
                if k == 4:
                    keep_clock(12, 7)
                pe.wait_ge(dw_done, k + 1)
                ins = nc.tensor.matmul(ps[:, 4, 0:SEQ], mean_w[:], dw[:, k, :], start=(k == 0), stop=(k == KT - 1))
            ins.then_inc(mean_t, 1)
            keep_clock(18, 7)
            pe.wait_ge(sq_sum_ready, 2)
            for t in range(TT):
                for g in range(2):
                    ins = nc.tensor.matmul(ps[:, 5, t:t + 1], sq_sum[:, g, t * P:(t + 1) * P], mean_w[:, 0:1],
                                           start=(g == 0), stop=(g == 1))
            ins.then_inc(var_t, 1)
            keep_clock(6, 7)
            pe.wait_ge(spread_r, 1)
            for t in range(TT):
                ins = nc.tensor.matmul(ps[:, 6, t * P:(t + 1) * P], mean_w[:], spread[:, t, :], start=True, stop=True)
            ins.then_inc(lnb_t, 1)
            keep_clock(20, 7)
            token_major(U_PW2, (z_hi, z_lo), 0, cz_lo)

            turn_tokens(res, res_ready, 4, range(4, 8), xr_t)
            pe.wait_ge(router_ready, 1)
            for k in range(KT):
                pe.wait_ge(xr_out, k // 2 + 1)
                ins = nc.tensor.matmul(ps[0:NE, 0, 0:SEQ], router[:, k, :], routed_t[:, k // 2, (k % 2) * SEQ:(k % 2 + 1) * SEQ],
                                       start=(k == 0), stop=(k == KT - 1))
            ins.then_inc(logits_t, 1)
            pe.wait_ge(logit_rows_r, 1)
            for t in range(TT):
                ins = nc.tensor.transpose(ps[:, 1, t * NE:(t + 1) * NE], logit_rows[:, t * P:(t + 1) * P], ident[0:NE, 0:NE])
            ins.then_inc(logits_t, 1)
            keep_clock(12, 3)
            pe.wait_ge(ranked, 1)
            nc.tensor.matmul(ps[:, 6, 0:NE], upper[:], chosen[:, 0, :], start=True, stop=True)
            nc.tensor.matmul(ps[:, 6, NE:2 * NE], ones[:], chosen[:, 0, :], start=True, stop=False)
            nc.tensor.matmul(ps[:, 6, NE:2 * NE], upper[:], chosen[:, 1, :], start=False, stop=True)
            nc.tensor.matmul(ps[:, 2, 0:NE], ones[:], chosen[:, 0, :], start=True, stop=False)
            nc.tensor.matmul(ps[:, 2, 0:NE], ones[:], chosen[:, 1, :], start=False, stop=True).then_inc(counted, 1)
            keep_clock(9, 3)

            def expert_pass(p, first):
                n0, s0 = p * NE, p * NE * NB
                y0, a0 = p * (NE + 1), p * TT * (NE + 1)

                def weights(base, rounds=0):
                    pe.wait_ge(lo_ready, base + 1 + RAW * rounds)
                    return base % PARTS

                def gate_or_up(bank, base, rounds=0, tokens=None):
                    for kh in range(2):
                        if tokens is not None:
                            pe.wait_ge(xe_lo_r, tokens + kh)
                        q = weights(base + kh, rounds)
                        for k in range(4):
                            kk = 4 * kh + k
                            ins = project(ps[:, bank, :], (xe_hi[:, kk, :], xe_lo[:, kk, :]), q, k,
                                          start=(kk == 0), stop=(kk == KT - 1), loose=False)
                        ins.then_inc(units_used, 1)

                def turn(s):
                    pe.wait_ge(m_hid, s0 + 1 + s)
                    hidden_transpose(ps[:, 2, :], hid[:, 0, :]).then_inc(m_t, 1)

                def down(s, base, rounds=0):
                    pe.wait_ge(m_htlo, s0 + 1 + s)
                    for c in range(2):
                        q = weights(base + c, rounds)
                        for k in range(4):
                            ins = project(ps[:, 4 + c, :], (ht_hi[:, 0, k, :], ht_lo[:, 0, k, :]), q, k,
                                          start=False, stop=False, loose=True)
                        ins.then_inc(units_used, 1)

                def gather(n):
                    pe.wait_ge(pick_r, n + 1 + p * (NE + 1))
                    for k in range(KT):
                        dst = ps[:, 6 + k // 4, (k % 4) * P:(k % 4 + 1) * P]
                        for t in range(TT):
                            for part, x in enumerate((xs_hi, xs_lo)):
                                ins = nc.tensor.matmul(dst, x[:, t, k * P:(k + 1) * P], pick[:, t, :],
                                                       start=(t == 0 and part == 0), stop=(t == TT - 1 and part == 1))
                        if k % 4 == 3:
                            ins.then_inc(gathered, 1)
                    for t in range(TT):
                        ins = nc.tensor.transpose(ps[:, 3, t * P:(t + 1) * P], pick[:, t, :].bitcast(F32), ident[:])
                    ins.then_inc(pick_t, 1)

                def scatter_half(t, c, bank):
                    for part, y in enumerate((ye_hi, ye_lo)):
                        ins = nc.tensor.matmul(ps[:, bank + c, :], place_e[:, t, :], y[:, c * NC:(c + 1) * NC],
                                               start=(part == 0), stop=(part == 1))
                    return ins

                def scatter(t):
                    scatter_half(t, 0, 6)
                    scatter_half(t, 1, 6).then_inc(scattered, 1)

                def open_output():
                    for c in range(2):
                        nc.tensor.matmul(ps[:, 4 + c, :], zeros[:, 0:P], zeros[:, :], start=True, stop=False,
                                         skip_group_check=True)

                def step(e, j, scatter_last=False):
                    s = NB * e + j
                    pe.wait_ge(m_sil, s0 + s)
                    gate_or_up(0, first - 2, s)
                    if scatter_last:
                        pe.wait_ge(place_r, n0 + e)
                        pe.wait_ge(ye_lo_r, y0 + e)
                        scatter(0)
                    turn(s - 1)
                    gate_or_up(1, first, s)
                    if scatter_last:
                        pe.wait_ge(added, a0 + TT * e - 1)
                        scatter(1)
                        open_output()
                    down(s - 1, first + 2, s)

                gather(0)
                open_output()
                gate_or_up(0, first, tokens=1 + 2 * p * (NE + 1))
                gate_or_up(1, first + 2)
                step(0, 1)
                pe.wait_ge(place_r, n0 + 1)
                gather(1)
                with pe.Fori(2, NB) as j:
                    step(0, j)
                with pe.Fori(1, NE) as e:
                    pe.wait_ge(xe_lo_r, 2 * e + 2 + 2 * p * (NE + 1))
                    step(e, 0)
                    step(e, 1, scatter_last=True)
                    pe.wait_ge(place_r, n0 + e + 1)
                    pe.wait_ge(added, a0 + TT * e)
                    gather(e + 1)
                    with pe.Fori(2, NB) as j:
                        step(e, j)
                last = first + NE * EXPERT_UNITS - 2
                turn(NE * NB - 1)
                down(NE * NB - 1, last)
                pe.wait_ge(xe_lo_r, 2 * (p + 1) * (NE + 1))
                for c in range(2):
                    pe.wait_ge(ye_lo_r, y0 + NE + c)
                    for t in range(TT):
                        scatter_half(t, c, LAST_BANKS[t]).then_inc(scattered, 1)
                pe.wait_ge(added, a0 + TT * (NE + 1))

            pe.wait_ge(xs_lo_r, TT)
            pe.wait_ge(consts, 9)
            expert_pass(0, U_MOE)
            pe.wait_ge(most_r, 1)
            crowd = pe.value_load(most[0:1, 0:1], min_val=0, max_val=SEQ)
            with pe.If(crowd > P):
                expert_pass(1, N_UNITS)
            pe.nop()
    return nc


_VECTORS = ["norm_mix", "norm_ffn", "rec_conv_w", "rec_conv_b", "rec_gate_a_b", "rec_gate_x_b", "rec_lambda",
            "cnv_b_pw1", "cnv_dw_w", "cnv_dw_b", "cnv_ln_g", "cnv_ln_b"]
_INS = ["x", "norm_ffn", "norm_out", "rec_w_in", "rec_gate_a_w", "rec_gate_x_w", "rec_w_out", "ffn_w_gate_up",
        "ffn_w_down", "cnv_w_pw1", "cnv_w_pw2", "cnv_b_pw2", "moe_router", "moe_w_gate_up", "moe_w_down"]


def kernel(**inputs):
    import numpy as np
    import concourse.bacc as bacc
    from concourse.bass_utils import run_bass_kernel_spmd

    nc = bacc.Bacc("TRN2", target_bir_lowering=False, num_devices=1)
    arrays, aps = {}, {}
    laid = {name: inputs[name] for name in _INS}
    laid["vectors"] = np.concatenate([np.asarray(inputs[name]).reshape(-1, D) for name in _VECTORS])
    for name, a in laid.items():
        a = np.ascontiguousarray(a)
        arrays[f"in_{name}"] = a
        aps[name] = nc.dram_tensor(f"in_{name}", a.shape, F32, kind="ExternalInput").ap()
    out = nc.dram_tensor("out", (1, SEQ, D), F32, kind="ExternalOutput").ap()
    build(nc, aps, out)
    r = run_bass_kernel_spmd(nc, [arrays], core_ids=[0])
    return r.results[0]["out"]
```
